# Optimizing a Trainium2 kernel written in Bass

```python
import jax, jax.numpy as jnp
from jax import lax
import numpy as np

D_MODEL = 1024
BATCH = 1
SEQ = 512
DEPTH = 2

CHUNK = 64
D_MIX = D_MODEL
A_WIDTH = D_MIX // 4
A_HEADS = 4
A_HEAD_DIM = A_WIDTH // A_HEADS
A_BLOCK = 128
POOL_WINDOWS = (2, 4, 8, 16)
B_WIDTH = D_MIX // 4
B_GROUP_DIM = B_WIDTH // len(POOL_WINDOWS)
C_WIDTH = D_MIX - A_WIDTH - B_WIDTH
C_HEADS = 8
C_HEAD_DIM = C_WIDTH // C_HEADS
ROPE_BASE = 10000.0
IN_COLS = 2 * A_WIDTH + B_WIDTH + 4 * C_WIDTH
D_FF = ((8 * D_MODEL // 3 + 127) // 128) * 128
CONV_WIDTH = 3
EPS = 1e-6


def rms_norm(x, g):
    xf = x.astype(jnp.float32)
    y = xf * lax.rsqrt(jnp.mean(xf * xf, axis=-1, keepdims=True) + EPS)
    return (y * g.astype(jnp.float32)).astype(x.dtype)

def spatial_gating(z, vnorm_g, ws, bs):
    bsz, s_len, _ = z.shape
    u, v = jnp.split(z, 2, axis=-1)
    v = rms_norm(v, vnorm_g)
    nb = s_len // A_BLOCK
    v = v.reshape(bsz, nb, A_BLOCK, A_HEADS, A_HEAD_DIM)
    chunk_id = jnp.arange(A_BLOCK) // CHUNK
    mask = chunk_id[:, None] >= chunk_id[None, :]
    w = jnp.where(mask[None], ws, jnp.zeros_like(ws))
    sv = jnp.einsum('hts,bnshd->bnthd', w, v) + bs.T[None, None, :, :, None]
    return u * sv.reshape(bsz, s_len, A_WIDTH)

def multiscale_pool(xb, w_grp, scale):
    bsz, s_len, _ = xb.shape
    xf = xb.astype(jnp.float32)
    cs = jnp.concatenate([jnp.zeros((bsz, 1, B_WIDTH), jnp.float32), jnp.cumsum(xf, axis=1)], axis=1)
    t = jnp.arange(s_len)
    outs = []
    for gi, win in enumerate(POOL_WINDOWS):
        sl = slice(gi * B_GROUP_DIM, (gi + 1) * B_GROUP_DIM)
        lo = jnp.maximum(t + 1 - win, 0)
        cnt = (t + 1 - lo).astype(jnp.float32)
        outs.append((cs[:, 1:, sl] - cs[:, lo, sl]) / cnt[None, :, None])
    pooled = jnp.concatenate(outs, axis=-1).astype(xb.dtype) - xb
    pooled = pooled.reshape(bsz, s_len, len(POOL_WINDOWS), B_GROUP_DIM)
    y = jnp.einsum('bsgc,gcd->bsgd', pooled, w_grp).reshape(bsz, s_len, B_WIDTH)
    return y * scale

def rotary(x, pos):
    half = x.shape[-1] // 2
    inv = ROPE_BASE ** (-jnp.arange(half, dtype=jnp.float32) / half)
    ang = pos.astype(jnp.float32)[:, None] * inv[None, :]
    cos = jnp.cos(ang)[None, :, None, :]
    sin = jnp.sin(ang)[None, :, None, :]
    xf = x.astype(jnp.float32)
    x1, x2 = xf[..., :half], xf[..., half:]
    return jnp.concatenate([x1 * cos - x2 * sin, x2 * cos + x1 * sin], axis=-1).astype(x.dtype)

def retention(q, k, v, g, norm_g):
    bsz, s_len, _ = q.shape
    n_chunks = s_len // CHUNK
    dt = q.dtype
    pos = jnp.arange(s_len)
    q = rotary(q.reshape(bsz, s_len, C_HEADS, C_HEAD_DIM), pos) * (C_HEAD_DIM ** -0.5)
    k = rotary(k.reshape(bsz, s_len, C_HEADS, C_HEAD_DIM), pos)
    v = v.reshape(bsz, s_len, C_HEADS, C_HEAD_DIM)
    log_gamma = jnp.log1p(-jnp.exp2(-5.0 - jnp.arange(C_HEADS, dtype=jnp.float32)))
    idx = jnp.arange(CHUNK, dtype=jnp.float32)
    d_intra = jnp.exp(log_gamma[:, None, None] * jnp.abs(idx[:, None] - idx[None, :])).astype(dt)
    k_dec = jnp.exp(log_gamma[None, :] * (CHUNK - 1 - idx)[:, None]).astype(dt)
    q_dec = jnp.exp(log_gamma[None, :] * (idx + 1)[:, None]).astype(dt)
    chunk_dec = jnp.exp(log_gamma * CHUNK).astype(dt)
    qc = q.reshape(bsz, n_chunks, CHUNK, C_HEADS, C_HEAD_DIM)
    kc = k.reshape(bsz, n_chunks, CHUNK, C_HEADS, C_HEAD_DIM)
    vc = v.reshape(bsz, n_chunks, CHUNK, C_HEADS, C_HEAD_DIM)
    scores = jnp.einsum('bnthd,bnshd->bnhts', qc, kc) * d_intra
    y_intra = jnp.einsum('bnhts,bnshe->bnthe', scores, vc)
    kv = jnp.einsum('bnshd,bnshe->nbhde', kc * k_dec[:, :, None], vc)

    def step(state, kv_n):
        return state * chunk_dec[None, :, None, None] + kv_n, state

    _, s_prev = lax.scan(step, jnp.zeros(kv.shape[1:], kv.dtype), kv)
    y_cross = jnp.einsum('bnthd,nbhde->bnthe', qc * q_dec[:, :, None], s_prev)
    y = (y_intra + y_cross).reshape(bsz, s_len, C_HEADS, C_HEAD_DIM)
    yf = y.astype(jnp.float32)
    mu = jnp.mean(yf, axis=-1, keepdims=True)
    var = jnp.mean(jnp.square(yf - mu), axis=-1, keepdims=True)
    yf = (yf - mu) * lax.rsqrt(var + EPS)
    y = (yf.reshape(bsz, s_len, C_WIDTH) * norm_g.astype(jnp.float32)).astype(dt)
    return jax.nn.silu(g) * y

def conv_ffn(h, w_up, conv_w, conv_b, w_down):
    up = h @ w_up
    s_len = up.shape[1]
    padded = jnp.pad(up, ((0, 0), (CONV_WIDTH - 1, 0), (0, 0)))
    conv = conv_b + padded[:, 0:s_len] * conv_w[0]
    for j in range(1, CONV_WIDTH):
        conv = conv + padded[:, j:j + s_len] * conv_w[j]
    gate, val = jnp.split(conv, 2, axis=-1)
    return (jax.nn.silu(gate) * val) @ w_down

def first_inputs(seed: int = 0) -> dict:
    key = jax.random.key(seed)
    ks = jax.random.split(key, 20)
    f32 = jnp.float32
    nrm = lambda k, shape, s: jax.random.normal(k, shape, f32) * s
    return {
        "x": jax.random.normal(ks[0], (BATCH, SEQ, D_MODEL), f32),
        "norm1_g": 1.0 + nrm(ks[1], (DEPTH, D_MODEL), 0.05),
        "w_in": nrm(ks[2], (DEPTH, D_MODEL, IN_COLS), D_MODEL ** -0.5),
        "a_vnorm_g": 1.0 + nrm(ks[3], (DEPTH, A_WIDTH), 0.05),
        "a_ws": nrm(ks[4], (DEPTH, A_HEADS, A_BLOCK, A_BLOCK), 0.5 * A_BLOCK ** -0.5),
        "a_bs": 1.0 + nrm(ks[5], (DEPTH, A_HEADS, A_BLOCK), 0.1),
        "b_w": nrm(ks[6], (DEPTH, len(POOL_WINDOWS), B_GROUP_DIM, B_GROUP_DIM), B_GROUP_DIM ** -0.5),
        "b_scale": 1.0 + nrm(ks[7], (DEPTH, B_WIDTH), 0.1),
        "c_norm_g": 1.0 + nrm(ks[8], (DEPTH, C_WIDTH), 0.05),
        "w_out": nrm(ks[9], (DEPTH, D_MIX, D_MODEL), D_MIX ** -0.5),
        "norm2_g": 1.0 + nrm(ks[10], (DEPTH, D_MODEL), 0.05),
        "w_up": nrm(ks[11], (DEPTH, D_MODEL, 2 * D_FF), D_MODEL ** -0.5),
        "conv_w": nrm(ks[12], (DEPTH, CONV_WIDTH, 2 * D_FF), CONV_WIDTH ** -0.5),
        "conv_b": nrm(ks[13], (DEPTH, 2 * D_FF), 0.02),
        "w_down": nrm(ks[14], (DEPTH, D_FF, D_MODEL), D_FF ** -0.5),
        "final_g": 1.0 + nrm(ks[15], (D_MODEL,), 0.05),
    }

def first_block(x, norm1_g, w_in, a_vnorm_g, a_ws, a_bs, b_w, b_scale, c_norm_g,
              w_out, norm2_g, w_up, conv_w, conv_b, w_down, final_g):
    splits = [2 * A_WIDTH, 2 * A_WIDTH + B_WIDTH, 2 * A_WIDTH + B_WIDTH + C_WIDTH,
              2 * A_WIDTH + B_WIDTH + 2 * C_WIDTH, 2 * A_WIDTH + B_WIDTH + 3 * C_WIDTH]
    for l in range(DEPTH):
        h = rms_norm(x, norm1_g[l])
        proj = h @ w_in[l]
        za, xb, q, k, v, g = jnp.split(proj, splits, axis=-1)
        ya = spatial_gating(jax.nn.gelu(za), a_vnorm_g[l], a_ws[l], a_bs[l])
        yb = multiscale_pool(xb, b_w[l], b_scale[l])
        yc = retention(q, k, v, g, c_norm_g[l])
        x = x + jnp.concatenate([ya, yb, yc], axis=-1) @ w_out[l]
        x = x + conv_ffn(rms_norm(x, norm2_g[l]), w_up[l], conv_w[l], conv_b[l], w_down[l])
    return rms_norm(x, final_g)


DEPTH_2 = 1

D_RNN = D_MODEL // 2
RNN_BLOCKS = 8
RNN_BLOCK = D_RNN // RNN_BLOCKS
CONV_WIDTH_2 = 4
LRU_C = 8.0
N_HEADS = 8
HEAD_DIM = 64
N_KV = 2
REP = N_HEADS // N_KV
D_ATT = N_HEADS * HEAD_DIM
CMP_LEN = 32
CMP_STRIDE = 16
CMP_HIDDEN = 256
SLC_BLOCK = 64
SLC_TOPK = 16
WINDOW = 512
Q_BLOCK = 64
D_FF_2 = 4 * D_MODEL
NEG = -1e30
FORCED = 1e4


def rms_norm_2(x, g):
    xf = x.astype(jnp.float32)
    y = xf * lax.rsqrt(jnp.mean(xf * xf, axis=-1, keepdims=True) + EPS)
    return (y * g.astype(jnp.float32)).astype(x.dtype)

def modulate(h, shift, scale):
    return h * (1.0 + scale[:, None, :]) + shift[:, None, :]

def alibi_slopes():
    return jnp.asarray(2.0 ** (-8.0 * np.arange(1, N_HEADS + 1) / N_HEADS), jnp.float32)

def causal_depthwise_conv(x, w, b):
    y = lax.conv_general_dilated(x, w[:, None, :], window_strides=(1,), padding=[(CONV_WIDTH_2 - 1, 0)],
                                 dimension_numbers=('NWC', 'WIO', 'NWC'), feature_group_count=x.shape[-1])
    return y + b

def block_diag(x, w, b):
    xb = x.reshape(x.shape[:-1] + (RNN_BLOCKS, RNN_BLOCK))
    return jnp.einsum('bsni,nij->bsnj', xb, w.astype(jnp.float32)).reshape(x.shape) + b.astype(jnp.float32)

def rg_lru(x, w_a, b_a, w_x, b_x, lam):
    xf = x.astype(jnp.float32)
    r = jax.nn.sigmoid(block_diag(xf, w_a, b_a))
    i = jax.nn.sigmoid(block_diag(xf, w_x, b_x))
    log_a = -LRU_C * r * jax.nn.softplus(-lam.astype(jnp.float32))
    a = jnp.exp(log_a)
    u = jnp.sqrt(-jnp.expm1(2.0 * log_a)) * (i * xf)

    def combine(e1, e2):
        a1, b1 = e1
        a2, b2 = e2
        return a1 * a2, a2 * b1 + b2

    _, h = lax.associative_scan(combine, (a, u), axis=1)
    return h.astype(x.dtype)

def to_heads(t):
    B, S, _ = t.shape
    return t.reshape(B, S, N_KV, HEAD_DIM).transpose(0, 2, 1, 3)

def compress_blocks(k, pos_emb, w1, w2):
    B, G, S, D = k.shape
    n_cmp = (S - CMP_LEN) // CMP_STRIDE + 1
    idx = CMP_STRIDE * jnp.arange(n_cmp)[:, None] + jnp.arange(CMP_LEN)[None, :]
    blocks = (k[:, :, idx] + pos_emb).reshape(B, G, n_cmp, CMP_LEN * D)
    return jax.nn.gelu(blocks @ w1) @ w2

def nsa_attention(q, k_c, v_c, k_s, v_s, k_w, v_w, gate_logits,
                  cmp_pos_k, cmp_w1_k, cmp_w2_k, cmp_pos_v, cmp_w1_v, cmp_w2_v):
    B, S, _ = q.shape
    f32 = jnp.float32
    n_cmp = (S - CMP_LEN) // CMP_STRIDE + 1
    n_slc = S // SLC_BLOCK
    n_sel = min(SLC_TOPK, n_slc)
    n_qb = S // Q_BLOCK
    qh = q.reshape(B, S, N_KV, REP, HEAD_DIM).transpose(0, 2, 3, 1, 4) * (HEAD_DIM ** -0.5)
    kc = compress_blocks(to_heads(k_c), cmp_pos_k, cmp_w1_k, cmp_w2_k)
    vc = compress_blocks(to_heads(v_c), cmp_pos_v, cmp_w1_v, cmp_w2_v).astype(f32)
    ks = to_heads(k_s).reshape(B, N_KV, n_slc, SLC_BLOCK, HEAD_DIM)
    vs = to_heads(v_s).reshape(B, N_KV, n_slc, SLC_BLOCK, HEAD_DIM)
    pad = ((0, 0), (0, 0), (WINDOW, 0), (0, 0))
    kw = jnp.pad(to_heads(k_w), pad)
    vw = jnp.pad(to_heads(v_w), pad)
    gates = jax.nn.sigmoid(gate_logits.astype(f32)).reshape(B, S, 3, N_KV, REP).transpose(2, 0, 3, 4, 1)
    slopes = alibi_slopes().reshape(1, N_KV, REP, 1, 1)
    c_start = CMP_STRIDE * jnp.arange(n_cmp)
    cmp_end = c_start + (CMP_LEN - 1)
    s_start = SLC_BLOCK * jnp.arange(n_slc)
    overlap = ((c_start[:, None] < s_start[None, :] + SLC_BLOCK) &
               (c_start[:, None] + CMP_LEN > s_start[None, :])).astype(f32)
    blk_ids = jnp.arange(n_slc)
    gather = jax.vmap(jax.vmap(lambda kb, ix: kb[ix]))

    def one_block(i):
        q0 = i * Q_BLOCK
        qb = lax.dynamic_slice_in_dim(qh, q0, Q_BLOCK, axis=3)
        t = q0 + jnp.arange(Q_BLOCK)
        d_c = (t[:, None] - cmp_end[None, :]).astype(f32)
        sc = jnp.einsum('bgrqd,bgcd->bgrqc', qb, kc).astype(f32) - slopes * d_c
        sc = jnp.where(d_c >= 0, sc, NEG)
        p_c = jax.nn.softmax(sc, axis=-1) * (t >= CMP_LEN - 1).astype(f32)[:, None]
        o_c = jnp.einsum('bgrqc,bgcd->bgrqd', p_c, vc)
        imp = jnp.einsum('bgrqc,cj->bgqj', p_c, overlap)
        cur = t // SLC_BLOCK
        forced = (blk_ids[None, :] == 0) | (blk_ids[None, :] == cur[:, None]) | (blk_ids[None, :] == cur[:, None] - 1)
        visible = s_start[None, :] <= t[:, None]
        imp = jnp.where(forced, FORCED, jnp.where(visible, imp, NEG))
        _, sel = lax.top_k(imp, n_sel)
        k_sel = gather(ks, sel)
        v_sel = gather(vs, sel).astype(f32)
        pos = sel[..., None] * SLC_BLOCK + jnp.arange(SLC_BLOCK)
        d_s = (t[:, None, None] - pos).astype(f32)[:, :, None]
        ss = jnp.einsum('bgrqd,bgqnkd->bgrqnk', qb, k_sel).astype(f32) - slopes[..., None] * d_s
        ss = jnp.where(d_s >= 0, ss, NEG)
        p_s = jax.nn.softmax(ss.reshape(ss.shape[:4] + (-1,)), axis=-1).reshape(ss.shape)
        o_s = jnp.einsum('bgrqnk,bgqnkd->bgrqd', p_s, v_sel)
        kwb = lax.dynamic_slice_in_dim(kw, q0, WINDOW + Q_BLOCK, axis=2)
        vwb = lax.dynamic_slice_in_dim(vw, q0, WINDOW + Q_BLOCK, axis=2).astype(f32)
        s_pos = q0 - WINDOW + jnp.arange(WINDOW + Q_BLOCK)
        d_w = (t[:, None] - s_pos[None, :]).astype(f32)
        ok = (d_w >= 0) & (d_w < WINDOW) & (s_pos[None, :] >= 0)
        sw = jnp.einsum('bgrqd,bgkd->bgrqk', qb, kwb).astype(f32) - slopes * d_w
        sw = jnp.where(ok, sw, NEG)
        o_w = jnp.einsum('bgrqk,bgkd->bgrqd', jax.nn.softmax(sw, axis=-1), vwb)
        gb = lax.dynamic_slice_in_dim(gates, q0, Q_BLOCK, axis=4)[..., None]
        return gb[0] * o_c + gb[1] * o_s + gb[2] * o_w

    out = lax.map(one_block, jnp.arange(n_qb))
    return out.transpose(1, 0, 4, 2, 3, 5).reshape(B, S, D_ATT).astype(q.dtype)

def hybrid_mixer(h, w_in, conv_w, conv_b, lru_wa, lru_ba, lru_wx, lru_bx, lru_lambda,
                 cmp_pos_k, cmp_w1_k, cmp_w2_k, cmp_pos_v, cmp_w1_v, cmp_w2_v,
                 norm_rnn_out, norm_att_out, w_out):
    sizes = [D_RNN, D_RNN, D_ATT] + [N_KV * HEAD_DIM] * 6 + [3 * N_HEADS]
    splits = np.cumsum(sizes)[:-1].tolist()
    z = h @ w_in
    g_rnn, x_rnn, q, k_c, v_c, k_s, v_s, k_w, v_w, gate_logits = jnp.split(z, splits, axis=-1)
    rnn = jax.nn.gelu(g_rnn) * rg_lru(causal_depthwise_conv(x_rnn, conv_w, conv_b),
                                      lru_wa, lru_ba, lru_wx, lru_bx, lru_lambda)
    att = nsa_attention(q, k_c, v_c, k_s, v_s, k_w, v_w, gate_logits,
                        cmp_pos_k, cmp_w1_k, cmp_w2_k, cmp_pos_v, cmp_w1_v, cmp_w2_v)
    y = jnp.concatenate([rms_norm_2(rnn, norm_rnn_out), rms_norm_2(att, norm_att_out)], axis=-1)
    return y @ w_out

def second_inputs(seed: int = 0) -> dict:
    key = jax.random.key(seed)
    ks = jax.random.split(key, 32)
    L = DEPTH_2
    f32 = jnp.float32

    def nrm(k, shape, scale):
        return jax.random.normal(k, shape, f32) * scale

    def gain(k, n):
        return 1.0 + 0.05 * jax.random.normal(k, (L, n), f32)

    d_in = 2 * D_RNN + D_ATT + 6 * N_KV * HEAD_DIM + 3 * N_HEADS
    u = jax.random.uniform(ks[31], (L, D_RNN), f32, minval=0.9, maxval=0.999)
    a0 = u ** (1.0 / LRU_C)
    lam = jnp.log(a0) - jnp.log1p(-a0)
    return {
        'x': nrm(ks[0], (BATCH, SEQ, D_MODEL), 1.0),
        'c': nrm(ks[1], (BATCH, D_MODEL), 1.0),
        'ada_w': nrm(ks[2], (L, D_MODEL, 6 * D_MODEL), 0.1 * D_MODEL ** -0.5),
        'ada_b': nrm(ks[3], (L, 6 * D_MODEL), 0.01),
        'pre_norm_mix': gain(ks[4], D_MODEL),
        'w_in': nrm(ks[5], (L, D_MODEL, d_in), D_MODEL ** -0.5),
        'conv_w': nrm(ks[6], (L, CONV_WIDTH_2, D_RNN), CONV_WIDTH_2 ** -0.5),
        'conv_b': nrm(ks[7], (L, D_RNN), 0.01),
        'lru_wa': nrm(ks[8], (L, RNN_BLOCKS, RNN_BLOCK, RNN_BLOCK), RNN_BLOCK ** -0.5),
        'lru_ba': nrm(ks[9], (L, D_RNN), 0.01),
        'lru_wx': nrm(ks[10], (L, RNN_BLOCKS, RNN_BLOCK, RNN_BLOCK), RNN_BLOCK ** -0.5),
        'lru_bx': nrm(ks[11], (L, D_RNN), 0.01),
        'lru_lambda': lam,
        'cmp_pos_k': nrm(ks[12], (L, CMP_LEN, HEAD_DIM), 0.1),
        'cmp_w1_k': nrm(ks[13], (L, CMP_LEN * HEAD_DIM, CMP_HIDDEN), (CMP_LEN * HEAD_DIM) ** -0.5),
        'cmp_w2_k': nrm(ks[14], (L, CMP_HIDDEN, HEAD_DIM), CMP_HIDDEN ** -0.5),
        'cmp_pos_v': nrm(ks[15], (L, CMP_LEN, HEAD_DIM), 0.1),
        'cmp_w1_v': nrm(ks[16], (L, CMP_LEN * HEAD_DIM, CMP_HIDDEN), (CMP_LEN * HEAD_DIM) ** -0.5),
        'cmp_w2_v': nrm(ks[17], (L, CMP_HIDDEN, HEAD_DIM), CMP_HIDDEN ** -0.5),
        'norm_rnn_out': gain(ks[18], D_RNN),
        'norm_att_out': gain(ks[19], D_ATT),
        'w_out': nrm(ks[20], (L, D_RNN + D_ATT, D_MODEL), (D_RNN + D_ATT) ** -0.5),
        'post_norm_mix': gain(ks[21], D_MODEL),
        'pre_norm_mlp': gain(ks[22], D_MODEL),
        'w_ff1': nrm(ks[23], (L, D_MODEL, D_FF_2), D_MODEL ** -0.5),
        'w_ff2': nrm(ks[24], (L, D_FF_2, D_MODEL), D_FF_2 ** -0.5),
        'post_norm_mlp': gain(ks[25], D_MODEL),
    }

def second_block(x, c, ada_w, ada_b, pre_norm_mix, w_in, conv_w, conv_b, lru_wa, lru_ba, lru_wx, lru_bx,
              lru_lambda, cmp_pos_k, cmp_w1_k, cmp_w2_k, cmp_pos_v, cmp_w1_v, cmp_w2_v,
              norm_rnn_out, norm_att_out, w_out, post_norm_mix, pre_norm_mlp, w_ff1, w_ff2, post_norm_mlp):
    for l in range(DEPTH_2):
        mod = jax.nn.silu(c) @ ada_w[l] + ada_b[l]
        sh1, sc1, g1, sh2, sc2, g2 = jnp.split(mod, 6, axis=-1)
        h = modulate(rms_norm_2(x, pre_norm_mix[l]), sh1, sc1)
        y = hybrid_mixer(h, w_in[l], conv_w[l], conv_b[l], lru_wa[l], lru_ba[l], lru_wx[l], lru_bx[l],
                         lru_lambda[l], cmp_pos_k[l], cmp_w1_k[l], cmp_w2_k[l], cmp_pos_v[l], cmp_w1_v[l],
                         cmp_w2_v[l], norm_rnn_out[l], norm_att_out[l], w_out[l])
        x = x + (1.0 + g1[:, None, :]) * rms_norm_2(y, post_norm_mix[l])
        h = modulate(rms_norm_2(x, pre_norm_mlp[l]), sh2, sc2)
        y = jnp.square(jax.nn.relu(h @ w_ff1[l])) @ w_ff2[l]
        x = x + (1.0 + g2[:, None, :]) * rms_norm_2(y, post_norm_mlp[l])
    return x


def setup_inputs(seed=0):
    out = dict(first_inputs(seed))
    for name, value in second_inputs(seed + 1).items():
        if name != "x":
            out[name + "_2"] = value
    return out


def reference(
    x, norm1_g, w_in, a_vnorm_g, a_ws, a_bs, b_w, b_scale, c_norm_g, w_out, norm2_g, w_up,
    conv_w, conv_b, w_down, final_g, c_2, ada_w_2, ada_b_2, pre_norm_mix_2, w_in_2, conv_w_2,
    conv_b_2, lru_wa_2, lru_ba_2, lru_wx_2, lru_bx_2, lru_lambda_2, cmp_pos_k_2, cmp_w1_k_2,
    cmp_w2_k_2, cmp_pos_v_2, cmp_w1_v_2, cmp_w2_v_2, norm_rnn_out_2, norm_att_out_2, w_out_2,
    post_norm_mix_2, pre_norm_mlp_2, w_ff1_2, w_ff2_2, post_norm_mlp_2,
):
    x = first_block(
        x, norm1_g, w_in, a_vnorm_g, a_ws, a_bs, b_w, b_scale, c_norm_g, w_out, norm2_g, w_up,
        conv_w, conv_b, w_down, final_g,
    )
    return second_block(
        x, c_2, ada_w_2, ada_b_2, pre_norm_mix_2, w_in_2, conv_w_2, conv_b_2, lru_wa_2,
        lru_ba_2, lru_wx_2, lru_bx_2, lru_lambda_2, cmp_pos_k_2, cmp_w1_k_2, cmp_w2_k_2,
        cmp_pos_v_2, cmp_w1_v_2, cmp_w2_v_2, norm_rnn_out_2, norm_att_out_2, w_out_2,
        post_norm_mix_2, pre_norm_mlp_2, w_ff1_2, w_ff2_2, post_norm_mlp_2,
    )


_drawn_inputs = setup_inputs


def setup_inputs(seed=0):
    import zlib

    import numpy as np

    out = dict(_drawn_inputs(seed))
    spreads = {}
    factors = {'a_vnorm_g': 5.748, 'lru_ba_2': 56.751, 'lru_bx_2': 25.725, 'cmp_pos_k_2': 8.0}
    for name, (base, spread) in spreads.items():
        noise = np.random.default_rng([zlib.crc32(name.encode()), seed]).standard_normal(out[name].shape)
        drawn = base * np.exp(spread * noise) if base else spread * noise
        out[name] = __import__('jax').numpy.asarray(drawn.astype(out[name].dtype))
    for name, factor in factors.items():
        out[name] = (out[name] * factor).astype(out[name].dtype)
    return out
```

```python
import numpy as np
import concourse.bass as bass
from concourse import mybir
from contextlib import ExitStack

F32 = mybir.dt.float32
F32R = mybir.dt.float32r
ALU = mybir.AluOpType
ACT = mybir.ActivationFunctionType
AX = mybir.AxisListType

P = 128
S = 512
D = 1024
KT = D // P
LAYERS = 2
NT = S // P
DFF = 2816
GRP = 2 * P
NG = DFF // GRP
DFF2 = 4096
NG2 = DFF2 // GRP
HD = 64
CHUNK = 64
RET_HEADS = 8
EPS = 1e-6
SLABW = 2048
RING = 3
ADA_SLABS = 24
ADA_L = ADA_SLABS // LAYERS

W_IN, W_OUT = 11, 4
MLP0 = W_IN + W_OUT
LAYER_SLABS = MLP0 + 3 * NG
B2 = LAYERS * LAYER_SLABS
CMP0 = B2 + 5
RNN0 = CMP0 + 4
WO2 = RNN0 + 4
FF0 = WO2 + 4
SLABS = FF0 + 2 * NG2

PC_L, PC_LN = 0, 24
PC_CONV, PC_CONVN = 48, 16 * NG
PC_FINAL = PC_CONV + LAYERS * PC_CONVN
PC_C = PC_FINAL + 8
PC_ADAB = PC_C + 8
PC_PREMIX = PC_ADAB + 48
PC_POSTMIX = PC_PREMIX + 8
PC_PREMLP = PC_POSTMIX + 8
PC_POSTMLP = PC_PREMLP + 8
PC_RCONV = PC_POSTMLP + 8
PC_BA = PC_RCONV + 20
PC_BX = PC_BA + 4
PC_LAM = PC_BX + 4
PC_NRNN = PC_LAM + 4
PC_NATT = PC_NRNN + 4
PC_POS = PC_NATT + 4
PC_N = PC_POS + 32

N_CMP = 31
CMPC = 34
KKW = 16 * CMPC + 16
BANDW = 144
POOL_WINDOWS = (2, 4, 8, 16)
POS_COL = 32

C1 = {}
_at = 0
for _name, _w in (("ident", P), ("ones", P), ("head_mean", P), ("rot", P), ("cos", S), ("sin", S),
                  ("decay", RET_HEADS * S), ("band", 2 * 4 * BANDW)):
    C1[_name] = (_at, _w)
    _at += _w
C1_KEEP = 2 * P
C1_N = _at
C2 = {}
_at = 0
for _name, _w in (("dup", 2 * P), ("alibi", S), ("alibi_c", NT * 32), ("slopes", 8), ("seen", 1)):
    C2[_name] = (_at, _w)
    _at += _w
C2_N = _at


def constants():
    p = np.arange(P)
    t = np.arange(S)
    c1 = np.zeros((P, C1_N), np.float32)

    def put(table, where, name, value):
        a, w = where[name]
        table[:, a:a + w] = np.asarray(value, np.float32).reshape(P, w)

    put(c1, C1, "ident", np.eye(P))
    put(c1, C1, "ones", np.ones((P, P)))
    put(c1, C1, "head_mean", (p[:, None] // HD == p[None, :] // HD) / HD)
    rot = np.zeros((P, P))
    for m in range(P):
        if m % HD < HD // 2:
            rot[m + HD // 2, m] = -1.0
        else:
            rot[m - HD // 2, m] = 1.0
    put(c1, C1, "rot", rot)
    half = HD // 2
    inv = np.float32(10000.0) ** (-np.arange(half, dtype=np.float32) / np.float32(half))
    ang = (t.astype(np.float32)[None, :] * inv[p % half][:, None]).astype(np.float64)
    put(c1, C1, "cos", np.cos(ang))
    put(c1, C1, "sin", np.sin(ang))
    lg = np.log1p(-np.exp2(-5.0 - np.arange(RET_HEADS)))
    dist = np.abs(t[None, :] - p[:, None])
    ok = t[None, :] // CHUNK >= p[:, None] // CHUNK
    put(c1, C1, "decay", np.stack([np.where(ok, np.exp(g * dist), 0.0) * HD ** -0.5 for g in lg], 1))
    tb = np.arange(BANDW)
    band = np.zeros((P, 2, 4, BANDW))
    for first in range(2):
        for g, w in enumerate(POOL_WINDOWS):
            lag = tb[None, :] - p[:, None]
            cnt = np.minimum(tb + 1, w) if first == 0 else np.full(BANDW, w)
            band[:, first, g] = np.where((lag >= 0) & (lag < w), 1.0 / cnt[None, :], 0.0) - (lag == 0)
    put(c1, C1, "band", band)

    c2 = np.zeros((P, C2_N), np.float32)
    put(c2, C2, "dup", np.concatenate([(p[:, None] == g * HD + p[None, :] % HD) for g in range(2)], 1))
    d = p[:, None] + 384 - t[None, :]
    put(c2, C2, "alibi", np.where(d >= 0, d, 1e32))
    end = 16 * np.arange(32) + 31
    dc = (np.arange(NT) * P)[None, :, None] + p[:, None, None] - end[None, None, :]
    put(c2, C2, "alibi_c", np.where(dc >= 0, dc, 1e32))
    put(c2, C2, "slopes", np.broadcast_to(2.0 ** -(np.arange(8) + 1.0), (P, 8)))
    put(c2, C2, "seen", (p >= 31))
    return c1, c2


def build(nc, weights, ada, params, xin, wsT, bsb_in, bw_in, cst1, cst2, gatew, w2k, w2v_in, lruw, yout):
    ctx = ExitStack()
    with ctx:
        top = [16512]

        def at(name, shape, dt, offset):
            return nc.alloc_sbuf_tensor_at(name, shape, dt, offset=offset)

        def size(shape):
            return 4 * int(np.prod(shape[1:]))

        def keep(name, shape, dt=F32):
            t = at(name, shape, dt, top[0])
            top[0] += -(-size(shape) // 32) * 32
            return t

        def sem(name):
            return ctx.enter_context(nc.semaphore(name))

        x = keep("x", [P, KT, S])
        xh = keep("xh", [P, KT, S], F32R)
        xl = keep("xl", [P, KT, S], F32R)
        wh = keep("wh", [P, RING, SLABW], F32R)
        raw_at = top[0]
        raw = keep("raw", [P, RING, SLABW])
        wl = at("wl", [P, RING, SLABW], F32R, raw_at)
        prm = keep("prm", [P, PC_N])
        keep1 = keep("keep1", [P, C1_KEEP])
        mod = keep("mod", [P, 48])
        silu_c = keep("silu_c", [P, KT])
        eps = keep("eps", [P, 1])
        std = keep("std", [P, S])
        rstd = keep("rstd", [P, S])
        gains = keep("gains", [P, 4, KT])
        lru_c = keep("lru_c", [P, 6, 4])
        arena = top[0]
        ident = keep1[:, 0:P]
        ones = keep1[:, P:2 * P]

        t1 = keep("t1", [P, C1_N - C1_KEEP])

        def c1(name):
            a, w = C1[name]
            return t1[:, a - C1_KEEP:a - C1_KEEP + w]

        head_mean, rot, cos, sin = c1("head_mean"), c1("rot"), c1("cos"), c1("sin")
        decay = c1("decay")
        band = c1("band").rearrange("p (f g t) -> p f g t", f=2, g=4)
        ws = keep("ws", [P, LAYERS * 4, P])
        bsb = keep("bsb", [P, LAYERS * 2, P])
        bw = keep("bw", [P, LAYERS * 2, P])
        bw_cur = keep("bw_cur", [P, 2, P])
        kpad = keep("kpad", [P, 2, S])
        va_at = top[0]
        u = keep("u", [P, 2, S])
        va = keep("va", [P, NT, GRP])
        sqb = at("sqb", [P, 2, S], F32, va_at)
        nt = at("nt", [P, 2, S], F32, va_at + 4096)
        y = at("y", [P, 4, S], F32, va_at)
        st_at = top[0]
        xb = keep("xb", [P, NT, GRP])
        pooled = keep("pooled", [P, 2, S])
        rtmp = keep("rtmp", [P, 2, S])
        sT = at("sT", [P, 2, 1280], F32, st_at)
        gsq = at("gsq", [P, 4, S], F32, st_at)
        q_at = top[0]
        q = keep("q", [P, 4, S])
        k = keep("k", [P, 4, S])
        vr = keep("vr", [P, NT, S])
        sg = keep("sg", [P, 4, S])
        ya = keep("ya", [P, 2, S])
        vcur = keep("vcur", [P, NT, P])
        vss = keep("vss", [P, 3, NT])
        mix_end = top[0]
        ah = at("ah", [P, 2, 2, S], F32R, q_at)
        al = at("al", [P, 2, 2, S], F32R, q_at + 8192)
        cv = at("cv", [P, 4, S], F32, q_at + 16384)
        ab = at("ab", [P, 2, S], F32, q_at + 24576)
        adab = at("adab", [P, 8, GRP], F32, va_at + 8192)
        ada_acc = at("ada_acc", [P, GRP], F32, va_at + 16384)
        assert mix_end <= 229368, mix_end

        top[0] = arena
        t2 = keep("t2", [P, C2_N])

        def c2(name):
            a, w = C2[name]
            return t2[:, a:a + w]

        dup, alibi, slopes, seen = c2("dup"), c2("alibi"), c2("slopes"), c2("seen")
        alibi_c = c2("alibi_c").rearrange("p (i c) -> p i c", c=32)
        gw = keep("gw", [P, KT, 24])
        gwh = keep("gwh", [P, KT, 24], F32R)
        gwl = keep("gwl", [P, KT, 24], F32R)
        w2kp = keep("w2kp", [P, 2, 2, P])
        w2v = keep("w2v", [P, 2, HD])
        lru = keep("lru", [P, 2, 4, P])
        hid = keep("hid", [P, 2, 2, 2, 32])
        hbias = keep("hbias", [P, 4])
        kcT = keep("kcT", [P, 32])
        vcs = keep("vcs", [32, P])
        ptc = keep("ptc", [32, S])
        gates = keep("gates", [P, NT, 24])
        soft = keep("soft", [P, 4, 18])
        cst = keep("cst", [P, 4, NT])
        kcv_at = top[0]
        kcv = keep("kcv", [P, 2, S])
        vv = keep("vv", [P, NT, GRP])
        sqb2 = at("sqb2", [P, 2, S], F32, kcv_at)
        nt2 = at("nt2", [P, 2, S], F32, kcv_at + 4096)
        ksw = keep("ksw", [P, 2, S])
        q2 = keep("q2", [P, 4, S])
        qc = keep("qc", [P, 2, S])
        gg = keep("gg", [P, 4, S])
        cx = keep("cx", [P, 4, S])
        big = top[0]
        kkh = at("kkh", [P, 2, 2, KKW], F32R, big)
        kkl = at("kkl", [P, 2, 2, KKW], F32R, big + size([P, 2, 2, KKW]))
        rr = at("rr", [P, 4, S], F32, big)
        ii = at("ii", [P, 4, S], F32, big + 8192)
        mm = at("mm", [P, 4, S], F32, big + 16384)
        dd = at("dd", [P, 4, S], F32, big + 24576)
        att = at("att", [P, 4, S], F32, big)
        pb = at("pb", [P, 3, S], F32, big + 8192)
        tsl = at("tsl", [P, 2, S], F32, big + 14336)
        pt = at("pt", [P, 2, NT, S], F32, big + 18432)
        assert big + 18432 + 16384 <= 229368, big
        ymix = at("ymix", [P, KT, S], F32, big)
        ff_at = kcv_at + 8192
        ah2 = at("ah2", [P, 3, 2, S], F32R, ff_at)
        al2 = at("al2", [P, 3, 2, S], F32R, ff_at + 12288)
        rl = at("rl", [P, 2, S], F32, ff_at + 24576)
        ab2 = at("ab2", [P, 2, S], F32, ff_at + 28672)
        assert ff_at + 32768 <= big

        ps = ctx.enter_context(nc.psum_tensor("ps", [P, 8, S], F32))

        def bank(b):
            return ps[:, b, :]

        raw_loaded = [sem(f"raw_loaded{s}") for s in range(RING)]
        hi_made = sem("hi_made")
        slab_split = sem("slab_split")
        slab_used = sem("slab_used")
        x_loaded = sem("x_loaded")
        tables_loaded = sem("tables_loaded")
        eps_set = sem("eps_set")
        silu_c_ready = sem("silu_c_ready")
        lru_exp = sem("lru_exp")
        lru_step = sem("lru_step")
        sq_ready, sq_used = sem("sq_ready"), sem("sq_used")
        std_ready, rstd_ready = sem("std_ready"), sem("rstd_ready")
        nt_ready, nh_ready, nl_ready = sem("nt_ready"), sem("nh_ready"), sem("nl_ready")
        bw_ready = sem("bw_ready")
        kpad_zero = sem("kpad_zero")
        ws_masked = sem("ws_masked")
        proj_evac = sem("proj_evac")
        vss_ready, vstd_ready, vr_ready, va_ready = sem("vss_ready"), sem("vstd_ready"), sem("vrstd_ready"), sem("va_ready")
        rot_ready, rope_part, rope_done = sem("rot_ready"), sem("rope_part"), sem("rope_done")
        sv_ready, ya_part, ya_ready = sem("sv_ready"), sem("ya_part"), sem("ya_ready")
        pool_ready, pooled_ready, yb_ready = sem("pool_ready"), sem("pooled_ready"), sem("yb_ready")
        mix_hi, mix_split = sem("mix_hi"), sem("mix_split")
        staged, s_done, sT_ready = sem("staged"), sem("s_done"), sem("sT_ready")
        pv_done, y_evac = sem("pv_done"), sem("y_evac")
        mean_ready, yc_ready, gsq_ready = sem("mean_ready"), sem("yc_ready"), sem("gsq_ready")
        var_ready, gsd_ready, gr_ready = sem("var_ready"), sem("gsd_ready"), sem("gr_ready")
        yn_ready, gm_ready = sem("yn_ready"), sem("gm_ready")
        mix_added = sem("mix_added")
        cv_init, conv_mid, conv_done = sem("cv_init"), sem("conv_mid"), sem("conv_done")
        sil_ready, a_ready, ah_ready, act_split = sem("sil_ready"), sem("a_ready"), sem("ah_ready"), sem("act_split")
        down_done, ffn_added = sem("down_done"), sem("ffn_added")
        ada_loaded, ada_done, ada_evac = sem("ada_loaded"), sem("ada_done"), sem("ada_evac")
        ada_term, ada_summed = sem("ada_term"), sem("ada_summed")
        xf_ready = sem("xf_ready")
        tables2_loaded = sem("tables2_loaded")
        gains_ready = sem("gains_ready")
        zeroed = sem("zeroed")
        gwh_ready, gw_split = sem("gwh_ready"), sem("gw_split")
        proj2_evac = sem("proj2_evac")
        dup_ready, kkh_ready, kk_split = sem("dup_ready"), sem("kkh_ready"), sem("kk_split")
        gate_ready, gates_sig, gates_ready = sem("gate_ready"), sem("gates_sig"), sem("gates_ready")
        hbias_ready, hid_ready = sem("hbias_ready"), sem("hid_ready")
        kcv_ready, kcv_evac = sem("kcv_ready"), sem("kcv_evac")
        cx_init, cx_mid, cx_done = sem("cx_init"), sem("cx_mid"), sem("cx_done")
        lru_ready, sig_ready, th_ready, sqrt_ready = sem("lru_ready"), sem("sig_ready"), sem("th_ready"), sem("sqrt_ready")
        dd_ready, aa_ready, uu_ready, scan_ready, rnn_ready = (sem("dd_ready"), sem("aa_ready"), sem("uu_ready"),
                                                              sem("scan_ready"), sem("rnn_ready"))
        staged2, s2_done, sc_done, exp_done, rs_ready, p_ready = (sem("staged2"), sem("s2_done"), sem("sc_done"),
                                                                 sem("exp_done"), sem("rs_ready"), sem("p_ready"))
        cmp_step = sem("cmp_step")
        t_done, pt_evac, pv2_done, att_evac = sem("t_done"), sem("pt_evac"), sem("pv2_done"), sem("att_evac")
        sq4_ready, sq4_used, std4_ready, rstd4_ready = sem("sq4_ready"), sem("sq4_used"), sem("std4_ready"), sem("rstd4_ready")
        nt4_ready, nh4_ready, nl4_ready = sem("nt4_ready"), sem("nh4_ready"), sem("nl4_ready")
        y_ready = sem("y_ready")
        pn_ready, x2_ready = sem("pn_ready"), sem("x2_ready")
        y_zero = sem("y_zero")
        rl_ready, ab_ready, ah2_ready, act2_split = sem("rl_ready"), sem("ab_ready"), sem("ah2_ready"), sem("act2_split")
        down2_done, y2_added = sem("down2_done"), sem("y2_added")
        stored = sem("stored")

        block = ctx.enter_context(nc.Block())

        tensor_counts = (ada_done, pv_done, t_done, s2_done, pv2_done)
        scalar_counts = (y_evac, pt_evac, att_evac, rl_ready, ah2_ready)
        vector_counts = (ada_evac, ada_summed, conv_done, ffn_added, sc_done, a_ready, act_split, y2_added, act2_split, ab_ready)

        def past(eng, s, n):
            eng.wait_ge(s, n + 1)

        def col(i, n=1):
            return prm[:, i:i + n] if isinstance(i, int) else prm[:, bass.ds(i, n)]

        def cols(t, i, n):
            return t[:, i:i + n] if isinstance(i, int) else t[:, bass.ds(i, n)]

        q_f, D_f = q[:, :, :].rearrange("p a b -> p (a b)"), decay
        k_f, y_f = k[:, :, :].rearrange("p a b -> p (a b)"), y[:, :, :].rearrange("p a b -> p (a b)")
        q2_f, att_f = q2[:, :, :].rearrange("p a b -> p (a b)"), att[:, :, :].rearrange("p a b -> p (a b)")
        bsb_f = bsb[:, :, :].rearrange("p a b -> p (a b)")
        ws_f = ws[:, :, :].rearrange("p a b -> p (a b)")
        bw_f = bw[:, :, :].rearrange("p a b -> p (a b)")
        soffs = [0, 512, 896, 1152]
        sbank = [(0, 0), (1, 0), (2, 0), (1, 384)]

        @block.sync
        def _(sp):
            sp.dma_start(x[:, :, :], xin).then_inc(x_loaded, 16)

            def load(n, s):
                sp.wait_ge(slab_used, n + 1)
                sp.dma_start(raw[:, s, :], cols_dram(n)).then_inc(raw_loaded[s], 16)

            def cols_dram(n):
                return weights[n, :, :] if isinstance(n, int) else weights[bass.ds(n, 1), :, :].rearrange("a p c -> p (a c)")

            with sp.Fori(0, SLABS // RING) as i:
                for s in range(RING):
                    load(i * RING + s, s)
            for n in range(SLABS // RING * RING, SLABS):
                load(n, n % RING)
            for i in range(KT):
                sp.wait_ge(x2_ready, KT + i + 1)
                sp.dma_start(yout[:, i, :], x[:, i, :]).then_inc(stored, 16)
            sp.wait_ge(stored, 16 * KT)

        @block.gpsimd
        def _(pool):
            pool.memset(kpad[:, :, :], 0.0).then_inc(kpad_zero, 1)

            def low(n, s):
                pool.wait_ge(hi_made, n + 1)
                pool.tensor_tensor(wl[:, s, :], raw[:, s, :], wh[:, s, :].bitcast(F32), ALU.subtract).then_inc(slab_split, 1)

            with pool.Fori(0, SLABS // RING) as i:
                for s in range(RING):
                    low(i * RING + s, s)
            for n in range(SLABS // RING * RING, SLABS):
                low(n, n % RING)

        @block.tensor
        def _(pe):
            pe.sem_inc(slab_used, RING)
            for s in tensor_counts:
                pe.sem_inc(s, 1)

            def product(out, w_hi, w_lo, m_hi, m_lo, start, stop):
                pe.matmul(out, w_hi, m_hi, start=start, stop=False)
                pe.matmul(out, w_hi, m_lo, start=False, stop=False)
                return pe.matmul(out, w_lo, m_hi, start=False, stop=stop)

            def slab_fm(n, s, b0, fresh=None):
                pe.wait_ge(slab_split, n + 1)
                order = [(m, kt) for m in range(2) for kt in range(KT)]
                if fresh is not None:
                    order.sort(key=lambda o: o[1])
                for m, kt in order:
                    if fresh is not None and m == 0:
                        pe.wait_ge(nl_ready, fresh + kt + 1)
                    w = slice(kt * GRP + m * P, kt * GRP + m * P + P)
                    last = product(bank(b0 + m), wh[:, s, w], wl[:, s, w], xh[:, kt, :], xl[:, kt, :], kt == 0, kt == KT - 1)
                last.then_inc(slab_used, 1)

            def slab_tm(n, s, b0):
                pe.wait_ge(slab_split, n + 1)
                for i in range(NT):
                    out = ps[:, b0 + i // 2, (i % 2) * GRP:(i % 2 + 1) * GRP]
                    tok = slice(i * P, (i + 1) * P)
                    for kt in range(KT):
                        w = slice(kt * GRP, (kt + 1) * GRP)
                        last = product(out, xh[:, kt, tok], xl[:, kt, tok], wh[:, s, w], wl[:, s, w], kt == 0, kt == KT - 1)
                last.then_inc(slab_used, 1)

            def sum_squares(nk, buf):
                for i in range(KT):
                    pe.wait_ge(sq_ready, nk * KT + i + 1)
                    pe.matmul(bank(7), ones, buf[:, i % 2, :], start=(i == 0), stop=(i == KT - 1)).then_inc(sq_used, 1)

            def ada_part(a):
                past(pe, ada_summed, a + 1)
                past(pe, ada_evac, a)
                for m in range(2):
                    last = pe.matmul(ps[:, 7, m:m + 1], ada_acc[:, m * P:(m + 1) * P], ones[:, 0:1], start=True, stop=True)
                last.then_inc(ada_done, 1)

            pe.wait_ge(tables_loaded, 16 * 6)
            pe.wait_ge(silu_c_ready, 1)
            pe.wait_ge(kpad_zero, 1)
            with pe.Fori(0, LAYERS) as l:
                n0 = l * LAYER_SLABS
                past(pe, ada_evac, l * ADA_L)
                sum_squares(l * 2, sqb)
                kinds = ["fm", "tm", "tm", "fm", "fm", "fm", "fm", "tm", "tm", "fm", "fm"]
                for c in range(W_IN):
                    if c >= 2:
                        pe.wait_ge(proj_evac, l * W_IN + c - 1)
                    if kinds[c] == "fm":
                        slab_fm(n0 + c, c % RING, 2 * (c % 2), fresh=l * 2 * KT if c == 0 else None)
                    else:
                        slab_tm(n0 + c, c % RING, 2 * (c % 2))
                    if c in (5, 7):
                        src, o = (q, 0) if c == 5 else (k, 4)
                        pe.wait_ge(proj_evac, l * W_IN + (5 if c == 5 else 7))
                        for i in range(4):
                            if o:
                                pe.wait_ge(rope_part, l * 8 + i + 1)
                            pe.matmul(bank(4 + i), rot, src[:, i, :], start=True, stop=True).then_inc(rot_ready, 1)
                pe.wait_ge(va_ready, l + 1)
                pe.wait_ge(rope_part, l * 8 + 8)
                for i in range(NT):
                    for j in range(2):
                        last = pe.matmul(ps[:, 4 + i, j * 256:(j + 1) * 256], va[:, i, j * P:(j + 1) * P],
                                         cols(ws_f, l * 512 + j * 256, 256), start=True, stop=True)
                last.then_inc(sv_ready, 1)
                pe.wait_ge(proj_evac, l * W_IN + W_IN)
                for g in range(4):
                    pair = slice((g // 2) * P, (g // 2 + 1) * P)
                    for j in range(NT):
                        pe.matmul(ps[:, g, j * P:(j + 1) * P], xb[:, j, pair], band[:, min(j, 1), g, 0:P], start=(j == 0), stop=False)
                    for j in range(NT - 1):
                        last = pe.matmul(ps[:, g, (j + 1) * P:(j + 1) * P + BANDW - P], xb[:, j, pair], band[:, 1, g, P:BANDW],
                                         start=False, stop=(j == NT - 2))
                    last.then_inc(pool_ready, 1)
                pe.wait_ge(bw_ready, l + 1)
                pe.wait_ge(ya_ready, l * 2 + 2)
                pe.wait_ge(pooled_ready, l * 4 + 4)
                for j in range(2):
                    pe.matmul(bank(4 + j), bw_cur[:, j, :], pooled[:, j, :], start=True, stop=True).then_inc(yb_ready, 1)
                with pe.Fori(0, 4) as pr:
                    h0 = l * 8 + pr * 2
                    pe.wait_ge(mix_split, l * 8 + 4)
                    pe.wait_ge(staged, l * 4 + pr + 1)
                    for hh in range(2):
                        for j in range(NT):
                            b, o = sbank[j]
                            w = S - j * P
                            last = pe.matmul(ps[:, 3 * hh + b, o:o + w], kpad[:, hh, j * P:(j + 1) * P],
                                             cols(q_f, pr * S + j * P, w), start=True, stop=True)
                        last.then_inc(s_done, 1)
                    past(pe, y_evac, l * 4 + pr)
                    for hh in range(2):
                        pe.wait_ge(sT_ready, h0 + hh + 1)
                        for j in range(NT):
                            w = S - j * P
                            last = pe.matmul(ps[:, 6 + hh, j * P:S], vcur[:, j, :], sT[:, hh, soffs[j]:soffs[j] + w],
                                             start=(j == 0), stop=(j == NT - 1))
                        last.then_inc(pv_done, 1)
                past(pe, y_evac, l * 4 + 4)
                for i in range(4):
                    pe.matmul(bank(i), head_mean, y[:, i, :], start=True, stop=True).then_inc(mean_ready, 1)
                for i in range(4):
                    pe.wait_ge(gsq_ready, l * 4 + i + 1)
                    pe.matmul(bank(4 + i), head_mean, gsq[:, i, :], start=True, stop=True).then_inc(var_ready, 1)
                pe.wait_ge(mix_split, l * 8 + 8)
                for w in range(W_OUT):
                    c = W_IN + w
                    if w >= 2:
                        pe.wait_ge(mix_added, l * KT + 2 * (w - 1))
                    slab_fm(n0 + c, c % RING, 2 * (c % 2))
                sum_squares(l * 2 + 1, sqb)

                def up(j, n, s, fresh=None):
                    past(pe, conv_done, l * 4 * NG + j * 4)
                    slab_fm(n, s, 0, fresh)
                    slab_fm(n + 1, (s + 1) % RING, 2)

                def down(j, par, n, s):
                    past(pe, act_split, l * 2 * NG + j * 2 + 2)
                    pe.wait_ge(slab_split, n + 1)
                    past(pe, ffn_added, l * 8 * NG + j * 8)
                    for o in range(KT):
                        if o >= 3:
                            past(pe, ffn_added, l * 8 * NG + j * 8 + o - 2)
                        for kt in range(2):
                            w = slice(kt * D + o * P, kt * D + o * P + P)
                            last = product(bank(4 + o % 3), wh[:, s, w], wl[:, s, w], ah[:, par, kt, :], al[:, par, kt, :],
                                           kt == 0, kt == 1)
                        last.then_inc(down_done if o < KT - 1 else slab_used, 1)

                up(0, n0 + MLP0, MLP0 % RING, fresh=l * 2 * KT + KT)
                ada_part(l * ADA_L)
                with pe.Fori(0, (NG - 1) // 2) as it:
                    for v in range(2):
                        j = it * 2 + (1 + v)
                        n = n0 + it * 6 + (MLP0 + 2 + 3 * v)
                        up(j, n, (MLP0 + 2) % RING)
                        down(it * 2 + v, v, n + 2, (MLP0 + 4) % RING)
                        ada_part(l * ADA_L + j)
                down(NG - 1, 0, n0 + (LAYER_SLABS - 1), (LAYER_SLABS - 1) % RING)
                ada_part(l * ADA_L + (ADA_L - 1))

            past(pe, ada_evac, LAYERS * ADA_L)
            sum_squares(4, sqb)
            pe.wait_ge(tables2_loaded, 16 * 5)
            sum_squares(5, sqb2)
            pe.wait_ge(gw_split, 1)
            for c, kind in enumerate(("fm", "fm", "tm", "fm", "fm")):
                n = B2 + c
                if c >= 2:
                    pe.wait_ge(proj2_evac, c - 1)
                if kind == "fm":
                    slab_fm(n, n % RING, 2 * (c % 2), fresh=4 * KT if c == 0 else None)
                else:
                    slab_tm(n, n % RING, 2 * (c % 2))
                if c == 2:
                    pe.wait_ge(proj2_evac, 1)
                    for kv in range(2):
                        for g in range(2):
                            pe.matmul(bank(4 + 2 * kv + g), dup[:, g * P:(g + 1) * P], kcv[:, kv, :], start=True,
                                      stop=True).then_inc(dup_ready, 1)
            pe.wait_ge(kk_split, 4)
            for i in range(NT):
                tok = slice(i * P, (i + 1) * P)
                for kt in range(KT):
                    last = product(ps[:, 4, i * 24:(i + 1) * 24], xh[:, kt, tok], xl[:, kt, tok], gwh[:, kt, :], gwl[:, kt, :],
                                   kt == 0, kt == KT - 1)
            last.then_inc(gate_ready, 1)
            pe.wait_ge(proj2_evac, 4)
            for kv in range(2):
                for part in range(2):
                    n = CMP0 + 2 * kv + part
                    s = n % RING
                    pe.wait_ge(slab_split, n + 1)
                    for a8 in range(8):
                        a = part * 8 + a8
                        mh = kkh[:, kv, :, 2 * a:2 * a + 16 * (CMPC - 1) + 1:16]
                        ml = kkl[:, kv, :, 2 * a:2 * a + 16 * (CMPC - 1) + 1:16]
                        for m in range(2):
                            w = slice(a8 * GRP + m * P, a8 * GRP + m * P + P)
                            out = ps[:, 2 + 4 * kv + m, 0:2 * CMPC].rearrange("p (g c) -> p g c", g=2)
                            last = product(out, wh[:, s, w], wl[:, s, w], mh, ml, a == 0, a == 15)
                    last.then_inc(slab_used, 1)
            for c in range(4):
                n = RNN0 + c
                if c == 0:
                    pe.wait_ge(proj2_evac, 5)
                if c == 1:
                    pe.wait_ge(hid_ready, 4)
                if c >= 2:
                    pe.wait_ge(cx_done, 2 * (c - 1))
                slab_fm(n, n % RING, 2 * (c % 2))
                if c == 1:
                    pe.wait_ge(hid_ready, 8)
                    pe.wait_ge(gates_sig, 1)
                    for m in range(2):
                        for g in range(2):
                            last = pe.matmul(ps[:, 4, 0:N_CMP], w2kp[:, m, g, :], hid[:, 0, m, g, 0:N_CMP],
                                             start=(m == 0 and g == 0), stop=(m == 1 and g == 1))
                    for g in range(2):
                        for m in range(2):
                            last = pe.matmul(ps[0:N_CMP, 5, g * HD:(g + 1) * HD], hid[:, 1, m, g, 0:N_CMP], w2v[:, m, :],
                                             start=(m == 0), stop=(m == 1))
                    last.then_inc(kcv_ready, 1)
            pe.wait_ge(kcv_evac, 2)
            pe.wait_ge(cx_done, 4)
            pe.wait_ge(proj2_evac, 7)
            for i in range(4):
                pe.matmul(bank(4 + i), lru[:, 0, i, :], cx[:, i, :], start=True, stop=True).then_inc(lru_ready, 1)
            for i in range(4):
                pe.matmul(bank(i), lru[:, 1, i, :], cx[:, i, :], start=True, stop=True).then_inc(lru_ready, 1)
            pe.wait_ge(sig_ready, 8)
            pe.wait_ge(gates_ready, 1)

            with pe.Fori(0, 4) as r:
                def scores(U):
                    g, v = U // 9, U % 9
                    past(pe, sc_done, r * 18 + (U - 2 if U >= 3 else 0))
                    if v < 8:
                        i = v % 4
                        w = (i + 1) * P
                        pe.matmul(ps[:, U % 3, 0:w], qc[:, g, i * P:(i + 1) * P], ksw[:, v // 4, 0:w], start=True,
                                  stop=True).then_inc(s2_done, 1)
                    else:
                        for i in range(NT):
                            last = pe.matmul(ps[:, U % 3, i * 32:i * 32 + N_CMP], qc[:, g, i * P:(i + 1) * P], kcT[:, 0:N_CMP],
                                             start=True, stop=True)
                        last.then_inc(s2_done, 1)

                def turn(U):
                    v = U % 9
                    pe.wait_ge(p_ready, r * 18 + U + 1)
                    past(pe, pt_evac, r * 18 + (U - 2 if U >= 3 else 0))
                    if v < 8:
                        for j in range(v % 4 + 1):
                            last = pe.transpose(ps[:, 3 + U % 3, j * P:(j + 1) * P], pb[:, U % 3, j * P:(j + 1) * P], ident)
                    else:
                        for i in range(NT):
                            last = pe.transpose(ps[0:N_CMP, 3 + U % 3, i * P:(i + 1) * P], pb[:, U % 3, i * 32:i * 32 + N_CMP],
                                                ident)
                    last.then_inc(t_done, 1)

                def values(g):
                    past(pe, pt_evac, r * 18 + 9 * g + 9)
                    past(pe, att_evac, r * 2)
                    for b in range(2):
                        for j in range(NT):
                            pe.matmul(ps[:, 6 + g, j * P:S], vv[:, j, b * P:(b + 1) * P], pt[:, b, j, j * P:S],
                                      start=(b == 0 and j == 0), stop=False)
                    pe.matmul(bank(6 + g), vcs[0:N_CMP, :], ptc[0:N_CMP, :], start=False, stop=True).then_inc(pv2_done, 1)

                pe.wait_ge(staged2, r + 1)
                scores(0)
                scores(1)
                for U in range(18):
                    if U + 2 < 18:
                        scores(U + 2)
                    turn(U)
                    if U % 9 == 8:
                        values(U // 9)

            for b in range(2):
                for i in range(4):
                    pe.wait_ge(sq4_ready, 4 * b + i + 1)
                    pe.matmul(bank(7), ones, sqb2[:, i % 2, :], start=(i == 0), stop=(i == 3)).then_inc(sq4_used, 1)
            pe.wait_ge(nl4_ready, 8)
            for w in range(4):
                n = WO2 + w
                if w >= 2:
                    pe.wait_ge(y_ready, 2 * (w - 1))
                slab_fm(n, n % RING, 2 * (w % 2))
            sum_squares(6, sqb2)
            sum_squares(7, sqb2)

            def up2(g, n, s, fresh=None):
                past(pe, rl_ready, g * 2)
                slab_fm(n, s, 0, fresh)

            def down2(g, par, n, s):
                past(pe, act2_split, g * 2 + 2)
                pe.wait_ge(slab_split, n + 1)
                past(pe, y2_added, g * 8)
                for o in range(KT):
                    if o >= 4:
                        past(pe, y2_added, g * 8 + o - 3)
                    for kt in range(2):
                        w = slice(kt * D + o * P, kt * D + o * P + P)
                        last = product(bank(2 + o % 4), wh[:, s, w], wl[:, s, w], ah2[:, par, kt, :], al2[:, par, kt, :],
                                       kt == 0, kt == 1)
                    last.then_inc(down2_done if o < KT - 1 else slab_used, 1)

            up2(0, FF0, FF0 % RING, fresh=5 * KT)
            with pe.Fori(0, (NG2 - 1) // 3) as it:
                for v in range(3):
                    n = it * 6 + (FF0 + 1 + 2 * v)
                    up2(it * 3 + (1 + v), n, (FF0 + 1 + 2 * v) % RING)
                    down2(it * 3 + v, v, n + 1, (FF0 + 2 + 2 * v) % RING)
            down2(NG2 - 1, (NG2 - 1) % 3, SLABS - 1, (SLABS - 1) % RING)
            sum_squares(8, sqb2)

        @block.scalar
        def _(act):
            for s in scalar_counts:
                act.sem_inc(s, 1)
            for dst, src in ((prm[:, :], params), (keep1[:, :], cst1[:, 0:C1_KEEP]), (t1[:, :], cst1[:, C1_KEEP:C1_N]),
                             (ws[:, :, :], wsT), (bsb[:, :, :], bsb_in), (bw[:, :, :], bw_in)):
                act.dma_start(dst, src).then_inc(tables_loaded, 16)

            def high(n, s, third):
                act.wait_ge(raw_loaded[s], third * 16 + 16)
                act.activation(wh[:, s, :], raw[:, s, :], ACT.Copy).then_inc(hi_made, 1)

            def used(n):
                act.wait_ge(slab_used, n + 1 + RING)

            def ahead(c, base, thirds):
                high(base + c + RING, (c + RING) % RING, thirds + (c + RING) // RING)

            def squares(nk, buf, src, waits):
                for i in range(KT):
                    waits(i)
                    if i >= 2:
                        act.wait_ge(sq_used, nk * KT + i - 1)
                    act.activation(buf[:, i % 2, :], src[:, i, :], ACT.Square).then_inc(sq_ready, 1)
                act.wait_ge(sq_used, nk * KT + KT)
                act.activation(std[:, :], bank(7), ACT.Sqrt, bias=eps[:, :], scale=1.0 / D).then_inc(std_ready, 1)

            def highs(sk, buf, shift=None):
                for i in range(KT):
                    act.wait_ge(nt_ready, sk * KT + i + 1)
                    if shift is None:
                        act.activation(xh[:, i, :], buf[:, i % 2, :], ACT.Copy).then_inc(nh_ready, 1)
                    else:
                        act.activation(xh[:, i, :], buf[:, i % 2, :], ACT.Identity, bias=mod[:, shift + i:shift + i + 1])\
                           .then_inc(nh_ready, 1)

            for s in range(RING):
                high(s, s, 0)
            act.wait_ge(tables_loaded, 16 * 6)
            act.activation(silu_c[:, :], col(PC_C, KT), ACT.Silu).then_inc(silu_c_ready, 1)
            act.wait_ge(lru_step, 1)
            act.activation(lru_c[:, 1, :], lru_c[:, 0, :], ACT.Exp, scale=-1.0).then_inc(lru_exp, 1)
            act.wait_ge(x_loaded, 16)
            act.wait_ge(eps_set, 1)

            with act.Fori(0, LAYERS) as l:
                n0 = l * LAYER_SLABS
                n3 = l * (LAYER_SLABS // RING)
                past(act, ffn_added, l * 8 * NG)
                squares(l * 2, sqb, x, lambda i: None)
                act.activation(bw_cur[:, :, :].rearrange("p a b -> p (a b)"), cols(bw_f, l * 256, 256), ACT.Copy).then_inc(bw_ready, 1)
                highs(l * 2, nt)
                for c in range(W_IN):
                    used(n0 + c)
                    b0 = 2 * (c % 2)
                    for m in range(2):
                        tok2 = ps[:, b0 + m, :].rearrange("p (i d) -> p i d", i=2)
                        if c == 0:
                            last = act.activation(u[:, m, :], bank(b0 + m), ACT.Gelu_apprx_tanh)
                        elif c == 1:
                            last = act.activation(va[:, 2 * m:2 * m + 2, :], tok2, ACT.Gelu_apprx_tanh)
                        elif c == 2:
                            last = act.activation(xb[:, 2 * m:2 * m + 2, :], tok2, ACT.Copy)
                        elif c in (3, 4):
                            last = act.activation(q[:, 2 * (c - 3) + m, :], bank(b0 + m), ACT.Copy)
                        elif c in (5, 6):
                            last = act.activation(k[:, 2 * (c - 5) + m, :], bank(b0 + m), ACT.Copy)
                        elif c in (7, 8):
                            last = act.activation(vr[:, 2 * m:2 * m + 2, (c - 7) * 256:(c - 6) * 256], tok2, ACT.Copy)
                        else:
                            last = act.activation(sg[:, 2 * (c - 9) + m, :], bank(b0 + m), ACT.Silu)
                    last.then_inc(proj_evac, 1)
                    ahead(c, n0, n3)
                    if c == 1:
                        act.wait_ge(proj_evac, l * W_IN + 2)
                        for i in range(NT):
                            last = act.activation(ya[:, i // 2, (i % 2) * GRP:(i % 2 + 1) * GRP], va[:, i, :], ACT.Square, accum_out=vss[:, 0, i:i + 1])
                        last.then_inc(vss_ready, 1)
                    if c == 2:
                        act.wait_ge(vss_ready, l + 1)
                        act.activation(vss[:, 1, :], vss[:, 0, :], ACT.Sqrt, bias=eps[:, :], scale=1.0 / GRP).then_inc(vstd_ready, 1)
                for g in range(4):
                    act.wait_ge(pool_ready, l * 4 + g + 1)
                    h = slice(HD * (g % 2), HD * (g % 2) + HD)
                    act.activation(pooled[h, g // 2, :], ps[h, g, :], ACT.Copy).then_inc(pooled_ready, 1)
                for j in range(2):
                    act.wait_ge(ya_ready, l * 2 + j + 1)
                    act.activation(xh[:, j, :], ya[:, j, :], ACT.Copy).then_inc(mix_hi, 1)
                for j in range(2):
                    act.wait_ge(yb_ready, l * 2 + j + 1)
                    act.activation(xh[:, 2 + j, :], bank(4 + j), ACT.Copy, scale=col(l * PC_LN + (PC_L + 10 + j))).then_inc(mix_hi, 1)
                act.wait_ge(rope_done, l * 8 + 8)
                act.wait_ge(kpad_zero, 1)
                with act.Fori(0, 4) as pr:
                    past(act, pv_done, l * 8 + pr * 2)
                    for hh in range(2):
                        h = slice(HD * hh, HD * hh + HD)
                        act.activation(kpad[h, hh, :], k_f[h, bass.ds(pr * S, S)], ACT.Copy)
                    act.activation(vcur[:, :, :], vr[:, :, bass.ds(pr * P, P)], ACT.Copy).then_inc(staged, 1)
                    past(act, pv_done, l * 8 + pr * 2 + 2)
                    for hh in range(2):
                        h = slice(HD * hh, HD * hh + HD)
                        last = act.activation(y_f[h, bass.ds(pr * S, S)], ps[h, 6 + hh, :], ACT.Copy)
                    last.then_inc(y_evac, 1)
                for i in range(4):
                    act.wait_ge(yc_ready, l * 4 + i + 1)
                    act.activation(gsq[:, i, :], y[:, i, :], ACT.Square).then_inc(gsq_ready, 1)
                for i in range(4):
                    act.wait_ge(var_ready, l * 4 + i + 1)
                    act.activation(gsq[:, i, :], bank(4 + i), ACT.Sqrt, bias=eps[:, :]).then_inc(gsd_ready, 1)
                for i in range(4):
                    act.wait_ge(gm_ready, l * 4 + i + 1)
                    act.activation(xh[:, 4 + i, :], y[:, i, :], ACT.Copy).then_inc(mix_hi, 1)
                for w in range(W_OUT):
                    used(n0 + W_IN + w)
                    ahead(W_IN + w, n0, n3)
                squares(l * 2 + 1, sqb, x, lambda i: act.wait_ge(mix_added, l * KT + i + 1))
                highs(l * 2 + 1, nt)

                def ada_load(a):
                    past(act, ada_summed, a)
                    act.dma_start(adab[:, :, :].rearrange("p k c -> p (k c)"),
                                  ada[bass.ds(a, 1), :, :].rearrange("a p c -> p (a c)")).then_inc(ada_loaded, 16)

                def conv_tap(r, j):
                    c = l * PC_CONVN + j * 16 + (PC_CONV + r * 4)
                    act.activation(cv[:, r, :], bank(r), ACT.Identity, bias=col(c + 3), scale=col(c + 2)).then_inc(cv_init, 1)

                def mlp_step(j, base, thirds, c, par):
                    used(base + c)
                    for r in range(2):
                        conv_tap(r, j)
                    ahead(c, base, thirds)
                    past(act, conv_done, l * 4 * NG + j * 4 + 2)
                    for r in range(2):
                        act.activation(cv[:, r, :], cv[:, r, :], ACT.Silu).then_inc(sil_ready, 1)
                    used(base + c + 1)
                    for r in range(2, 4):
                        conv_tap(r, j)
                    ahead(c + 1, base, thirds)
                    for r in range(2):
                        past(act, a_ready, l * 2 * NG + j * 2 + r + 1)
                        act.activation(ah[:, par, r, :], ab[:, r, :], ACT.Copy).then_inc(ah_ready, 1)

                ada_load(l * ADA_L)
                mlp_step(0, n0, n3, MLP0, 0)
                with act.Fori(0, (NG - 1) // 2) as it:
                    for v in range(2):
                        j = it * 2 + (1 + v)
                        base, thirds, c = n0 + it * 6, n3 + it * 2, MLP0 + 2 + 3 * v
                        ada_load(l * ADA_L + j)
                        mlp_step(j, base, thirds, c, (1 + v) % 2)
                        used(base + c + 2)
                        ahead(c + 2, base, thirds)
                ada_load(l * ADA_L + (ADA_L - 1))
                used(n0 + (LAYER_SLABS - 1))
                ahead(LAYER_SLABS - 1, n0, n3)

            past(act, ffn_added, LAYERS * 8 * NG)
            squares(4, sqb, x, lambda i: None)
            act.wait_ge(xf_ready, KT)
            for dst, src in ((t2[:, :], cst2), (gw[:, :, :], gatew), (w2kp[:, :, :, :], w2k), (w2v[:, :, :], w2v_in),
                             (lru[:, :, :, :], lruw)):
                act.dma_start(dst, src).then_inc(tables2_loaded, 16)
            squares(5, sqb2, x, lambda i: None)
            act.wait_ge(tables2_loaded, 16 * 5)
            act.activation(gwh[:, :, :], gw[:, :, :], ACT.Copy).then_inc(gwh_ready, 1)
            act.wait_ge(gains_ready, 4)
            highs(4, nt2, shift=0)

            def after(n):
                if n + RING < SLABS:
                    high(n + RING, n % RING, (n + RING) // RING)

            act.wait_ge(zeroed, 1)
            for c in range(5):
                n = B2 + c
                used(n)
                b0 = 2 * (c % 2)
                for m in range(2):
                    if c == 0:
                        last = act.activation(kcv[:, m, :], bank(b0 + m), ACT.Copy)
                    elif c == 1:
                        last = act.activation(ksw[:, m, :], bank(b0 + m), ACT.Copy)
                    elif c == 2:
                        last = act.activation(vv[:, 2 * m:2 * m + 2, :], ps[:, b0 + m, :].rearrange("p (i d) -> p i d", i=2), ACT.Copy)
                    else:
                        last = act.activation(q2[:, 2 * (c - 3) + m, :], bank(b0 + m), ACT.Copy, scale=-HD ** -0.5)
                last.then_inc(proj2_evac, 1)
                after(n)
                if c == 2:
                    for kv in range(2):
                        for g in range(2):
                            act.wait_ge(dup_ready, 2 * kv + g + 1)
                            act.activation(kkh[0:HD, kv, g, 0:S], ps[0:HD, 4 + 2 * kv + g, :], ACT.Copy)
                            act.activation(kkh[HD:P, kv, g, 0:S - 1], ps[HD:P, 4 + 2 * kv + g, 1:S], ACT.Copy)
                            act.activation(kkh[:, kv, g, S:S + 31:2], col(PC_POS + 16 * kv, 16), ACT.Copy).then_inc(kkh_ready, 1)
            act.wait_ge(gate_ready, 1)
            act.activation(gates[:, :, :].rearrange("p i c -> p (i c)"), ps[:, 4, 0:NT * 24], ACT.Sigmoid).then_inc(gates_sig, 1)
            for kv in range(2):
                for part in range(2):
                    used(CMP0 + 2 * kv + part)
                    after(CMP0 + 2 * kv + part)
                for m in range(2):
                    act.activation(hbias[:, 2 * kv + m:2 * kv + m + 1], ps[:, 2 + 4 * kv + m, POS_COL:POS_COL + 1], ACT.Copy)\
                       .then_inc(hbias_ready, 1)
                act.wait_ge(hbias_ready, 2 * kv + 2)
                for m in range(2):
                    for g in range(2):
                        act.activation(hid[:, kv, m, g, 0:N_CMP], ps[:, 2 + 4 * kv + m, g * CMPC:g * CMPC + N_CMP],
                                       ACT.Gelu_apprx_tanh, bias=hbias[:, 2 * kv + m:2 * kv + m + 1]).then_inc(hid_ready, 1)
            for c in range(4):
                n = RNN0 + c
                used(n)
                for m in range(2):
                    i = 2 * (c % 2) + m
                    if c < 2:
                        act.activation(cx[:, i, :], bank(2 * (c % 2) + m), ACT.Identity, bias=col(PC_RCONV + 5 * i + 4),
                                       scale=col(PC_RCONV + 5 * i + 3)).then_inc(cx_init, 1)
                    else:
                        last = act.activation(gg[:, i, :], bank(2 * (c % 2) + m), ACT.Gelu_apprx_tanh)
                if c >= 2:
                    last.then_inc(proj2_evac, 1)
                after(n)
                if c == 1:
                    act.wait_ge(kcv_ready, 1)
                    act.activation(kcT[:, 0:N_CMP], ps[:, 4, 0:N_CMP], ACT.Copy).then_inc(kcv_evac, 1)
                    act.activation(vcs[0:N_CMP, :], ps[0:N_CMP, 5, 0:P], ACT.Copy).then_inc(kcv_evac, 1)
            for i in range(4):
                act.wait_ge(lru_ready, i + 1)
                act.activation(rr[:, i, :], bank(4 + i), ACT.Sigmoid, bias=col(PC_BA + i)).then_inc(sig_ready, 1)
            for i in range(4):
                act.wait_ge(lru_ready, 5 + i)
                act.activation(ii[:, i, :], bank(i), ACT.Sigmoid, bias=col(PC_BX + i)).then_inc(sig_ready, 1)
            act.wait_ge(sig_ready, 8)
            act.wait_ge(lru_step, 14)
            for i in range(4):
                act.activation(rr[:, i, :], rr[:, i, :], ACT.Tanh, scale=lru_c[:, 5, i:i + 1]).then_inc(th_ready, 1)
            act.wait_ge(th_ready, 4)
            for i in range(4):
                act.activation(mm[:, i, :], rr[:, i, :], ACT.Sqrt, scale=-1.0).then_inc(sqrt_ready, 1)
            act.wait_ge(rnn_ready, 4)

            with act.Fori(0, 4) as r:
                past(act, s2_done, r * 18)
                past(act, sc_done, r * 18)
                for g in range(2):
                    h = slice(HD * g, HD * g + HD)
                    act.activation(qc[h, g, :], q2_f[h, bass.ds(r * S, S)], ACT.Copy)
                for g in range(2):
                    last = act.activation(tsl[:, g, :], alibi, ACT.Copy, scale=slopes[:, bass.ds(r + 4 * g, 1)])
                last.then_inc(staged2, 1)

                def exps(U):
                    past(act, sc_done, r * 18 + U + 1)
                    if U % 9 < 8:
                        w = (U % 9 % 4 + 1) * P
                        act.activation(pb[:, U % 3, 0:w], pb[:, U % 3, 0:w], ACT.Exp, bias=soft[:, 0, U:U + 1], scale=-1.0,
                                       accum_out=soft[:, 1, U:U + 1]).then_inc(exp_done, 1)
                    else:
                        act.activation(pb[:, U % 3, 0:P], pb[:, U % 3, 0:P], ACT.Exp, scale=-1.0).then_inc(exp_done, 1)

                def keep_turned(U):
                    g, v = U // 9, U % 9
                    past(act, t_done, r * 18 + U + 1)
                    past(act, pv2_done, r * 2 + g)
                    if v < 8:
                        i = v % 4
                        act.activation(pt[:, v // 4, 0:i + 1, i * P:(i + 1) * P],
                                       ps[:, 3 + U % 3, 0:(i + 1) * P].rearrange("p (j t) -> p j t", t=P), ACT.Copy)\
                           .then_inc(pt_evac, 1)
                    else:
                        act.activation(ptc[0:N_CMP, :], ps[0:N_CMP, 3 + U % 3, :], ACT.Copy).then_inc(pt_evac, 1)

                def head_out(g):
                    h = slice(HD * g, HD * g + HD)
                    past(act, pv2_done, r * 2 + g + 1)
                    act.activation(att_f[h, bass.ds(r * S, S)], ps[h, 6 + g, :], ACT.Copy).then_inc(att_evac, 1)

                for U in range(18):
                    exps(U)
                    if U >= 2:
                        keep_turned(U - 2)
                    if U == 12:
                        head_out(0)
                keep_turned(16)
                keep_turned(17)
                head_out(1)

            past(act, att_evac, 8)
            for b, src in enumerate((cx, att)):
                for i in range(4):
                    if 4 * b + i >= 2:
                        act.wait_ge(sq4_used, 4 * b + i - 1)
                    act.activation(sqb2[:, i % 2, :], src[:, i, :], ACT.Square).then_inc(sq4_ready, 1)
                act.wait_ge(sq4_used, 4 * b + 4)
                if b:
                    act.wait_ge(rstd4_ready, 1)
                act.activation(std[:, :], bank(7), ACT.Sqrt, bias=eps[:, :], scale=2.0 / D).then_inc(std4_ready, 1)
                for i in range(4):
                    act.wait_ge(nt4_ready, 4 * b + i + 1)
                    act.activation(xh[:, 4 * b + i, :], nt2[:, i % 2, :], ACT.Copy).then_inc(nh4_ready, 1)
            for w in range(4):
                n = WO2 + w
                used(n)
                for m in range(2):
                    act.activation(ymix[:, 2 * w + m, :], bank(2 * (w % 2) + m), ACT.Copy).then_inc(y_ready, 1)
                after(n)
            act.wait_ge(y_ready, 8)
            squares(6, sqb2, ymix, lambda i: None)
            squares(7, sqb2, x, lambda i: act.wait_ge(x2_ready, i + 1))
            highs(5, nt2, shift=24)

            def relu_step(g, n, thirds, n_s, par):
                used(n)
                past(act, ab_ready, g * 2)
                past(act, ah2_ready, g * 2)
                for r in range(2):
                    act.activation(rl[:, r, :], bank(r), ACT.Relu).then_inc(rl_ready, 1)
                for r in range(2):
                    past(act, rl_ready, g * 2 + r + 1)
                    act.activation(ah2[:, par, r, :], rl[:, r, :], ACT.Square).then_inc(ah2_ready, 1)
                if n_s is not None:
                    high(n + RING, n_s, thirds)

            relu_step(0, FF0, (FF0 + RING) // RING, FF0 % RING, 0)
            with act.Fori(0, (NG2 - 1) // 3 - 1) as it:
                for v in range(3):
                    c = FF0 + 1 + 2 * v
                    n = it * 6 + c
                    relu_step(it * 3 + (1 + v), n, it * 2 + (c + RING) // RING, c % RING, (1 + v) % 3)
                    used(n + 1)
                    high(n + 1 + RING, (c + 1) % RING, it * 2 + (c + 1 + RING) // RING)
            for g in range(NG2 - 3, NG2):
                n = FF0 - 1 + 2 * g
                relu_step(g, n, (n + RING) // RING, n % RING if n + RING < SLABS else None, g % 3)
                used(n + 1)
                after(n + 1)
            past(act, y2_added, 8 * NG2)
            squares(8, sqb2, ymix, lambda i: None)

        @block.vector
        def _(dve):
            for s in vector_counts:
                dve.sem_inc(s, 1)
            dve.memset(eps[:, :], EPS).then_inc(eps_set, 1)
            dve.wait_ge(tables_loaded, 16 * 6)
            dve.wait_ge(silu_c_ready, 1)
            dve.memset(ws[HD:P, :, 0:HD], 0.0).then_inc(ws_masked, 1)
            lam = col(PC_LAM, 4)
            step = [0]

            def lru_op(ins):
                step[0] += 1
                ins.then_inc(lru_step, 1)
                dve.wait_ge(lru_step, step[0])

            lru_op(dve.scalar_tensor_tensor(lru_c[:, 0, :], lam, -1.0, lam, ALU.mult, ALU.max))
            dve.wait_ge(lru_exp, 1)
            lru_op(dve.tensor_scalar(lru_c[:, 2, :], lru_c[:, 1, :], 2.0, None, ALU.add))
            lru_op(dve.reciprocal(lru_c[:, 2, :], lru_c[:, 2, :]))
            lru_op(dve.tensor_tensor(lru_c[:, 3, :], lru_c[:, 1, :], lru_c[:, 2, :], ALU.mult))
            lru_op(dve.tensor_tensor(lru_c[:, 4, :], lru_c[:, 3, :], lru_c[:, 3, :], ALU.mult))
            lru_op(dve.tensor_scalar(lru_c[:, 5, :], lru_c[:, 4, :], 1.0 / 15, None, ALU.mult))
            for odd in (13, 11, 9, 7, 5, 3):
                lru_op(dve.scalar_tensor_tensor(lru_c[:, 5, :], lru_c[:, 5, :], 1.0 / odd, lru_c[:, 4, :], ALU.add, ALU.mult))
            lru_op(dve.scalar_tensor_tensor(lru_c[:, 3, :], lru_c[:, 5, :], 1.0, lru_c[:, 3, :], ALU.add, ALU.mult))
            lru_op(dve.tensor_scalar(lru_c[:, 2, :], lam, 0.0, 4.0, ALU.min, ALU.mult))
            dve.scalar_tensor_tensor(lru_c[:, 5, :], lru_c[:, 3, :], -8.0, lru_c[:, 2, :], ALU.mult, ALU.add).then_inc(lru_step, 1)

            def inverse(nk):
                dve.wait_ge(std_ready, nk + 1)
                dve.reciprocal(rstd[:, :], std[:, :]).then_inc(rstd_ready, 1)
                dve.wait_ge(rstd_ready, nk + 1)

            def normalise(nk, sk, buf, gain, shift=None):
                inverse(nk)

                def low(i):
                    dve.wait_ge(nh_ready, sk * KT + i + 1)
                    if shift is None:
                        ins = dve.tensor_tensor(xl[:, i, :], buf[:, i % 2, :], xh[:, i, :].bitcast(F32), ALU.subtract)
                    else:
                        ins = dve.scalar_tensor_tensor(xl[:, i, :], buf[:, i % 2, :], mod[:, shift + i:shift + i + 1],
                                                       xh[:, i, :].bitcast(F32), ALU.add, ALU.subtract)
                    ins.then_inc(nl_ready, 1)

                for i in range(KT):
                    if i >= 2:
                        dve.wait_ge(nl_ready, sk * KT + i - 1)
                    dve.scalar_tensor_tensor(buf[:, i % 2, :], x[:, i, :], gain(i), rstd[:, :], ALU.mult, ALU.mult).then_inc(nt_ready, 1)
                    if i >= 1:
                        low(i - 1)
                low(KT - 1)

            with dve.Fori(0, LAYERS) as l:
                normalise(l * 2, l * 2, nt, lambda i: col(l * PC_LN + (PC_L + i)))
                dve.wait_ge(vstd_ready, l + 1)
                dve.reciprocal(vss[:, 2, :], vss[:, 1, :]).then_inc(vr_ready, 1)
                dve.wait_ge(vr_ready, l + 1)
                for i in range(NT):
                    last = dve.tensor_scalar(va[:, i, :], va[:, i, :], vss[:, 2, i:i + 1], None, ALU.mult)
                last.then_inc(va_ready, 1)
                for i in range(8):
                    t = q if i < 4 else k
                    dve.wait_ge(rot_ready, l * 8 + i + 1)
                    if i >= 2:
                        dve.wait_ge(rope_done, l * 8 + i - 1)
                    dve.tensor_tensor(rtmp[:, i % 2, :], bank(4 + i % 4), sin, ALU.mult)
                    dve.tensor_tensor(t[:, i % 4, :], t[:, i % 4, :], cos, ALU.mult).then_inc(rope_part, 1)
                    dve.wait_ge(rope_part, l * 8 + i + 1)
                    dve.tensor_tensor(t[:, i % 4, :], t[:, i % 4, :], rtmp[:, i % 2, :], ALU.add).then_inc(rope_done, 1)
                dve.wait_ge(sv_ready, l + 1)
                for j in range(2):
                    for hh in range(2):
                        h = slice(HD * hh, HD * hh + HD)
                        o = ya[h, j, :].rearrange("p (i t) -> p i t", i=NT)
                        b = bsb_f[h, bass.ds(l * 256 + j * P, P)].rearrange("p (a t) -> p a t", a=1).broadcast_to((HD, NT, P))
                        dve.scalar_tensor_tensor(o, ps[h, 4:8, j * 256 + hh * P:j * 256 + hh * P + P],
                                                 prm[h, bass.ds(l * PC_LN + (PC_L + 8 + j), 1)], b, ALU.mult, ALU.add).then_inc(ya_part, 1)
                for j in range(2):
                    dve.wait_ge(ya_part, l * 4 + 2 * j + 2)
                    dve.tensor_tensor(ya[:, j, :], ya[:, j, :], u[:, j, :], ALU.mult).then_inc(ya_ready, 1)
                for j in range(2):
                    dve.wait_ge(mix_hi, l * 8 + j + 1)
                    dve.tensor_tensor(xl[:, j, :], ya[:, j, :], xh[:, j, :].bitcast(F32), ALU.subtract).then_inc(mix_split, 1)
                for j in range(2):
                    dve.wait_ge(mix_hi, l * 8 + j + 3)
                    dve.scalar_tensor_tensor(xl[:, 2 + j, :], bank(4 + j), col(l * PC_LN + (PC_L + 10 + j)),
                                             xh[:, 2 + j, :].bitcast(F32), ALU.mult, ALU.subtract).then_inc(mix_split, 1)
                with dve.Fori(0, 4) as pr:
                    past(dve, pv_done, l * 8 + pr * 2)
                    for hh in range(2):
                        dve.wait_ge(s_done, l * 8 + pr * 2 + hh + 1)
                        for j in range(NT):
                            b, o = sbank[j]
                            w = S - j * P
                            last = dve.tensor_tensor(sT[:, hh, soffs[j]:soffs[j] + w], ps[:, 3 * hh + b, o:o + w],
                                                     cols(D_f, pr * (2 * S) + hh * S, w), ALU.mult)
                        last.then_inc(sT_ready, 1)
                for i in range(4):
                    dve.wait_ge(mean_ready, l * 4 + i + 1)
                    dve.tensor_tensor(y[:, i, :], y[:, i, :], bank(i), ALU.subtract).then_inc(yc_ready, 1)
                for i in range(4):
                    dve.wait_ge(gsd_ready, l * 4 + i + 1)
                    dve.reciprocal(gsq[:, i, :], gsq[:, i, :]).then_inc(gr_ready, 1)
                for i in range(4):
                    dve.wait_ge(gr_ready, l * 4 + i + 1)
                    dve.scalar_tensor_tensor(y[:, i, :], y[:, i, :], col(l * PC_LN + (PC_L + 12 + i)), gsq[:, i, :], ALU.mult,
                                             ALU.mult).then_inc(yn_ready, 1)
                for i in range(4):
                    dve.wait_ge(yn_ready, l * 4 + i + 1)
                    dve.tensor_tensor(y[:, i, :], y[:, i, :], sg[:, i, :], ALU.mult).then_inc(gm_ready, 1)
                for i in range(4):
                    dve.wait_ge(mix_hi, l * 8 + i + 5)
                    dve.tensor_tensor(xl[:, 4 + i, :], y[:, i, :], xh[:, 4 + i, :].bitcast(F32), ALU.subtract).then_inc(mix_split, 1)
                for w in range(W_OUT):
                    dve.wait_ge(slab_used, l * LAYER_SLABS + (W_IN + w + 1 + RING))
                    for m in range(2):
                        i = 2 * w + m
                        dve.tensor_tensor(x[:, i, :], x[:, i, :], bank(2 * ((W_IN + w) % 2) + m), ALU.add).then_inc(mix_added, 1)
                normalise(l * 2 + 1, l * 2 + 1, nt, lambda i: col(l * PC_LN + (PC_L + 16 + i)))

                def conv(j, half):
                    c0 = l * PC_CONVN + j * 16 + PC_CONV
                    for r in (2 * half, 2 * half + 1):
                        dve.wait_ge(cv_init, l * 4 * NG + j * 4 + r + 1)
                        dve.scalar_tensor_tensor(cv[:, r, 1:S], ps[:, r, 0:S - 1], col(c0 + (r * 4 + 1)), cv[:, r, 1:S],
                                                 ALU.mult, ALU.add).then_inc(conv_mid, 1)
                    for r in (2 * half, 2 * half + 1):
                        dve.wait_ge(conv_mid, l * 4 * NG + j * 4 + r + 1)
                        dve.scalar_tensor_tensor(cv[:, r, 2:S], ps[:, r, 0:S - 2], col(c0 + r * 4), cv[:, r, 2:S],
                                                 ALU.mult, ALU.add).then_inc(conv_done, 1)

                def gate(j, par):
                    past(dve, conv_done, l * 4 * NG + j * 4 + 4)
                    past(dve, act_split, l * 2 * NG + j * 2)
                    for r in range(2):
                        dve.wait_ge(sil_ready, l * 2 * NG + j * 2 + r + 1)
                        dve.tensor_tensor(ab[:, r, :], cv[:, r, :], cv[:, 2 + r, :], ALU.mult).then_inc(a_ready, 1)
                    for r in range(2):
                        dve.wait_ge(ah_ready, l * 2 * NG + j * 2 + r + 1)
                        dve.tensor_tensor(al[:, par, r, :], ab[:, r, :], ah[:, par, r, :].bitcast(F32), ALU.subtract).then_inc(act_split, 1)

                def add_down(j, n):
                    for o in range(KT):
                        if o < KT - 1:
                            dve.wait_ge(down_done, l * (KT - 1) * NG + j * (KT - 1) + o + 1)
                        else:
                            dve.wait_ge(slab_used, n + 1 + RING)
                        dve.tensor_tensor(x[:, o, :], x[:, o, :], bank(4 + o % 3), ALU.add).then_inc(ffn_added, 1)

                def ada_sum(a):
                    dve.wait_ge(ada_loaded, a * 16 + 16)
                    past(dve, ada_done, a)
                    for kt in range(KT):
                        if kt == 0:
                            ins = dve.tensor_scalar(ada_acc[:, :], adab[:, 0, :], silu_c[:, 0:1], None, ALU.mult)
                        else:
                            dve.wait_ge(ada_term, a * (KT - 1) + kt)
                            ins = dve.scalar_tensor_tensor(ada_acc[:, :], adab[:, kt, :], silu_c[:, kt:kt + 1], ada_acc[:, :],
                                                           ALU.mult, ALU.add)
                        ins.then_inc(ada_term if kt < KT - 1 else ada_summed, 1)

                def ada_out(a):
                    past(dve, ada_done, a + 1)
                    dve.tensor_tensor(cols(mod, a * 2, 2), ps[:, 7, 0:2], col(a * 2 + PC_ADAB, 2), ALU.add).then_inc(ada_evac, 1)

                n0 = l * LAYER_SLABS
                conv(0, 0)
                ada_sum(l * ADA_L)
                conv(0, 1)
                gate(0, 0)
                ada_out(l * ADA_L)
                with dve.Fori(0, (NG - 1) // 2) as it:
                    for v in range(2):
                        j = it * 2 + (1 + v)
                        conv(j, 0)
                        ada_sum(l * ADA_L + j)
                        conv(j, 1)
                        add_down(it * 2 + v, n0 + it * 6 + (MLP0 + 4 + 3 * v))
                        gate(j, (1 + v) % 2)
                        ada_out(l * ADA_L + j)
                ada_sum(l * ADA_L + (ADA_L - 1))
                add_down(NG - 1, n0 + (LAYER_SLABS - 1))
                ada_out(l * ADA_L + (ADA_L - 1))

            inverse(4)
            for i in range(KT):
                dve.scalar_tensor_tensor(x[:, i, :], x[:, i, :], col(PC_FINAL + i), rstd[:, :], ALU.mult, ALU.mult).then_inc(xf_ready, 1)
            past(dve, ada_evac, LAYERS * ADA_L)
            for n, (scale, g) in enumerate(((8, PC_PREMIX), (16, PC_POSTMIX), (32, PC_PREMLP), (40, PC_POSTMLP))):
                dve.scalar_tensor_tensor(gains[:, n, :], mod[:, scale:scale + KT], 1.0, col(g, KT), ALU.add, ALU.mult).then_inc(gains_ready, 1)
            dve.wait_ge(gwh_ready, 1)
            dve.tensor_tensor(gwl[:, :, :], gw[:, :, :], gwh[:, :, :].bitcast(F32), ALU.subtract).then_inc(gw_split, 1)
            dve.memset(kkh[:, :, :, :].bitcast(F32), 0.0)
            dve.memset(kkl[:, :, :, :].bitcast(F32), 0.0)
            dve.memset(qc[:, :, :], 0.0).then_inc(zeroed, 1)
            dve.wait_ge(gains_ready, 4)
            normalise(5, 4, nt2, lambda i: gains[:, 0, i:i + 1], shift=0)
            dve.wait_ge(zeroed, 1)
            for kv in range(2):
                for g in range(2):
                    dve.wait_ge(kkh_ready, 2 * kv + g + 1)
                    b = 4 + 2 * kv + g
                    dve.tensor_tensor(kkl[0:HD, kv, g, 0:S], ps[0:HD, b, :], kkh[0:HD, kv, g, 0:S].bitcast(F32), ALU.subtract)
                    dve.tensor_tensor(kkl[HD:P, kv, g, 0:S - 1], ps[HD:P, b, 1:S], kkh[HD:P, kv, g, 0:S - 1].bitcast(F32), ALU.subtract)
                    dve.tensor_tensor(kkl[:, kv, g, S:S + 31:2], col(PC_POS + 16 * kv, 16), kkh[:, kv, g, S:S + 31:2].bitcast(F32),
                                      ALU.subtract).then_inc(kk_split, 1)
            dve.wait_ge(gates_sig, 1)
            dve.tensor_scalar(gates[:, 0, 0:8], gates[:, 0, 0:8], seen, None, ALU.mult).then_inc(gates_ready, 1)
            for c in range(2):
                for tap in (1, 2, 3):
                    for m in range(2):
                        i = 2 * c + m
                        if tap == 1:
                            dve.wait_ge(cx_init, i + 1)
                        else:
                            dve.wait_ge(cx_mid, 4 * c + 2 * (tap - 2) + m + 1)
                        dve.scalar_tensor_tensor(cx[:, i, tap:S], ps[:, i, 0:S - tap], col(PC_RCONV + 5 * i + 3 - tap), cx[:, i, tap:S],
                                                 ALU.mult, ALU.add).then_inc(cx_mid if tap < 3 else cx_done, 1)
            dve.wait_ge(cx_done, 4)
            dve.wait_ge(sig_ready, 8)
            for i in range(4):
                dve.tensor_tensor(ii[:, i, :], ii[:, i, :], cx[:, i, :], ALU.mult)
            for i in range(4):
                dve.wait_ge(th_ready, i + 1)
                dve.tensor_scalar(dd[:, i, :], rr[:, i, :], -1.0, 1.0, ALU.mult, ALU.add).then_inc(dd_ready, 1)
            for i in range(4):
                dve.wait_ge(dd_ready, i + 1)
                dve.reciprocal(dd[:, i, :], dd[:, i, :]).then_inc(dd_ready, 1)
            for i in range(4):
                dve.wait_ge(dd_ready, 5 + i)
                dve.wait_ge(sqrt_ready, i + 1)
                dve.scalar_tensor_tensor(rr[:, i, :], rr[:, i, :], 1.0, dd[:, i, :], ALU.add, ALU.mult)
                dve.scalar_tensor_tensor(mm[:, i, :], mm[:, i, :], 2.0, dd[:, i, :], ALU.mult, ALU.mult).then_inc(aa_ready, 1)
            for i in range(4):
                dve.wait_ge(aa_ready, i + 1)
                dve.tensor_tensor(mm[:, i, :], mm[:, i, :], ii[:, i, :], ALU.mult).then_inc(uu_ready, 1)
            for i in range(4):
                dve.wait_ge(uu_ready, i + 1)
                dve.tensor_tensor_scan(cx[:, i, :], rr[:, i, :], mm[:, i, :], 0.0, ALU.mult, ALU.add).then_inc(scan_ready, 1)
            dve.wait_ge(proj2_evac, 7)
            for i in range(4):
                dve.wait_ge(scan_ready, i + 1)
                dve.tensor_tensor(cx[:, i, :], cx[:, i, :], gg[:, i, :], ALU.mult).then_inc(rnn_ready, 1)

            dve.wait_ge(gates_ready, 1)
            with dve.Fori(0, 4) as r:
                dve.wait_ge(staged2, r + 1)

                def minima(U):
                    g, v = U // 9, U % 9
                    past(dve, s2_done, r * 18 + U + 1)
                    past(dve, t_done, r * 18 + (U - 2 if U >= 3 else 0))
                    if v < 8:
                        i = v % 4
                        w = (i + 1) * P
                        dve.memset(soft[:, 3, U:U + 1], 0.0)
                        dve.tensor_tensor_reduce(out=pb[:, U % 3, 0:w], in0=ps[:, U % 3, 0:w], in1=tsl[:, g, S - w:S], scale=1.0,
                                                 scalar=3e38, op0=ALU.add, op1=ALU.min, accum_out=soft[:, 0, U:U + 1]).then_inc(sc_done, 1)
                    else:
                        s3 = pb[:, U % 3, 0:P].rearrange("p (i c) -> p i c", c=32)
                        c31 = s3[:, :, 0:N_CMP]
                        base = r * 12 + 6 * g
                        dve.memset(pb[:, U % 3, 0:P], 0.0).then_inc(cmp_step, 1)
                        dve.wait_ge(cmp_step, base + 1)
                        dve.scalar_tensor_tensor(c31, alibi_c[:, :, 0:N_CMP], slopes[:, bass.ds(r + 4 * g, 1)],
                                                 ps[:, U % 3, 0:P].rearrange("p (i c) -> p i c", c=32)[:, :, 0:N_CMP],
                                                 ALU.mult, ALU.add).then_inc(cmp_step, 1)
                        dve.wait_ge(cmp_step, base + 2)
                        dve.tensor_reduce(cst[:, 0, :], c31, AX.X, ALU.min).then_inc(cmp_step, 1)
                        dve.wait_ge(cmp_step, base + 3)
                        dve.tensor_tensor(c31, c31, cst[:, 0, :].rearrange("p (i a) -> p i a", a=1).broadcast_to((P, NT, N_CMP)),
                                          ALU.subtract).then_inc(sc_done, 1)

                def weigh(U):
                    g, v = U // 9, U % 9
                    dve.wait_ge(exp_done, r * 18 + U + 1)
                    if v < 8:
                        i = v % 4
                        w = (i + 1) * P
                        dve.reciprocal(soft[:, 2, U:U + 1], soft[:, 1, U:U + 1]).then_inc(rs_ready, 1)
                        dve.wait_ge(rs_ready, r * 16 + 8 * g + v + 1)
                        dve.tensor_scalar(pb[:, U % 3, 0:w], pb[:, U % 3, 0:w], soft[:, 2, U:U + 1],
                                          gates[:, i, bass.ds(r + ((1 + v // 4) * 8 + 4 * g), 1)], ALU.mult, ALU.mult).then_inc(p_ready, 1)
                    else:
                        c31 = pb[:, U % 3, 0:P].rearrange("p (i c) -> p i c", c=32)[:, :, 0:N_CMP]
                        base = r * 12 + 6 * g
                        dve.tensor_reduce(cst[:, 1, :], c31, AX.X, ALU.add).then_inc(cmp_step, 1)
                        dve.wait_ge(cmp_step, base + 4)
                        dve.reciprocal(cst[:, 2, :], cst[:, 1, :]).then_inc(cmp_step, 1)
                        dve.wait_ge(cmp_step, base + 5)
                        dve.tensor_tensor(cst[:, 3, :], cst[:, 2, :], gates[:, :, bass.ds(r + 4 * g, 1)].rearrange("p i a -> p (i a)"),
                                          ALU.mult).then_inc(cmp_step, 1)
                        dve.wait_ge(cmp_step, base + 6)
                        dve.tensor_tensor(c31, c31, cst[:, 3, :].rearrange("p (i a) -> p i a", a=1).broadcast_to((P, NT, N_CMP)),
                                          ALU.mult).then_inc(p_ready, 1)

                for U in range(18):
                    minima(U)
                    if U >= 1:
                        weigh(U - 1)
                weigh(17)

            for b, (src, g) in enumerate(((cx, PC_NRNN), (att, PC_NATT))):
                dve.wait_ge(std4_ready, b + 1)
                dve.reciprocal(rstd[:, :], std[:, :]).then_inc(rstd4_ready, 1)
                dve.wait_ge(rstd4_ready, b + 1)

                def low4(i):
                    dve.wait_ge(nh4_ready, 4 * b + i + 1)
                    dve.tensor_tensor(xl[:, 4 * b + i, :], nt2[:, i % 2, :], xh[:, 4 * b + i, :].bitcast(F32), ALU.subtract).then_inc(nl4_ready, 1)

                for i in range(4):
                    if 4 * b + i >= 2:
                        dve.wait_ge(nl4_ready, 4 * b + i - 1)
                    dve.scalar_tensor_tensor(nt2[:, i % 2, :], src[:, i, :], col(g + i), rstd[:, :], ALU.mult, ALU.mult).then_inc(nt4_ready, 1)
                    if i >= 1:
                        low4(i - 1)
                low4(3)

            def post_norm(nk, n, first):
                inverse(nk)
                for i in range(KT + 1):
                    if i < KT:
                        dve.scalar_tensor_tensor(ymix[:, i, :], ymix[:, i, :], gains[:, n, i:i + 1], rstd[:, :], ALU.mult, ALU.mult)\
                           .then_inc(pn_ready, 1)
                    if i >= 1:
                        dve.wait_ge(pn_ready, first + i)
                        dve.tensor_tensor(x[:, i - 1, :], x[:, i - 1, :], ymix[:, i - 1, :], ALU.add).then_inc(x2_ready, 1)

            post_norm(6, 1, 0)
            dve.wait_ge(x2_ready, KT)
            dve.memset(ymix[:, :, :], 0.0).then_inc(y_zero, 1)
            normalise(7, 5, nt2, lambda i: gains[:, 2, i:i + 1], shift=24)
            dve.wait_ge(y_zero, 1)

            def relu_step(g, par):
                past(dve, act2_split, g * 2)
                for r in range(2):
                    past(dve, rl_ready, g * 2 + r + 1)
                    dve.tensor_tensor(ab2[:, r, :], rl[:, r, :], rl[:, r, :], ALU.mult).then_inc(ab_ready, 1)
                for r in range(2):
                    past(dve, ab_ready, g * 2 + r + 1)
                    past(dve, ah2_ready, g * 2 + r + 1)
                    dve.tensor_tensor(al2[:, par, r, :], ab2[:, r, :], ah2[:, par, r, :].bitcast(F32), ALU.subtract).then_inc(act2_split, 1)

            def add_down2(g, n):
                for o in range(KT):
                    if o < KT - 1:
                        dve.wait_ge(down2_done, g * (KT - 1) + o + 1)
                    else:
                        dve.wait_ge(slab_used, n + 1 + RING)
                    dve.tensor_tensor(ymix[:, o, :], ymix[:, o, :], bank(2 + o % 4), ALU.add).then_inc(y2_added, 1)

            relu_step(0, 0)
            with dve.Fori(0, (NG2 - 1) // 3) as it:
                for v in range(3):
                    add_down2(it * 3 + v, it * 6 + (FF0 + 2 + 2 * v))
                    relu_step(it * 3 + (1 + v), (1 + v) % 3)
            add_down2(NG2 - 1, SLABS - 1)
            post_norm(8, 3, KT)


def slab8(w):
    return w.reshape(KT, P, GRP).transpose(1, 0, 2).reshape(P, SLABW)


def slab2(w):
    return w.reshape(2, P, D).transpose(1, 0, 2).reshape(P, SLABW)


def columns(v):
    return v.reshape(-1, P).T


def kernel(**inputs):
    import concourse.bacc as bacc
    from concourse.bass_utils import run_bass_kernel_spmd

    a = {n: np.asarray(v) for n, v in inputs.items()}
    f = np.float32
    pairs = np.concatenate([np.r_[r * HD:(r + 1) * HD, (4 + r) * HD:(5 + r) * HD] for r in range(4)])

    slabs = np.empty((SLABS, P, SLABW), f)
    n = 0

    def add(slab):
        nonlocal n
        slabs[n] = slab
        n += 1

    for l in range(LAYERS):
        for c in range(W_IN):
            add(slab8(a["w_in"][l][:, c * GRP:(c + 1) * GRP]))
        for c in range(W_OUT):
            add(slab8(a["w_out"][l][:, c * GRP:(c + 1) * GRP]))
        for j in range(NG):
            add(slab8(a["w_up"][l][:, j * GRP:(j + 1) * GRP]))
            add(slab8(a["w_up"][l][:, DFF + j * GRP:DFF + (j + 1) * GRP]))
            if j:
                add(slab2(a["w_down"][l][(j - 1) * GRP:j * GRP]))
        add(slab2(a["w_down"][l][DFF - GRP:]))
    w2 = a["w_in_2"][0]
    heads = w2[:, 1024:1536][:, pairs]
    rest = {m: w2[:, 1536 + P * i:1536 + P * (i + 1)] for i, m in enumerate(("kc", "vc", "ks", "vs", "kw", "vw"))}
    add(slab8(np.concatenate([rest["kc"], rest["vc"]], 1)))
    add(slab8(np.concatenate([rest["ks"], rest["kw"]], 1)))
    add(slab8(np.concatenate([rest["vs"], rest["vw"]], 1)))
    add(slab8(heads[:, 0:GRP]))
    add(slab8(heads[:, GRP:]))
    for w1 in (a["cmp_w1_k_2"][0], a["cmp_w1_v_2"][0]):
        for part in range(2):
            add(slab8(w1[part * D:(part + 1) * D]))
    for c in (2, 3, 0, 1):
        add(slab8(w2[:, c * GRP:(c + 1) * GRP]))
    wo = a["w_out_2"][0]
    wo = np.concatenate([wo[0:512], wo[512:][pairs]], 0)
    for c in range(4):
        add(slab8(wo[:, c * GRP:(c + 1) * GRP]))
    for g in range(NG2):
        add(slab8(a["w_ff1_2"][0][:, g * GRP:(g + 1) * GRP]))
        if g:
            add(slab2(a["w_ff2_2"][0][(g - 1) * GRP:g * GRP]))
    add(slab2(a["w_ff2_2"][0][DFF2 - GRP:]))
    assert n == SLABS

    ada = np.stack([slab8(a["ada_w_2"][0][:, i * GRP:(i + 1) * GRP]) for i in range(ADA_SLABS)])

    prm = []
    for l in range(LAYERS):
        prm += [columns(a[m][l]) for m in ("norm1_g", "a_vnorm_g", "b_scale", "c_norm_g", "norm2_g")]
    for l in range(LAYERS):
        taps = np.concatenate([a["conv_w"][l], a["conv_b"][l][None]], 0).reshape(4, 2, NG, 2, P)
        prm.append(taps.transpose(4, 2, 1, 3, 0).reshape(P, PC_CONVN))
    prm += [columns(a["final_g"]), columns(a["c_2"][0]), columns(a["ada_b_2"][0])]
    prm += [columns(a[m][0]) for m in ("pre_norm_mix_2", "post_norm_mix_2", "pre_norm_mlp_2", "post_norm_mlp_2")]
    taps = np.concatenate([a["conv_w_2"][0], a["conv_b_2"][0][None]], 0).reshape(5, 4, P)
    prm.append(taps.transpose(2, 1, 0).reshape(P, 20))
    prm += [columns(a[m][0]) for m in ("lru_ba_2", "lru_bx_2", "lru_lambda_2", "norm_rnn_out_2")]
    prm.append(columns(a["norm_att_out_2"][0][pairs]))
    prm += [columns(a["cmp_pos_k_2"][0].reshape(-1)), columns(a["cmp_pos_v_2"][0].reshape(-1))]
    prm = np.ascontiguousarray(np.concatenate(prm, 1))

    def half_pairs(w):
        out = np.zeros((P, len(w) // 2, P), f)
        for i in range(len(w)):
            o = HD * (i % 2)
            out[o:o + HD, i // 2, o:o + HD] = w[i]
        return out

    bs = a["a_bs"].reshape(LAYERS * 2, 2, P)
    w2k = np.zeros((P, 2, 2, P), f)
    for m in range(2):
        for g in range(2):
            w2k[:, m, g, g * HD:(g + 1) * HD] = a["cmp_w2_k_2"][0][m * P:(m + 1) * P]
    c1, c2 = constants()
    arrays = {
        "weights": slabs,
        "ada": ada,
        "params": prm,
        "xin": a["x"][0].T.reshape(KT, P, S).transpose(1, 0, 2),
        "wsT": a["a_ws"].reshape(LAYERS * 4, P, P).transpose(2, 0, 1),
        "bsb": np.repeat(bs.transpose(1, 0, 2), HD, axis=0),
        "bw": half_pairs(a["b_w"].reshape(LAYERS * 4, HD, HD)),
        "cst1": c1,
        "cst2": c2,
        "gatew": w2[:, 2304:2328].reshape(KT, P, 24).transpose(1, 0, 2),
        "w2k": w2k,
        "w2v": a["cmp_w2_v_2"][0].reshape(2, P, HD).transpose(1, 0, 2),
        "lruw": np.stack([half_pairs(a["lru_wa_2"][0]), half_pairs(a["lru_wx_2"][0])], 1),
    }
    nc = bacc.Bacc("TRN2", target_bir_lowering=False, num_devices=1)
    args = []
    feed = {}
    for name, v in arrays.items():
        feed[f"in_{name}"] = np.ascontiguousarray(v)
        args.append(nc.dram_tensor(f"in_{name}", v.shape, F32, kind="ExternalInput").ap())
    yout = nc.dram_tensor("out_y", (P, KT, S), F32, kind="ExternalOutput").ap()
    build(nc, *args, yout)
    got = run_bass_kernel_spmd(nc, [feed], core_ids=[0]).results[0]["out_y"]
    return np.ascontiguousarray(got.transpose(1, 0, 2).reshape(D, S).T)[None]
```

```python
import numpy as np
import concourse.bass as bass
from concourse import mybir
from contextlib import ExitStack

F32 = mybir.dt.float32
F32R = mybir.dt.float32r
ALU = mybir.AluOpType
ACT = mybir.ActivationFunctionType
AX = mybir.AxisListType

P = 128
S = 512
D = 1024
KT = D // P
LAYERS = 2
NT = S // P
DFF = 2816
GRP = 2 * P
NG = DFF // GRP
DFF2 = 4096
NG2 = DFF2 // GRP
HD = 64
CHUNK = 64
RET_HEADS = 8
EPS = 1e-6
SLABW = 2048
RING = 3
ADA_SLABS = 24

W_IN, W_OUT = 11, 4
MLP0 = W_IN + W_OUT
LAYER_SLABS = MLP0 + 3 * NG
B2 = LAYERS * LAYER_SLABS
CMP0 = B2 + 5
RNN0 = CMP0 + 4
WO2 = RNN0 + 4
FF0 = WO2 + 4
SLABS = FF0 + 2 * NG2

PC_L, PC_LN = 0, 24
PC_CONV, PC_CONVN = 48, 16 * NG
PC_FINAL = PC_CONV + LAYERS * PC_CONVN
PC_C = PC_FINAL + 8
PC_ADAB = PC_C + 8
PC_PREMIX = PC_ADAB + 48
PC_POSTMIX = PC_PREMIX + 8
PC_PREMLP = PC_POSTMIX + 8
PC_POSTMLP = PC_PREMLP + 8
PC_RCONV = PC_POSTMLP + 8
PC_BA = PC_RCONV + 20
PC_BX = PC_BA + 4
PC_LAM = PC_BX + 4
PC_NRNN = PC_LAM + 4
PC_NATT = PC_NRNN + 4
PC_POS = PC_NATT + 4
PC_N = PC_POS + 32

N_CMP = 31
CMPC = 34
KKW = 16 * CMPC + 16
BANDW = 144
POOL_WINDOWS = (2, 4, 8, 16)
POS_COL = 32

C1 = {}
_at = 0
for _name, _w in (("ident", P), ("ones", P), ("head_mean", P), ("rot", P), ("cos", S), ("sin", S),
                  ("decay", RET_HEADS * S), ("band", 2 * 4 * BANDW)):
    C1[_name] = (_at, _w)
    _at += _w
C1_KEEP = 2 * P
C1_N = _at
C2 = {}
_at = 0
for _name, _w in (("dup", 2 * P), ("alibi", S), ("alibi_c", NT * 32), ("slopes", 8), ("seen", 1)):
    C2[_name] = (_at, _w)
    _at += _w
C2_N = _at


def constants():
    p = np.arange(P)
    t = np.arange(S)
    c1 = np.zeros((P, C1_N), np.float32)

    def put(table, where, name, value):
        a, w = where[name]
        table[:, a:a + w] = np.asarray(value, np.float32).reshape(P, w)

    put(c1, C1, "ident", np.eye(P))
    put(c1, C1, "ones", np.ones((P, P)))
    put(c1, C1, "head_mean", (p[:, None] // HD == p[None, :] // HD) / HD)
    rot = np.zeros((P, P))
    for m in range(P):
        if m % HD < HD // 2:
            rot[m + HD // 2, m] = -1.0
        else:
            rot[m - HD // 2, m] = 1.0
    put(c1, C1, "rot", rot)
    half = HD // 2
    inv = np.float32(10000.0) ** (-np.arange(half, dtype=np.float32) / np.float32(half))
    ang = (t.astype(np.float32)[None, :] * inv[p % half][:, None]).astype(np.float64)
    put(c1, C1, "cos", np.cos(ang))
    put(c1, C1, "sin", np.sin(ang))
    lg = np.log1p(-np.exp2(-5.0 - np.arange(RET_HEADS)))
    dist = np.abs(t[None, :] - p[:, None])
    ok = t[None, :] // CHUNK >= p[:, None] // CHUNK
    put(c1, C1, "decay", np.stack([np.where(ok, np.exp(g * dist), 0.0) * HD ** -0.5 for g in lg], 1))
    tb = np.arange(BANDW)
    band = np.zeros((P, 2, 4, BANDW))
    for first in range(2):
        for g, w in enumerate(POOL_WINDOWS):
            lag = tb[None, :] - p[:, None]
            cnt = np.minimum(tb + 1, w) if first == 0 else np.full(BANDW, w)
            band[:, first, g] = np.where((lag >= 0) & (lag < w), 1.0 / cnt[None, :], 0.0) - (lag == 0)
    put(c1, C1, "band", band)

    c2 = np.zeros((P, C2_N), np.float32)
    put(c2, C2, "dup", np.concatenate([(p[:, None] == g * HD + p[None, :] % HD) for g in range(2)], 1))
    d = p[:, None] + 384 - t[None, :]
    put(c2, C2, "alibi", np.where(d >= 0, d, 1e32))
    end = 16 * np.arange(32) + 31
    dc = (np.arange(NT) * P)[None, :, None] + p[:, None, None] - end[None, None, :]
    put(c2, C2, "alibi_c", np.where(dc >= 0, dc, 1e32))
    put(c2, C2, "slopes", np.broadcast_to(2.0 ** -(np.arange(8) + 1.0), (P, 8)))
    put(c2, C2, "seen", (p >= 31))
    return c1, c2


def build(nc, weights, ada, params, xin, wsT, bsb_in, bw_in, cst1, cst2, gatew, w2k, w2v_in, lruw, yout):
    ctx = ExitStack()
    with ctx:
        top = [16512]

        def at(name, shape, dt, offset):
            return nc.alloc_sbuf_tensor_at(name, shape, dt, offset=offset)

        def size(shape):
            return 4 * int(np.prod(shape[1:]))

        def keep(name, shape, dt=F32):
            t = at(name, shape, dt, top[0])
            top[0] += -(-size(shape) // 32) * 32
            return t

        def sem(name):
            return ctx.enter_context(nc.semaphore(name))

        x = keep("x", [P, KT, S])
        xh = keep("xh", [P, KT, S], F32R)
        xl = keep("xl", [P, KT, S], F32R)
        wh = keep("wh", [P, RING, SLABW], F32R)
        raw_at = top[0]
        raw = keep("raw", [P, RING, SLABW])
        wl = at("wl", [P, RING, SLABW], F32R, raw_at)
        prm = keep("prm", [P, PC_N])
        keep1 = keep("keep1", [P, C1_KEEP])
        mod = keep("mod", [P, 48])
        silu_c = keep("silu_c", [P, KT])
        eps = keep("eps", [P, 1])
        std = keep("std", [P, S])
        rstd = keep("rstd", [P, S])
        gains = keep("gains", [P, 4, KT])
        lru_c = keep("lru_c", [P, 6, 4])
        ada_acc = keep("ada_acc", [P, GRP])
        arena = top[0]
        ident = keep1[:, 0:P]
        ones = keep1[:, P:2 * P]

        t1 = keep("t1", [P, C1_N - C1_KEEP])

        def c1(name):
            a, w = C1[name]
            return t1[:, a - C1_KEEP:a - C1_KEEP + w]

        head_mean, rot, cos, sin = c1("head_mean"), c1("rot"), c1("cos"), c1("sin")
        decay = c1("decay")
        band = c1("band").rearrange("p (f g t) -> p f g t", f=2, g=4)
        ws = keep("ws", [P, LAYERS * 4, P])
        bsb = keep("bsb", [P, LAYERS * 2, P])
        bw = keep("bw", [P, LAYERS * 2, P])
        bw_cur = keep("bw_cur", [P, 2, P])
        kpad = keep("kpad", [P, 2, 2, S])
        va_at = top[0]
        u = keep("u", [P, 2, S])
        va = keep("va", [P, NT, GRP])
        sqb = at("sqb", [P, 2, S], F32, va_at)
        nt = at("nt", [P, 2, S], F32, va_at + 4096)
        y = at("y", [P, 4, S], F32, va_at)
        st_at = top[0]
        xb = keep("xb", [P, NT, GRP])
        pooled = keep("pooled", [P, 2, S])
        rtmp = keep("rtmp", [P, 2, S])
        sT = at("sT", [P, 2, 1280], F32, st_at)
        gsq = at("gsq", [P, 2, S], F32, st_at)
        q_at = top[0]
        q = keep("q", [P, 4, S])
        k = keep("k", [P, 4, S])
        vr = keep("vr", [P, NT, S])
        sg = keep("sg", [P, 4, S])
        ya = keep("ya", [P, 2, S])
        vcur = keep("vcur", [P, 2, NT, P])
        vss = keep("vss", [P, 3, NT])
        mix_end = top[0]
        ah = at("ah", [P, 2, 2, S], F32R, q_at)
        al = at("al", [P, 2, 2, S], F32R, q_at + 8192)
        cv = at("cv", [P, 4, S], F32, q_at + 16384)
        ab = at("ab", [P, 2, S], F32, q_at + 24576)
        adab = at("adab", [P, 8, GRP], F32, va_at + 8192)
        assert mix_end <= 229368, mix_end

        top[0] = arena
        t2 = keep("t2", [P, C2_N])

        def c2(name):
            a, w = C2[name]
            return t2[:, a:a + w]

        dup, alibi, slopes, seen = c2("dup"), c2("alibi"), c2("slopes"), c2("seen")
        alibi_c = c2("alibi_c").rearrange("p (i c) -> p i c", c=32)
        gw = keep("gw", [P, KT, 24])
        gwh = keep("gwh", [P, KT, 24], F32R)
        gwl = keep("gwl", [P, KT, 24], F32R)
        w2kp = keep("w2kp", [P, 2, 2, P])
        w2v = keep("w2v", [P, 2, HD])
        lru = keep("lru", [P, 2, 4, P])
        hid = keep("hid", [P, 2, 2, 2, 32])
        hbias = keep("hbias", [P, 4])
        kcT = keep("kcT", [P, 32])
        vcs = keep("vcs", [32, P])
        ptc = keep("ptc", [32, S])
        gates = keep("gates", [P, NT, 24])
        soft = keep("soft", [P, 4, 18])
        cst = keep("cst", [P, 4, NT])
        kcv_at = top[0]
        kcv = keep("kcv", [P, 2, S])
        vv = keep("vv", [P, NT, GRP])
        sqb2 = at("sqb2", [P, 2, S], F32, kcv_at)
        nt2 = at("nt2", [P, 2, S], F32, kcv_at + 4096)
        ksw = keep("ksw", [P, 2, S])
        q2 = keep("q2", [P, 4, S])
        qc = keep("qc", [P, 2, S])
        gg = keep("gg", [P, 4, S])
        cx = keep("cx", [P, 4, S])
        big = top[0]
        kkh = at("kkh", [P, 2, 2, KKW], F32R, big)
        kkl = at("kkl", [P, 2, 2, KKW], F32R, big + size([P, 2, 2, KKW]))
        rr = at("rr", [P, 4, S], F32, big)
        ii = at("ii", [P, 4, S], F32, big + 8192)
        mm = at("mm", [P, 4, S], F32, big + 16384)
        dd = at("dd", [P, 4, S], F32, big + 24576)
        att = at("att", [P, 4, S], F32, big)
        pb = at("pb", [P, 3, S], F32, big + 8192)
        tsl = at("tsl", [P, 2, S], F32, big + 14336)
        pt = at("pt", [P, 2, NT, S], F32, big + 18432)
        adab_tail = at("adab_tail", [P, ADA_SLABS - LAYERS * NG, KT, GRP], F32, big + 18432)
        assert big + 18432 + 16384 <= 229368, big
        ymix = at("ymix", [P, KT, S], F32, big)
        ff_at = kcv_at + 8192
        ah2 = at("ah2", [P, 3, 2, S], F32R, ff_at)
        al2 = at("al2", [P, 3, 2, S], F32R, ff_at + 12288)
        rl = at("rl", [P, 2, S], F32, ff_at + 24576)
        ab2 = at("ab2", [P, 2, S], F32, ff_at + 28672)
        assert ff_at + 32768 <= big

        ps = ctx.enter_context(nc.psum_tensor("ps", [P, 8, S], F32))

        def bank(b):
            return ps[:, b, :]

        raw_loaded = [sem(f"raw_loaded{s}") for s in range(RING)]
        hi_made = sem("hi_made")
        slab_split = sem("slab_split")
        slab_used = sem("slab_used")
        x_loaded = [sem(f"x_loaded{i}") for i in range(2)]
        params_loaded = sem("params_loaded")
        tables_loaded = sem("tables_loaded")
        eps_set = sem("eps_set")
        silu_c_ready = sem("silu_c_ready")
        lru_exp = sem("lru_exp")
        lru_step = sem("lru_step")
        sq_ready, sq_used = sem("sq_ready"), sem("sq_used")
        sq_added, sum_done = sem("sq_added"), sem("sum_done")
        std_ready, rstd_ready = sem("std_ready"), sem("rstd_ready")
        nt_ready, nh_ready, nl_ready = sem("nt_ready"), sem("nh_ready"), sem("nl_ready")
        bw_ready = sem("bw_ready")
        kpad_zero = sem("kpad_zero")
        ws_masked = sem("ws_masked")
        proj_evac = sem("proj_evac")
        vss_ready, vstd_ready, vr_ready, va_ready = sem("vss_ready"), sem("vstd_ready"), sem("vrstd_ready"), sem("va_ready")
        rot_ready, rope_part, rope_done = sem("rot_ready"), sem("rope_part"), sem("rope_done")
        sv_ready, ya_part, ya_ready = sem("sv_ready"), sem("ya_part"), sem("ya_ready")
        pool_ready, pooled_ready, yb_ready = sem("pool_ready"), sem("pooled_ready"), sem("yb_ready")
        mix_hi, mix_split = sem("mix_hi"), sem("mix_split")
        staged, s_done, sT_ready = sem("staged"), sem("s_done"), sem("sT_ready")
        pv_done, y_evac = sem("pv_done"), sem("y_evac")
        mean_ready, yc_ready, gsq_ready = sem("mean_ready"), sem("yc_ready"), sem("gsq_ready")
        var_ready, gsd_ready, gr_ready = sem("var_ready"), sem("gsd_ready"), sem("gr_ready")
        yn_ready, gm_ready = sem("yn_ready"), sem("gm_ready")
        half_done, mix_added = sem("half_done"), sem("mix_added")
        cv_init, conv_mid, conv_done = sem("cv_init"), sem("conv_mid"), sem("conv_done")
        sil_ready, a_ready, ah_ready, act_split = sem("sil_ready"), sem("a_ready"), sem("ah_ready"), sem("act_split")
        down_done, ffn_added = sem("down_done"), sem("ffn_added")
        ada_loaded, ada_done, ada_evac = sem("ada_loaded"), sem("ada_done"), sem("ada_evac")
        ada_term, ada_summed = sem("ada_term"), sem("ada_summed")
        xf_ready = sem("xf_ready")
        tables2_loaded = sem("tables2_loaded")
        gains_ready = sem("gains_ready")
        zeroed = sem("zeroed")
        gwh_ready, gw_split = sem("gwh_ready"), sem("gw_split")
        proj2_evac = sem("proj2_evac")
        dup_ready, kkh_ready, kk_split = sem("dup_ready"), sem("kkh_ready"), sem("kk_split")
        gate_ready, gates_sig, gates_ready = sem("gate_ready"), sem("gates_sig"), sem("gates_ready")
        hbias_ready, hid_ready = sem("hbias_ready"), sem("hid_ready")
        kcv_ready, kcv_evac = sem("kcv_ready"), sem("kcv_evac")
        cx_init, cx_mid, cx_done = sem("cx_init"), sem("cx_mid"), sem("cx_done")
        lru_ready, sig_ready, th_ready, sqrt_ready = sem("lru_ready"), sem("sig_ready"), sem("th_ready"), sem("sqrt_ready")
        dd_ready, aa_ready, uu_ready, scan_ready, rnn_ready = (sem("dd_ready"), sem("aa_ready"), sem("uu_ready"),
                                                              sem("scan_ready"), sem("rnn_ready"))
        staged2, s2_done, sc_done, exp_done, rs_ready, p_ready = (sem("staged2"), sem("s2_done"), sem("sc_done"),
                                                                 sem("exp_done"), sem("rs_ready"), sem("p_ready"))
        cmp_step = sem("cmp_step")
        t_done, pt_evac, pv2_done, att_evac = sem("t_done"), sem("pt_evac"), sem("pv2_done"), sem("att_evac")
        sq4_ready, sq4_used, std4_ready, rstd4_ready = sem("sq4_ready"), sem("sq4_used"), sem("std4_ready"), sem("rstd4_ready")
        nt4_ready, nh4_ready, nl4_ready = sem("nt4_ready"), sem("nh4_ready"), sem("nl4_ready")
        y_ready = sem("y_ready")
        pn_ready, x2_ready = sem("pn_ready"), sem("x2_ready")
        y_zero = sem("y_zero")
        rl_ready, ab_ready, ah2_ready, act2_split = sem("rl_ready"), sem("ab_ready"), sem("ah2_ready"), sem("act2_split")
        down2_done, y2_added = sem("down2_done"), sem("y2_added")
        stored = sem("stored")

        block = ctx.enter_context(nc.Block())

        tensor_counts = (ada_done, pv_done, pv_done, pv_done, t_done, s2_done, pv2_done)
        scalar_counts = (y_evac, y_evac, pt_evac, att_evac, rl_ready, ah2_ready)
        vector_counts = (ada_evac, ada_summed, conv_done, ffn_added, sc_done, a_ready, act_split, y2_added, act2_split, ab_ready)

        def past(eng, s, n):
            eng.wait_ge(s, n + 1)

        def col(i, n=1):
            return prm[:, i:i + n] if isinstance(i, int) else prm[:, bass.ds(i, n)]

        def cols(t, i, n):
            return t[:, i:i + n] if isinstance(i, int) else t[:, bass.ds(i, n)]

        q_f, D_f = q[:, :, :].rearrange("p a b -> p (a b)"), decay
        k_f, y_f = k[:, :, :].rearrange("p a b -> p (a b)"), y[:, :, :].rearrange("p a b -> p (a b)")
        q2_f, att_f = q2[:, :, :].rearrange("p a b -> p (a b)"), att[:, :, :].rearrange("p a b -> p (a b)")
        ya_f = ya[:, :, :].rearrange("p a b -> p (a b)")
        bsb_f = bsb[:, :, :].rearrange("p a b -> p (a b)")
        ws_f = ws[:, :, :].rearrange("p a b -> p (a b)")
        bw_f = bw[:, :, :].rearrange("p a b -> p (a b)")
        turn_order = (0, 2, 1, 3)
        soffs = [0, 512, 896, 1152]
        sbank = [(0, 0), (1, 0), (2, 0), (1, 384)]

        @block.sync
        def _(sp):
            for i in range(2):
                f = slice(i * KT // 2, (i + 1) * KT // 2)
                sp.dma_start(x[:, f, :], xin[:, f, :]).then_inc(x_loaded[i], 16)

            def load(n, s):
                sp.wait_ge(slab_used, n + 1)
                sp.dma_start(raw[:, s, :], cols_dram(n)).then_inc(raw_loaded[s], 16)

            def cols_dram(n):
                return weights[n, :, :] if isinstance(n, int) else weights[bass.ds(n, 1), :, :].rearrange("a p c -> p (a c)")

            with sp.Fori(0, SLABS // RING) as i:
                for s in range(RING):
                    load(i * RING + s, s)
            for n in range(SLABS // RING * RING, SLABS):
                load(n, n % RING)
            for i in range(KT):
                sp.wait_ge(x2_ready, KT + i + 1)
                sp.dma_start(yout[:, i, :], x[:, i, :]).then_inc(stored, 16)
            sp.wait_ge(stored, 16 * KT)

        @block.gpsimd
        def _(pool):
            pool.memset(kpad[:, :, :, :], 0.0).then_inc(kpad_zero, 1)

            def low(n, s):
                pool.wait_ge(hi_made, n + 1)
                pool.tensor_tensor(wl[:, s, :], raw[:, s, :], wh[:, s, :].bitcast(F32), ALU.subtract).then_inc(slab_split, 1)

            with pool.Fori(0, SLABS // RING) as i:
                for s in range(RING):
                    low(i * RING + s, s)
            for n in range(SLABS // RING * RING, SLABS):
                low(n, n % RING)

        @block.tensor
        def _(pe):
            pe.sem_inc(slab_used, RING)
            for s in tensor_counts:
                pe.sem_inc(s, 1)

            def product(out, w_hi, w_lo, m_hi, m_lo, start, stop):
                pe.matmul(out, w_hi, m_hi, start=start, stop=False)
                pe.matmul(out, w_hi, m_lo, start=False, stop=False)
                return pe.matmul(out, w_lo, m_hi, start=False, stop=stop)

            def slab_fm(n, s, b0, fresh=None, half=None, kts=tuple(range(KT)), start=True, stop=True):
                pe.wait_ge(slab_split, n + 1)
                order = [(m, i) for m in range(2) for i in range(len(kts))]
                if fresh is not None:
                    order.sort(key=lambda o: o[1])
                for m, i in order:
                    if fresh is not None and m == 0:
                        pe.wait_ge(fresh[0], fresh[1] + i + 1)
                    kt = kts[i]
                    w = slice(kt * GRP + m * P, kt * GRP + m * P + P)
                    last = product(bank(b0 + m), wh[:, s, w], wl[:, s, w], xh[:, kt, :], xl[:, kt, :],
                                   start and i == 0, stop and i == len(kts) - 1)
                    if half is not None and m == 0 and i == len(kts) - 1:
                        last.then_inc(half, 1)
                if stop:
                    last.then_inc(slab_used, 1)

            def slab_tm(n, s, b0):
                pe.wait_ge(slab_split, n + 1)
                for i in range(NT):
                    out = ps[:, b0 + i // 2, (i % 2) * GRP:(i % 2 + 1) * GRP]
                    tok = slice(i * P, (i + 1) * P)
                    for kt in range(KT):
                        w = slice(kt * GRP, (kt + 1) * GRP)
                        last = product(out, xh[:, kt, tok], xl[:, kt, tok], wh[:, s, w], wl[:, s, w], kt == 0, kt == KT - 1)
                last.then_inc(slab_used, 1)

            def sum_squares(nk, th, buf):
                for i in range(KT):
                    pe.wait_ge(sq_ready, nk * KT + i + 1)
                    pe.matmul(bank(7), ones, buf[:, i % 2, :], start=(i == 0), stop=(i == KT - 1)).then_inc(sq_used, 1)

            def sum_added(nk, th, buf):
                pe.wait_ge(sq_added, th * (KT - 2) + (KT - 2))
                pe.matmul(bank(7), ones, std[:, :], start=True, stop=False)
                pe.wait_ge(sq_ready, nk * KT + KT)
                pe.matmul(bank(7), ones, buf[:, 1, :], start=False, stop=True).then_inc(sum_done, 1)

            def ada_part(a):
                past(pe, ada_summed, a + 1)
                past(pe, ada_evac, a)
                for m in range(2):
                    last = pe.matmul(ps[:, 7, m:m + 1], ada_acc[:, m * P:(m + 1) * P], ones[:, 0:1], start=True, stop=True)
                last.then_inc(ada_done, 1)

            pe.wait_ge(params_loaded, 16 * 3)
            pe.wait_ge(kpad_zero, 1)
            sum_squares(0, 0, sqb)
            with pe.Fori(0, LAYERS) as l:
                n0 = l * LAYER_SLABS
                kinds = ["fm", "tm", "tm", "fm", "fm", "fm", "fm", "tm", "tm", "fm", "fm"]
                for c in range(W_IN):
                    if c >= 2:
                        pe.wait_ge(proj_evac, l * W_IN + c - 1)
                    if kinds[c] == "fm":
                        slab_fm(n0 + c, c % RING, 2 * (c % 2), fresh=(nl_ready, l * 2 * KT) if c == 0 else None)
                    else:
                        slab_tm(n0 + c, c % RING, 2 * (c % 2))
                    if c in (5, 7):
                        src, o = (q, 0) if c == 5 else (k, 4)
                        pe.wait_ge(tables_loaded, 16 * 3)
                        pe.wait_ge(proj_evac, l * W_IN + (5 if c == 5 else 7))
                        for i in range(4):
                            if o:
                                pe.wait_ge(rope_part, l * 8 + i + 1)
                            pe.matmul(bank(4 + i), rot, src[:, i, :], start=True, stop=True).then_inc(rot_ready, 1)
                pe.wait_ge(va_ready, l + 1)
                pe.wait_ge(rope_part, l * 8 + 8)
                for i in range(NT):
                    for j in range(2):
                        last = pe.matmul(ps[:, 4 + i, j * 256:(j + 1) * 256], va[:, i, j * P:(j + 1) * P],
                                         cols(ws_f, l * 512 + j * 256, 256), start=True, stop=True)
                last.then_inc(sv_ready, 1)
                pe.wait_ge(proj_evac, l * W_IN + W_IN)
                for g in range(4):
                    pair = slice((g // 2) * P, (g // 2 + 1) * P)
                    for j in range(NT):
                        pe.matmul(ps[:, g, j * P:(j + 1) * P], xb[:, j, pair], band[:, min(j, 1), g, 0:P], start=(j == 0), stop=False)
                    for j in range(NT - 1):
                        last = pe.matmul(ps[:, g, (j + 1) * P:(j + 1) * P + BANDW - P], xb[:, j, pair], band[:, 1, g, P:BANDW],
                                         start=False, stop=(j == NT - 2))
                    last.then_inc(pool_ready, 1)
                pe.wait_ge(bw_ready, l + 1)
                pe.wait_ge(ya_ready, l * 2 + 2)
                pe.wait_ge(pooled_ready, l * 4 + 4)
                for j in range(2):
                    pe.matmul(bank(4 + j), bw_cur[:, j, :], pooled[:, j, :], start=True, stop=True).then_inc(yb_ready, 1)
                with pe.Fori(0, 2) as it:
                    def ret_scores(p, hh):
                        if hh == 0:
                            pe.wait_ge(staged, l * 4 + it * 2 + p + 1)
                        for j in range(NT):
                            b, o = sbank[j]
                            w = S - j * P
                            last = pe.matmul(ps[:, 3 * hh + b, o:o + w], kpad[:, p, hh, j * P:(j + 1) * P],
                                             cols(q_f, it * (2 * S) + (p * S + j * P), w), start=True, stop=True)
                        last.then_inc(s_done, 1)

                    def ret_values(p, hh):
                        head = l * 8 + it * 4 + (2 * p + hh)
                        pe.wait_ge(sT_ready, head + 1)
                        pe.wait_ge(y_evac, head + 1)
                        for j in range(NT):
                            w = S - j * P
                            last = pe.matmul(ps[:, 6 + hh, j * P:S], vcur[:, p, j, :], sT[:, hh, soffs[j]:soffs[j] + w],
                                             start=(j == 0), stop=(j == NT - 1))
                        last.then_inc(pv_done, 1)

                    pe.wait_ge(mix_split, l * 8 + 4)
                    ret_scores(0, 0)
                    ret_scores(0, 1)
                    ret_values(0, 0)
                    ret_scores(1, 0)
                    ret_values(0, 1)
                    ret_scores(1, 1)
                    ret_values(1, 0)
                    pe.wait_ge(y_evac, l * 8 + it * 4 + 4)
                    pe.matmul(bank(2), head_mean, y_f[:, bass.ds(it * (2 * S), S)], start=True, stop=True).then_inc(mean_ready, 1)
                    ret_values(1, 1)
                    pe.wait_ge(gsq_ready, l * 4 + it + 1)
                    pe.matmul(bank(5), head_mean, ya_f[:, bass.ds(it * S, S)], start=True, stop=True).then_inc(var_ready, 1)
                pe.wait_ge(gsd_ready, l * 4 + 2)
                for t in range(2):
                    pe.wait_ge(y_evac, l * 8 + 4 * t + 6)
                    pe.matmul(bank(4 + t), head_mean, y[:, 2 * t + 1, :], start=True, stop=True).then_inc(mean_ready, 1)
                others, turned = (0, 1, 2, 3), tuple(4 + i for i in turn_order)
                bank0 = [2 * ((W_IN + w) % 2) for w in range(W_OUT)]
                pe.wait_ge(mix_split, l * 8 + 4)
                slab_fm(n0 + W_IN, W_IN % RING, bank0[0], kts=others, stop=False)
                for t in range(2):
                    pe.wait_ge(gsq_ready, l * 4 + t + 3)
                    pe.matmul(bank(6 + t), head_mean, gsq[:, t, :], start=True, stop=True).then_inc(var_ready, 1)
                slab_fm(n0 + W_IN + 1, (W_IN + 1) % RING, bank0[1], kts=others, stop=False)
                for w in range(2):
                    slab_fm(n0 + W_IN + w, (W_IN + w) % RING, bank0[w], fresh=(mix_split, l * 8 + 4), half=half_done, kts=turned,
                            start=False)
                for w in range(2, W_OUT):
                    pe.wait_ge(mix_added, l * KT + 2 * (w - 1))
                    slab_fm(n0 + W_IN + w, (W_IN + w) % RING, bank0[w], half=half_done)
                sum_added(l * 2 + 1, l * 2, sqb)

                def up(j, n, s, fresh=None):
                    past(pe, conv_done, l * 4 * NG + j * 4)
                    slab_fm(n, s, 0, fresh)
                    slab_fm(n + 1, (s + 1) % RING, 2)

                def down(j, par, n, s):
                    past(pe, act_split, l * 2 * NG + j * 2 + 2)
                    pe.wait_ge(slab_split, n + 1)
                    past(pe, ffn_added, l * 8 * NG + j * 8)
                    for o in range(KT):
                        if o >= 3:
                            past(pe, ffn_added, l * 8 * NG + j * 8 + o - 2)
                        for kt in range(2):
                            w = slice(kt * D + o * P, kt * D + o * P + P)
                            last = product(bank(4 + o % 3), wh[:, s, w], wl[:, s, w], ah[:, par, kt, :], al[:, par, kt, :],
                                           kt == 0, kt == 1)
                        last.then_inc(down_done if o < KT - 1 else slab_used, 1)

                up(0, n0 + MLP0, MLP0 % RING, fresh=(nl_ready, l * 2 * KT + KT))
                ada_part(l * NG)
                with pe.Fori(0, (NG - 1) // 2) as it:
                    for v in range(2):
                        j = it * 2 + (1 + v)
                        n = n0 + it * 6 + (MLP0 + 2 + 3 * v)
                        up(j, n, (MLP0 + 2) % RING)
                        down(it * 2 + v, v, n + 2, (MLP0 + 4) % RING)
                        ada_part(l * NG + j)
                down(NG - 1, 0, n0 + (LAYER_SLABS - 1), (LAYER_SLABS - 1) % RING)
                past(pe, ada_evac, l * NG + NG)
                sum_added(l * 2 + 2, l * 2 + 1, sqb)

            sum_squares(5, 1, sqb2)
            pe.wait_ge(tables2_loaded, 16 * 5)
            pe.wait_ge(gw_split, 1)
            for c, kind in enumerate(("fm", "fm", "tm", "fm", "fm")):
                n = B2 + c
                if c >= 2:
                    pe.wait_ge(proj2_evac, c - 1)
                if kind == "fm":
                    slab_fm(n, n % RING, 2 * (c % 2), fresh=(nl_ready, 4 * KT) if c == 0 else None)
                else:
                    slab_tm(n, n % RING, 2 * (c % 2))
                if c < 2:
                    ada_part(LAYERS * NG + c)
                if c == 2:
                    past(pe, ada_evac, ADA_SLABS)
                    pe.wait_ge(proj2_evac, 1)
                    for kv in range(2):
                        for g in range(2):
                            pe.matmul(bank(4 + 2 * kv + g), dup[:, g * P:(g + 1) * P], kcv[:, kv, :], start=True,
                                      stop=True).then_inc(dup_ready, 1)
            pe.wait_ge(kk_split, 4)
            for i in range(NT):
                tok = slice(i * P, (i + 1) * P)
                for kt in range(KT):
                    last = product(ps[:, 4, i * 24:(i + 1) * 24], xh[:, kt, tok], xl[:, kt, tok], gwh[:, kt, :], gwl[:, kt, :],
                                   kt == 0, kt == KT - 1)
            last.then_inc(gate_ready, 1)
            pe.wait_ge(proj2_evac, 4)
            for kv in range(2):
                for part in range(2):
                    n = CMP0 + 2 * kv + part
                    s = n % RING
                    pe.wait_ge(slab_split, n + 1)
                    for a8 in range(8):
                        a = part * 8 + a8
                        mh = kkh[:, kv, :, 2 * a:2 * a + 16 * (CMPC - 1) + 1:16]
                        ml = kkl[:, kv, :, 2 * a:2 * a + 16 * (CMPC - 1) + 1:16]
                        for m in range(2):
                            w = slice(a8 * GRP + m * P, a8 * GRP + m * P + P)
                            out = ps[:, 2 + 4 * kv + m, 0:2 * CMPC].rearrange("p (g c) -> p g c", g=2)
                            last = product(out, wh[:, s, w], wl[:, s, w], mh, ml, a == 0, a == 15)
                    last.then_inc(slab_used, 1)
            for c in range(4):
                n = RNN0 + c
                if c == 0:
                    pe.wait_ge(proj2_evac, 5)
                if c == 1:
                    pe.wait_ge(hid_ready, 4)
                if c >= 2:
                    pe.wait_ge(cx_done, 2 * (c - 1))
                slab_fm(n, n % RING, 2 * (c % 2))
                if c == 1:
                    pe.wait_ge(hid_ready, 8)
                    pe.wait_ge(gates_sig, 1)
                    for m in range(2):
                        for g in range(2):
                            last = pe.matmul(ps[:, 4, 0:N_CMP], w2kp[:, m, g, :], hid[:, 0, m, g, 0:N_CMP],
                                             start=(m == 0 and g == 0), stop=(m == 1 and g == 1))
                    for g in range(2):
                        for m in range(2):
                            last = pe.matmul(ps[0:N_CMP, 5, g * HD:(g + 1) * HD], hid[:, 1, m, g, 0:N_CMP], w2v[:, m, :],
                                             start=(m == 0), stop=(m == 1))
                    last.then_inc(kcv_ready, 1)
            pe.wait_ge(kcv_evac, 2)
            pe.wait_ge(cx_done, 4)
            pe.wait_ge(proj2_evac, 7)
            for i in range(4):
                pe.matmul(bank(4 + i), lru[:, 0, i, :], cx[:, i, :], start=True, stop=True).then_inc(lru_ready, 1)
            for i in range(4):
                pe.matmul(bank(i), lru[:, 1, i, :], cx[:, i, :], start=True, stop=True).then_inc(lru_ready, 1)
            pe.wait_ge(sig_ready, 8)
            pe.wait_ge(gates_ready, 1)

            with pe.Fori(0, 4) as r:
                def scores(U):
                    g, v = U // 9, U % 9
                    past(pe, sc_done, r * 18 + (U - 2 if U >= 3 else 0))
                    if v < 8:
                        i = v % 4
                        w = (i + 1) * P
                        pe.matmul(ps[:, U % 3, 0:w], qc[:, g, i * P:(i + 1) * P], ksw[:, v // 4, 0:w], start=True,
                                  stop=True).then_inc(s2_done, 1)
                    else:
                        for i in range(NT):
                            last = pe.matmul(ps[:, U % 3, i * 32:i * 32 + N_CMP], qc[:, g, i * P:(i + 1) * P], kcT[:, 0:N_CMP],
                                             start=True, stop=True)
                        last.then_inc(s2_done, 1)

                def turn(U):
                    v = U % 9
                    pe.wait_ge(p_ready, r * 18 + U + 1)
                    past(pe, pt_evac, r * 18 + (U - 2 if U >= 3 else 0))
                    if v < 8:
                        for j in range(v % 4 + 1):
                            last = pe.transpose(ps[:, 3 + U % 3, j * P:(j + 1) * P], pb[:, U % 3, j * P:(j + 1) * P], ident)
                    else:
                        for i in range(NT):
                            last = pe.transpose(ps[0:N_CMP, 3 + U % 3, i * P:(i + 1) * P], pb[:, U % 3, i * 32:i * 32 + N_CMP],
                                                ident)
                    last.then_inc(t_done, 1)

                def values(g):
                    past(pe, pt_evac, r * 18 + 9 * g + 9)
                    past(pe, att_evac, r * 2)
                    for b in range(2):
                        for j in range(NT):
                            pe.matmul(ps[:, 6 + g, j * P:S], vv[:, j, b * P:(b + 1) * P], pt[:, b, j, j * P:S],
                                      start=(b == 0 and j == 0), stop=False)
                    pe.matmul(bank(6 + g), vcs[0:N_CMP, :], ptc[0:N_CMP, :], start=False, stop=True).then_inc(pv2_done, 1)

                pe.wait_ge(staged2, r + 1)
                scores(0)
                scores(1)
                for U in range(18):
                    if U + 2 < 18:
                        scores(U + 2)
                    turn(U)
                    if U % 9 == 8:
                        values(U // 9)

            for b in range(2):
                for i in range(4):
                    pe.wait_ge(sq4_ready, 4 * b + i + 1)
                    pe.matmul(bank(7), ones, sqb2[:, i % 2, :], start=(i == 0), stop=(i == 3)).then_inc(sq4_used, 1)
            pe.wait_ge(nl4_ready, 8)
            for w in range(4):
                n = WO2 + w
                if w >= 2:
                    pe.wait_ge(y_ready, 2 * (w - 1))
                slab_fm(n, n % RING, 2 * (w % 2))
            sum_added(6, 4, sqb2)
            sum_squares(7, 2, sqb2)

            def up2(g, n, s, fresh=None):
                past(pe, rl_ready, g * 2)
                slab_fm(n, s, 0, fresh)

            def down2(g, par, n, s):
                past(pe, act2_split, g * 2 + 2)
                pe.wait_ge(slab_split, n + 1)
                past(pe, y2_added, g * 8)
                for o in range(KT):
                    if o >= 4:
                        past(pe, y2_added, g * 8 + o - 3)
                    for kt in range(2):
                        w = slice(kt * D + o * P, kt * D + o * P + P)
                        last = product(bank(2 + o % 4), wh[:, s, w], wl[:, s, w], ah2[:, par, kt, :], al2[:, par, kt, :],
                                       kt == 0, kt == 1)
                    last.then_inc(down2_done if o < KT - 1 else slab_used, 1)

            up2(0, FF0, FF0 % RING, fresh=(nl_ready, 5 * KT))
            with pe.Fori(0, (NG2 - 1) // 3) as it:
                for v in range(3):
                    n = it * 6 + (FF0 + 1 + 2 * v)
                    up2(it * 3 + (1 + v), n, (FF0 + 1 + 2 * v) % RING)
                    down2(it * 3 + v, v, n + 1, (FF0 + 2 + 2 * v) % RING)
            down2(NG2 - 1, (NG2 - 1) % 3, SLABS - 1, (SLABS - 1) % RING)
            sum_added(8, 5, sqb2)

        @block.scalar
        def _(act):
            for s in scalar_counts:
                act.sem_inc(s, 1)
            for dst, src in ((prm[:, :], params), (keep1[:, :], cst1[:, 0:C1_KEEP]), (ws[:, :, :], wsT)):
                act.dma_start(dst, src).then_inc(params_loaded, 16)

            def high(n, s, third):
                act.wait_ge(raw_loaded[s], third * 16 + 16)
                act.activation(wh[:, s, :], raw[:, s, :], ACT.Copy).then_inc(hi_made, 1)

            def used(n):
                act.wait_ge(slab_used, n + 1 + RING)

            def ahead(c, base, thirds):
                high(base + c + RING, (c + RING) % RING, thirds + (c + RING) // RING)

            def square(nk, i, buf, src, alone=None, th=None):
                if i >= 2 and alone is not None:
                    act.wait_ge(sq_used, alone * KT + i - 1)
                elif i >= 2:
                    act.wait_ge(sq_added, th * (KT - 2) + max(1, i - 2))
                act.activation(buf[:, i % 2, :], src[:, i, :], ACT.Square).then_inc(sq_ready, 1)

            def root(alone=None, th=None):
                if alone is not None:
                    act.wait_ge(sq_used, alone * KT + KT)
                else:
                    act.wait_ge(sum_done, th + 1)
                act.activation(std[:, :], bank(7), ACT.Sqrt, bias=eps[:, :], scale=1.0 / D).then_inc(std_ready, 1)

            def highs(sk, buf, shift=None):
                for i in range(KT):
                    act.wait_ge(nt_ready, sk * KT + i + 1)
                    if shift is None:
                        act.activation(xh[:, i, :], buf[:, i % 2, :], ACT.Copy).then_inc(nh_ready, 1)
                    else:
                        act.activation(xh[:, i, :], buf[:, i % 2, :], ACT.Identity, bias=mod[:, shift + i:shift + i + 1])\
                           .then_inc(nh_ready, 1)

            act.wait_ge(params_loaded, 16 * 3)
            act.activation(silu_c[:, :], col(PC_C, KT), ACT.Silu).then_inc(silu_c_ready, 1)
            act.wait_ge(lru_step, 1)
            act.activation(lru_c[:, 1, :], lru_c[:, 0, :], ACT.Exp, scale=-1.0).then_inc(lru_exp, 1)
            act.wait_ge(eps_set, 1)
            for i in range(KT):
                if i % (KT // 2) == 0:
                    act.wait_ge(x_loaded[i // (KT // 2)], 16)
                square(0, i, sqb, x, alone=0)
            for dst, src in ((t1[:, :], cst1[:, C1_KEEP:C1_N]), (bsb[:, :, :], bsb_in), (bw[:, :, :], bw_in)):
                act.dma_start(dst, src).then_inc(tables_loaded, 16)
            high(0, 0, 0)
            root(alone=0)
            high(1, 1, 0)

            with act.Fori(0, LAYERS) as l:
                n0 = l * LAYER_SLABS
                n3 = l * (LAYER_SLABS // RING)
                highs(l * 2, nt)
                high(n0 + 2, 2, n3)
                for c in range(W_IN):
                    used(n0 + c)
                    b0 = 2 * (c % 2)
                    for m in range(2):
                        tok2 = ps[:, b0 + m, :].rearrange("p (i d) -> p i d", i=2)
                        if c == 0:
                            last = act.activation(u[:, m, :], bank(b0 + m), ACT.Gelu_apprx_tanh)
                        elif c == 1:
                            last = act.activation(va[:, 2 * m:2 * m + 2, :], tok2, ACT.Gelu_apprx_tanh)
                        elif c == 2:
                            last = act.activation(xb[:, 2 * m:2 * m + 2, :], tok2, ACT.Copy)
                        elif c in (3, 4):
                            last = act.activation(q[:, 2 * (c - 3) + m, :], bank(b0 + m), ACT.Copy)
                        elif c in (5, 6):
                            last = act.activation(k[:, 2 * (c - 5) + m, :], bank(b0 + m), ACT.Copy)
                        elif c in (7, 8):
                            last = act.activation(vr[:, 2 * m:2 * m + 2, (c - 7) * 256:(c - 6) * 256], tok2, ACT.Copy)
                        else:
                            last = act.activation(sg[:, 2 * (c - 9) + m, :], bank(b0 + m), ACT.Silu)
                    last.then_inc(proj_evac, 1)
                    if c == 1:
                        act.wait_ge(proj_evac, l * W_IN + 2)
                        for i in range(NT):
                            last = act.activation(ya[:, i // 2, (i % 2) * GRP:(i % 2 + 1) * GRP], va[:, i, :], ACT.Square, accum_out=vss[:, 0, i:i + 1])
                        last.then_inc(vss_ready, 1)
                        act.wait_ge(vss_ready, l + 1)
                        act.activation(vss[:, 1, :], vss[:, 0, :], ACT.Sqrt, bias=eps[:, :], scale=1.0 / GRP).then_inc(vstd_ready, 1)
                    ahead(c, n0, n3)
                act.wait_ge(tables_loaded, 16 * 3)
                act.activation(bw_cur[:, :, :].rearrange("p a b -> p (a b)"), cols(bw_f, l * 256, 256), ACT.Copy).then_inc(bw_ready, 1)
                for g in range(4):
                    act.wait_ge(pool_ready, l * 4 + g + 1)
                    h = slice(HD * (g % 2), HD * (g % 2) + HD)
                    act.activation(pooled[h, g // 2, :], ps[h, g, :], ACT.Copy).then_inc(pooled_ready, 1)
                for j in range(2):
                    act.wait_ge(ya_ready, l * 2 + j + 1)
                    act.activation(xh[:, j, :], ya[:, j, :], ACT.Copy).then_inc(mix_hi, 1)
                for j in range(2):
                    act.wait_ge(yb_ready, l * 2 + j + 1)
                    act.activation(xh[:, 2 + j, :], bank(4 + j), ACT.Copy, scale=col(l * PC_LN + (PC_L + 10 + j))).then_inc(mix_hi, 1)
                act.wait_ge(kpad_zero, 1)
                with act.Fori(0, 2) as it:
                    act.wait_ge(rope_done, l * 8 + 8)
                    for p in range(2):
                        act.wait_ge(pv_done, l * 8 + it * 4 + (2 * p + 1))
                        for hh in range(2):
                            h = slice(HD * hh, HD * hh + HD)
                            act.activation(kpad[h, p, hh, :], k_f[h, bass.ds(it * (2 * S) + p * S, S)], ACT.Copy)
                        act.activation(vcur[:, p, :, :], vr[:, :, bass.ds(it * (2 * P) + p * P, P)], ACT.Copy).then_inc(staged, 1)
                    for p in range(2):
                        for hh in range(2):
                            h = slice(HD * hh, HD * hh + HD)
                            act.wait_ge(pv_done, l * 8 + it * 4 + (2 * p + hh + 4))
                            act.activation(y_f[h, bass.ds(it * (2 * S) + p * S, S)], ps[h, 6 + hh, :], ACT.Copy).then_inc(y_evac, 1)
                    act.wait_ge(var_ready, l * 4 + it + 1)
                    act.activation(ya_f[:, bass.ds(it * S, S)], bank(5), ACT.Sqrt, bias=eps[:, :]).then_inc(gsd_ready, 1)
                for t in range(2):
                    act.wait_ge(yc_ready, l * 4 + t + 3)
                    act.activation(gsq[:, t, :], y[:, 2 * t + 1, :], ACT.Square).then_inc(gsq_ready, 1)
                for turn, i in enumerate(turn_order):
                    if turn == 2:
                        for t in range(2):
                            act.wait_ge(var_ready, l * 4 + t + 3)
                            act.activation(gsq[:, t, :], bank(6 + t), ACT.Sqrt, bias=eps[:, :]).then_inc(gsd_ready, 1)
                    act.wait_ge(gm_ready, l * 4 + turn + 1)
                    act.activation(xh[:, 4 + i, :], y[:, i, :], ACT.Copy).then_inc(mix_hi, 1)

                def ada_load(a):
                    past(act, ada_summed, a)
                    act.dma_start(adab[:, :, :].rearrange("p k c -> p (k c)"),
                                  ada[bass.ds(a, 1), :, :].rearrange("a p c -> p (a c)")).then_inc(ada_loaded, 16)

                ada_load(l * NG)
                for w in range(W_OUT):
                    for i in (2 * w, 2 * w + 1):
                        act.wait_ge(mix_added, l * KT + i + 1)
                        square(l * 2 + 1, i, sqb, x, th=l * 2)
                    if w < W_OUT - 1:
                        used(n0 + W_IN + w)
                        ahead(W_IN + w, n0, n3)
                root(th=l * 2)
                highs(l * 2 + 1, nt)
                used(n0 + MLP0 - 1)
                ahead(MLP0 - 1, n0, n3)

                def conv_tap(r, j):
                    c = l * PC_CONVN + j * 16 + (PC_CONV + r * 4)
                    act.activation(cv[:, r, :], bank(r), ACT.Identity, bias=col(c + 3), scale=col(c + 2)).then_inc(cv_init, 1)

                def mlp_step(j, base, thirds, c, par):
                    used(base + c)
                    for r in range(2):
                        conv_tap(r, j)
                    ahead(c, base, thirds)
                    past(act, conv_done, l * 4 * NG + j * 4 + 2)
                    for r in range(2):
                        act.activation(cv[:, r, :], cv[:, r, :], ACT.Silu).then_inc(sil_ready, 1)
                    used(base + c + 1)
                    for r in range(2, 4):
                        conv_tap(r, j)
                    ahead(c + 1, base, thirds)
                    for r in range(2):
                        past(act, a_ready, l * 2 * NG + j * 2 + r + 1)
                        act.activation(ah[:, par, r, :], ab[:, r, :], ACT.Copy).then_inc(ah_ready, 1)

                mlp_step(0, n0, n3, MLP0, 0)
                with act.Fori(0, (NG - 1) // 2) as it:
                    for v in range(2):
                        j = it * 2 + (1 + v)
                        base, thirds, c = n0 + it * 6, n3 + it * 2, MLP0 + 2 + 3 * v
                        ada_load(l * NG + j)
                        mlp_step(j, base, thirds, c, (1 + v) % 2)
                        used(base + c + 2)
                        ahead(c + 2, base, thirds)
                for i in range(KT):
                    past(act, ffn_added, l * 8 * NG + (8 * NG - 8 + i + 1))
                    square(l * 2 + 2, i, sqb, x, th=l * 2 + 1)
                root(th=l * 2 + 1)

            for dst, src in ((t2[:, :], cst2), (gw[:, :, :], gatew), (w2kp[:, :, :, :], w2k), (w2v[:, :, :], w2v_in),
                             (lru[:, :, :, :], lruw)):
                act.dma_start(dst, src).then_inc(tables2_loaded, 16)
            for t in range(ADA_SLABS - LAYERS * NG):
                act.dma_start(adab_tail[:, t, :, :].rearrange("p k c -> p (k c)"), ada[LAYERS * NG + t, :, :]).then_inc(ada_loaded, 16)
            for i in range(KT):
                act.wait_ge(xf_ready, i + 1)
                square(5, i, sqb2, x, alone=1)
            root(alone=1)
            act.wait_ge(tables2_loaded, 16 * 5)
            act.activation(gwh[:, :, :], gw[:, :, :], ACT.Copy).then_inc(gwh_ready, 1)
            highs(4, nt2, shift=0)
            high(B2 + 2, (B2 + 2) % RING, (B2 + 2) // RING)

            def after(n):
                if n + RING < SLABS:
                    high(n + RING, n % RING, (n + RING) // RING)

            act.wait_ge(zeroed, 1)
            for c in range(5):
                n = B2 + c
                used(n)
                b0 = 2 * (c % 2)
                for m in range(2):
                    if c == 0:
                        last = act.activation(kcv[:, m, :], bank(b0 + m), ACT.Copy)
                    elif c == 1:
                        last = act.activation(ksw[:, m, :], bank(b0 + m), ACT.Copy)
                    elif c == 2:
                        last = act.activation(vv[:, 2 * m:2 * m + 2, :], ps[:, b0 + m, :].rearrange("p (i d) -> p i d", i=2), ACT.Copy)
                    else:
                        last = act.activation(q2[:, 2 * (c - 3) + m, :], bank(b0 + m), ACT.Copy, scale=-HD ** -0.5)
                last.then_inc(proj2_evac, 1)
                after(n)
                if c == 2:
                    for kv in range(2):
                        for g in range(2):
                            act.wait_ge(dup_ready, 2 * kv + g + 1)
                            act.activation(kkh[0:HD, kv, g, 0:S], ps[0:HD, 4 + 2 * kv + g, :], ACT.Copy)
                            act.activation(kkh[HD:P, kv, g, 0:S - 1], ps[HD:P, 4 + 2 * kv + g, 1:S], ACT.Copy)
                            act.activation(kkh[:, kv, g, S:S + 31:2], col(PC_POS + 16 * kv, 16), ACT.Copy).then_inc(kkh_ready, 1)
            act.wait_ge(gate_ready, 1)
            act.activation(gates[:, :, :].rearrange("p i c -> p (i c)"), ps[:, 4, 0:NT * 24], ACT.Sigmoid).then_inc(gates_sig, 1)
            for kv in range(2):
                for part in range(2):
                    used(CMP0 + 2 * kv + part)
                    after(CMP0 + 2 * kv + part)
                for m in range(2):
                    act.activation(hbias[:, 2 * kv + m:2 * kv + m + 1], ps[:, 2 + 4 * kv + m, POS_COL:POS_COL + 1], ACT.Copy)\
                       .then_inc(hbias_ready, 1)
                act.wait_ge(hbias_ready, 2 * kv + 2)
                for m in range(2):
                    for g in range(2):
                        act.activation(hid[:, kv, m, g, 0:N_CMP], ps[:, 2 + 4 * kv + m, g * CMPC:g * CMPC + N_CMP],
                                       ACT.Gelu_apprx_tanh, bias=hbias[:, 2 * kv + m:2 * kv + m + 1]).then_inc(hid_ready, 1)
            for c in range(4):
                n = RNN0 + c
                used(n)
                for m in range(2):
                    i = 2 * (c % 2) + m
                    if c < 2:
                        act.activation(cx[:, i, :], bank(2 * (c % 2) + m), ACT.Identity, bias=col(PC_RCONV + 5 * i + 4),
                                       scale=col(PC_RCONV + 5 * i + 3)).then_inc(cx_init, 1)
                    else:
                        last = act.activation(gg[:, i, :], bank(2 * (c % 2) + m), ACT.Gelu_apprx_tanh)
                if c >= 2:
                    last.then_inc(proj2_evac, 1)
                after(n)
                if c == 1:
                    act.wait_ge(kcv_ready, 1)
                    act.activation(kcT[:, 0:N_CMP], ps[:, 4, 0:N_CMP], ACT.Copy).then_inc(kcv_evac, 1)
                    act.activation(vcs[0:N_CMP, :], ps[0:N_CMP, 5, 0:P], ACT.Copy).then_inc(kcv_evac, 1)
            for i in range(4):
                act.wait_ge(lru_ready, i + 1)
                act.activation(rr[:, i, :], bank(4 + i), ACT.Sigmoid, bias=col(PC_BA + i)).then_inc(sig_ready, 1)
            for i in range(4):
                act.wait_ge(lru_ready, 5 + i)
                act.activation(ii[:, i, :], bank(i), ACT.Sigmoid, bias=col(PC_BX + i)).then_inc(sig_ready, 1)
            act.wait_ge(sig_ready, 8)
            act.wait_ge(lru_step, 14)
            for i in range(4):
                act.activation(rr[:, i, :], rr[:, i, :], ACT.Tanh, scale=lru_c[:, 5, i:i + 1]).then_inc(th_ready, 1)
            act.wait_ge(th_ready, 4)
            for i in range(4):
                act.activation(mm[:, i, :], rr[:, i, :], ACT.Sqrt, scale=-1.0).then_inc(sqrt_ready, 1)
            act.wait_ge(rnn_ready, 4)

            with act.Fori(0, 4) as r:
                past(act, s2_done, r * 18)
                past(act, sc_done, r * 18)
                for g in range(2):
                    h = slice(HD * g, HD * g + HD)
                    act.activation(qc[h, g, :], q2_f[h, bass.ds(r * S, S)], ACT.Copy)
                for g in range(2):
                    last = act.activation(tsl[:, g, :], alibi, ACT.Copy, scale=slopes[:, bass.ds(r + 4 * g, 1)])
                last.then_inc(staged2, 1)

                def exps(U):
                    past(act, sc_done, r * 18 + U + 1)
                    if U % 9 < 8:
                        w = (U % 9 % 4 + 1) * P
                        act.activation(pb[:, U % 3, 0:w], pb[:, U % 3, 0:w], ACT.Exp, bias=soft[:, 0, U:U + 1], scale=-1.0,
                                       accum_out=soft[:, 1, U:U + 1]).then_inc(exp_done, 1)
                    else:
                        act.activation(pb[:, U % 3, 0:P], pb[:, U % 3, 0:P], ACT.Exp, scale=-1.0).then_inc(exp_done, 1)

                def keep_turned(U):
                    g, v = U // 9, U % 9
                    past(act, t_done, r * 18 + U + 1)
                    past(act, pv2_done, r * 2 + g)
                    if v < 8:
                        i = v % 4
                        act.activation(pt[:, v // 4, 0:i + 1, i * P:(i + 1) * P],
                                       ps[:, 3 + U % 3, 0:(i + 1) * P].rearrange("p (j t) -> p j t", t=P), ACT.Copy)\
                           .then_inc(pt_evac, 1)
                    else:
                        act.activation(ptc[0:N_CMP, :], ps[0:N_CMP, 3 + U % 3, :], ACT.Copy).then_inc(pt_evac, 1)

                def head_out(g):
                    h = slice(HD * g, HD * g + HD)
                    past(act, pv2_done, r * 2 + g + 1)
                    act.activation(att_f[h, bass.ds(r * S, S)], ps[h, 6 + g, :], ACT.Copy).then_inc(att_evac, 1)

                for U in range(18):
                    exps(U)
                    if U >= 2:
                        keep_turned(U - 2)
                    if U == 12:
                        head_out(0)
                keep_turned(16)
                keep_turned(17)
                head_out(1)

            past(act, att_evac, 8)
            for b, src in enumerate((cx, att)):
                for i in range(4):
                    if 4 * b + i >= 2:
                        act.wait_ge(sq4_used, 4 * b + i - 1)
                    act.activation(sqb2[:, i % 2, :], src[:, i, :], ACT.Square).then_inc(sq4_ready, 1)
                act.wait_ge(sq4_used, 4 * b + 4)
                if b:
                    act.wait_ge(rstd4_ready, 1)
                act.activation(std[:, :], bank(7), ACT.Sqrt, bias=eps[:, :], scale=2.0 / D).then_inc(std4_ready, 1)
                for i in range(4):
                    act.wait_ge(nt4_ready, 4 * b + i + 1)
                    act.activation(xh[:, 4 * b + i, :], nt2[:, i % 2, :], ACT.Copy).then_inc(nh4_ready, 1)
            for w in range(4):
                n = WO2 + w
                used(n)
                for m in range(2):
                    act.activation(ymix[:, 2 * w + m, :], bank(2 * (w % 2) + m), ACT.Copy).then_inc(y_ready, 1)
                for m in range(2):
                    act.wait_ge(y_ready, 2 * w + m + 1)
                    square(6, 2 * w + m, sqb2, ymix, th=4)
                if w < 3:
                    after(n)
            root(th=4)
            for i in range(KT):
                act.wait_ge(x2_ready, i + 1)
                square(7, i, sqb2, x, alone=2)
            root(alone=2)
            highs(5, nt2, shift=24)
            after(FF0 - 1)

            def relu_step(g, n, thirds, n_s, par):
                used(n)
                past(act, ab_ready, g * 2)
                past(act, ah2_ready, g * 2)
                for r in range(2):
                    act.activation(rl[:, r, :], bank(r), ACT.Relu).then_inc(rl_ready, 1)
                for r in range(2):
                    past(act, rl_ready, g * 2 + r + 1)
                    act.activation(ah2[:, par, r, :], rl[:, r, :], ACT.Square).then_inc(ah2_ready, 1)
                if n_s is not None:
                    high(n + RING, n_s, thirds)

            relu_step(0, FF0, (FF0 + RING) // RING, FF0 % RING, 0)
            with act.Fori(0, (NG2 - 1) // 3 - 1) as it:
                for v in range(3):
                    c = FF0 + 1 + 2 * v
                    n = it * 6 + c
                    relu_step(it * 3 + (1 + v), n, it * 2 + (c + RING) // RING, c % RING, (1 + v) % 3)
                    used(n + 1)
                    high(n + 1 + RING, (c + 1) % RING, it * 2 + (c + 1 + RING) // RING)
            for g in range(NG2 - 3, NG2):
                n = FF0 - 1 + 2 * g
                relu_step(g, n, (n + RING) // RING, n % RING if n + RING < SLABS else None, g % 3)
                used(n + 1)
                after(n + 1)
            for i in range(KT):
                past(act, y2_added, 8 * NG2 - 8 + i + 1)
                square(8, i, sqb2, ymix, th=5)
            root(th=5)

        @block.vector
        def _(dve):
            for s in vector_counts:
                dve.sem_inc(s, 1)
            dve.memset(eps[:, :], EPS).then_inc(eps_set, 1)
            dve.wait_ge(params_loaded, 16 * 3)
            dve.wait_ge(silu_c_ready, 1)
            dve.memset(ws[HD:P, :, 0:HD], 0.0).then_inc(ws_masked, 1)
            lam = col(PC_LAM, 4)
            step = [0]

            def lru_op(ins):
                step[0] += 1
                ins.then_inc(lru_step, 1)
                dve.wait_ge(lru_step, step[0])

            lru_op(dve.scalar_tensor_tensor(lru_c[:, 0, :], lam, -1.0, lam, ALU.mult, ALU.max))
            dve.wait_ge(lru_exp, 1)
            lru_op(dve.tensor_scalar(lru_c[:, 2, :], lru_c[:, 1, :], 2.0, None, ALU.add))
            lru_op(dve.reciprocal(lru_c[:, 2, :], lru_c[:, 2, :]))
            lru_op(dve.tensor_tensor(lru_c[:, 3, :], lru_c[:, 1, :], lru_c[:, 2, :], ALU.mult))
            lru_op(dve.tensor_tensor(lru_c[:, 4, :], lru_c[:, 3, :], lru_c[:, 3, :], ALU.mult))
            lru_op(dve.tensor_scalar(lru_c[:, 5, :], lru_c[:, 4, :], 1.0 / 15, None, ALU.mult))
            for odd in (13, 11, 9, 7, 5, 3):
                lru_op(dve.scalar_tensor_tensor(lru_c[:, 5, :], lru_c[:, 5, :], 1.0 / odd, lru_c[:, 4, :], ALU.add, ALU.mult))
            lru_op(dve.scalar_tensor_tensor(lru_c[:, 3, :], lru_c[:, 5, :], 1.0, lru_c[:, 3, :], ALU.add, ALU.mult))
            lru_op(dve.tensor_scalar(lru_c[:, 2, :], lam, 0.0, 4.0, ALU.min, ALU.mult))
            dve.scalar_tensor_tensor(lru_c[:, 5, :], lru_c[:, 3, :], -8.0, lru_c[:, 2, :], ALU.mult, ALU.add).then_inc(lru_step, 1)

            def add_square(nk, th, i, buf):
                dve.wait_ge(sq_ready, nk * KT + i + 1)
                if i == 1:
                    ins = dve.tensor_tensor(std[:, :], buf[:, 0, :], buf[:, 1, :], ALU.add)
                else:
                    dve.wait_ge(sq_added, th * (KT - 2) + i - 1)
                    ins = dve.tensor_tensor(std[:, :], std[:, :], buf[:, i % 2, :], ALU.add)
                ins.then_inc(sq_added, 1)

            def inverse(nk):
                dve.wait_ge(std_ready, nk + 1)
                dve.reciprocal(rstd[:, :], std[:, :]).then_inc(rstd_ready, 1)
                dve.wait_ge(rstd_ready, nk + 1)

            def normalise(nk, sk, buf, gain, shift=None):
                inverse(nk)

                def low(i):
                    dve.wait_ge(nh_ready, sk * KT + i + 1)
                    if shift is None:
                        ins = dve.tensor_tensor(xl[:, i, :], buf[:, i % 2, :], xh[:, i, :].bitcast(F32), ALU.subtract)
                    else:
                        ins = dve.scalar_tensor_tensor(xl[:, i, :], buf[:, i % 2, :], mod[:, shift + i:shift + i + 1],
                                                       xh[:, i, :].bitcast(F32), ALU.add, ALU.subtract)
                    ins.then_inc(nl_ready, 1)

                for i in range(KT):
                    if i >= 2:
                        dve.wait_ge(nl_ready, sk * KT + i - 1)
                    dve.scalar_tensor_tensor(buf[:, i % 2, :], x[:, i, :], gain(i), rstd[:, :], ALU.mult, ALU.mult).then_inc(nt_ready, 1)
                    if i >= 1:
                        low(i - 1)
                low(KT - 1)

            def ada_sum(a, buf, loaded):
                dve.wait_ge(ada_loaded, loaded * 16)
                past(dve, ada_done, a)
                for kt in range(KT):
                    if kt == 0:
                        ins = dve.tensor_scalar(ada_acc[:, :], buf[:, 0, :], silu_c[:, 0:1], None, ALU.mult)
                    else:
                        dve.wait_ge(ada_term, a * (KT - 1) + kt)
                        ins = dve.scalar_tensor_tensor(ada_acc[:, :], buf[:, kt, :], silu_c[:, kt:kt + 1], ada_acc[:, :],
                                                       ALU.mult, ALU.add)
                    ins.then_inc(ada_term if kt < KT - 1 else ada_summed, 1)

            def ada_out(a):
                past(dve, ada_done, a + 1)
                dve.tensor_tensor(cols(mod, a * 2, 2), ps[:, 7, 0:2], col(a * 2 + PC_ADAB, 2), ALU.add).then_inc(ada_evac, 1)

            with dve.Fori(0, LAYERS) as l:
                normalise(l * 2, l * 2, nt, lambda i: col(l * PC_LN + (PC_L + i)))
                dve.wait_ge(vstd_ready, l + 1)
                dve.reciprocal(vss[:, 2, :], vss[:, 1, :]).then_inc(vr_ready, 1)
                dve.wait_ge(vr_ready, l + 1)
                for i in range(NT):
                    last = dve.tensor_scalar(va[:, i, :], va[:, i, :], vss[:, 2, i:i + 1], None, ALU.mult)
                last.then_inc(va_ready, 1)
                for i in range(8):
                    t = q if i < 4 else k
                    dve.wait_ge(rot_ready, l * 8 + i + 1)
                    if i >= 2:
                        dve.wait_ge(rope_done, l * 8 + i - 1)
                    dve.tensor_tensor(rtmp[:, i % 2, :], bank(4 + i % 4), sin, ALU.mult)
                    dve.tensor_tensor(t[:, i % 4, :], t[:, i % 4, :], cos, ALU.mult).then_inc(rope_part, 1)
                    dve.wait_ge(rope_part, l * 8 + i + 1)
                    dve.tensor_tensor(t[:, i % 4, :], t[:, i % 4, :], rtmp[:, i % 2, :], ALU.add).then_inc(rope_done, 1)
                dve.wait_ge(sv_ready, l + 1)
                for j in range(2):
                    for hh in range(2):
                        h = slice(HD * hh, HD * hh + HD)
                        o = ya[h, j, :].rearrange("p (i t) -> p i t", i=NT)
                        b = bsb_f[h, bass.ds(l * 256 + j * P, P)].rearrange("p (a t) -> p a t", a=1).broadcast_to((HD, NT, P))
                        dve.scalar_tensor_tensor(o, ps[h, 4:8, j * 256 + hh * P:j * 256 + hh * P + P],
                                                 prm[h, bass.ds(l * PC_LN + (PC_L + 8 + j), 1)], b, ALU.mult, ALU.add).then_inc(ya_part, 1)
                for j in range(2):
                    dve.wait_ge(ya_part, l * 4 + 2 * j + 2)
                    dve.tensor_tensor(ya[:, j, :], ya[:, j, :], u[:, j, :], ALU.mult).then_inc(ya_ready, 1)
                for j in range(2):
                    dve.wait_ge(mix_hi, l * 8 + j + 1)
                    dve.tensor_tensor(xl[:, j, :], ya[:, j, :], xh[:, j, :].bitcast(F32), ALU.subtract).then_inc(mix_split, 1)
                for j in range(2):
                    dve.wait_ge(mix_hi, l * 8 + j + 3)
                    dve.scalar_tensor_tensor(xl[:, 2 + j, :], bank(4 + j), col(l * PC_LN + (PC_L + 10 + j)),
                                             xh[:, 2 + j, :].bitcast(F32), ALU.mult, ALU.subtract).then_inc(mix_split, 1)
                with dve.Fori(0, 2) as it:
                    for p in range(2):
                        for hh in range(2):
                            head = l * 8 + it * 4 + (2 * p + hh)
                            dve.wait_ge(pv_done, head + 2)
                            dve.wait_ge(s_done, head + 1)
                            for j in range(NT):
                                b, o = sbank[j]
                                w = S - j * P
                                last = dve.tensor_tensor(sT[:, hh, soffs[j]:soffs[j] + w], ps[:, 3 * hh + b, o:o + w],
                                                         cols(D_f, it * (4 * S) + (2 * p + hh) * S, w), ALU.mult)
                            last.then_inc(sT_ready, 1)
                    dve.wait_ge(mean_ready, l * 4 + it + 1)
                    even = y_f[:, bass.ds(it * (2 * S), S)]
                    dve.tensor_tensor(even, even, bank(2), ALU.subtract).then_inc(yc_ready, 1)
                    dve.wait_ge(yc_ready, l * 4 + it + 1)
                    dve.tensor_tensor(ya_f[:, bass.ds(it * S, S)], even, even, ALU.mult).then_inc(gsq_ready, 1)
                for t in range(2):
                    dve.wait_ge(mean_ready, l * 4 + t + 3)
                    dve.tensor_tensor(y[:, 2 * t + 1, :], y[:, 2 * t + 1, :], bank(4 + t), ALU.subtract).then_inc(yc_ready, 1)
                for half in range(2):
                    turns = [(2 * half + t, turn_order[2 * half + t], (gsq if half else ya)[:, t, :]) for t in range(2)]
                    for turn, i, dev in turns:
                        dve.wait_ge(gsd_ready, l * 4 + turn + 1)
                        dve.reciprocal(dev, dev).then_inc(gr_ready, 1)
                    for turn, i, dev in turns:
                        dve.wait_ge(gr_ready, l * 4 + turn + 1)
                        dve.scalar_tensor_tensor(y[:, i, :], y[:, i, :], col(l * PC_LN + (PC_L + 12 + i)), dev, ALU.mult,
                                                 ALU.mult).then_inc(yn_ready, 1)
                    for turn, i, dev in turns:
                        dve.wait_ge(yn_ready, l * 4 + turn + 1)
                        dve.tensor_tensor(y[:, i, :], y[:, i, :], sg[:, i, :], ALU.mult).then_inc(gm_ready, 1)
                    for turn, i, dev in turns:
                        dve.wait_ge(mix_hi, l * 8 + turn + 5)
                        dve.tensor_tensor(xl[:, 4 + i, :], y[:, i, :], xh[:, 4 + i, :].bitcast(F32), ALU.subtract).then_inc(mix_split, 1)
                for i in range(KT):
                    w = i // 2
                    if i % 2 == 0:
                        dve.wait_ge(half_done, l * W_OUT + w + 1)
                    else:
                        dve.wait_ge(slab_used, l * LAYER_SLABS + (W_IN + w + 1 + RING))
                    dve.tensor_tensor(x[:, i, :], x[:, i, :], bank(2 * ((W_IN + w) % 2) + i % 2), ALU.add).then_inc(mix_added, 1)
                    if i >= 2:
                        add_square(l * 2 + 1, l * 2, i - 1, sqb)
                normalise(l * 2 + 1, l * 2 + 1, nt, lambda i: col(l * PC_LN + (PC_L + 16 + i)))

                def conv(j, half):
                    c0 = l * PC_CONVN + j * 16 + PC_CONV
                    for r in (2 * half, 2 * half + 1):
                        dve.wait_ge(cv_init, l * 4 * NG + j * 4 + r + 1)
                        dve.scalar_tensor_tensor(cv[:, r, 1:S], ps[:, r, 0:S - 1], col(c0 + (r * 4 + 1)), cv[:, r, 1:S],
                                                 ALU.mult, ALU.add).then_inc(conv_mid, 1)
                    for r in (2 * half, 2 * half + 1):
                        dve.wait_ge(conv_mid, l * 4 * NG + j * 4 + r + 1)
                        dve.scalar_tensor_tensor(cv[:, r, 2:S], ps[:, r, 0:S - 2], col(c0 + r * 4), cv[:, r, 2:S],
                                                 ALU.mult, ALU.add).then_inc(conv_done, 1)

                def gate(j, r):
                    past(dve, conv_done, l * 4 * NG + j * 4 + r + 3)
                    past(dve, act_split, l * 2 * NG + j * 2)
                    dve.wait_ge(sil_ready, l * 2 * NG + j * 2 + r + 1)
                    dve.tensor_tensor(ab[:, r, :], cv[:, r, :], cv[:, 2 + r, :], ALU.mult).then_inc(a_ready, 1)

                def gate_low(j, par, r):
                    dve.wait_ge(ah_ready, l * 2 * NG + j * 2 + r + 1)
                    dve.tensor_tensor(al[:, par, r, :], ab[:, r, :], ah[:, par, r, :].bitcast(F32), ALU.subtract).then_inc(act_split, 1)

                def add_down(j, n, between):
                    for o in range(KT):
                        if o < KT - 1:
                            dve.wait_ge(down_done, l * (KT - 1) * NG + j * (KT - 1) + o + 1)
                        else:
                            dve.wait_ge(slab_used, n + 1 + RING)
                        dve.tensor_tensor(x[:, o, :], x[:, o, :], bank(4 + o % 3), ALU.add).then_inc(ffn_added, 1)
                        between(o)

                n0 = l * LAYER_SLABS
                conv(0, 0)
                ada_sum(l * NG, adab, l * NG + 1)
                conv(0, 1)
                for r in range(2):
                    gate(0, r)
                for r in range(2):
                    gate_low(0, 0, r)
                ada_out(l * NG)
                with dve.Fori(0, (NG - 1) // 2) as it:
                    for v in range(2):
                        j = it * 2 + (1 + v)

                        def gating(o):
                            if o in (2, 3):
                                gate(j, o - 2)
                            if o in (5, 6):
                                gate_low(j, (1 + v) % 2, o - 5)

                        conv(j, 0)
                        ada_sum(l * NG + j, adab, l * NG + j + 1)
                        conv(j, 1)
                        add_down(it * 2 + v, n0 + it * 6 + (MLP0 + 4 + 3 * v), gating)
                        ada_out(l * NG + j)

                def next_norm(o):
                    if o >= 2:
                        add_square(l * 2 + 2, l * 2 + 1, o - 1, sqb)

                add_down(NG - 1, n0 + (LAYER_SLABS - 1), next_norm)

            inverse(4)
            for i in range(KT):
                dve.scalar_tensor_tensor(x[:, i, :], x[:, i, :], col(PC_FINAL + i), rstd[:, :], ALU.mult, ALU.mult).then_inc(xf_ready, 1)
            past(dve, ada_evac, LAYERS * NG)

            def fold(n, scale, g):
                dve.scalar_tensor_tensor(gains[:, n, :], mod[:, scale:scale + KT], 1.0, col(g, KT), ALU.add, ALU.mult).then_inc(gains_ready, 1)

            for n, (scale, g) in enumerate(((8, PC_PREMIX), (16, PC_POSTMIX), (32, PC_PREMLP))):
                fold(n, scale, g)
            dve.memset(kkh[:, :, :, :].bitcast(F32), 0.0)
            dve.memset(kkl[:, :, :, :].bitcast(F32), 0.0)
            dve.memset(qc[:, :, :], 0.0).then_inc(zeroed, 1)
            dve.wait_ge(gains_ready, 3)
            normalise(5, 4, nt2, lambda i: gains[:, 0, i:i + 1], shift=0)
            dve.wait_ge(gwh_ready, 1)
            dve.tensor_tensor(gwl[:, :, :], gw[:, :, :], gwh[:, :, :].bitcast(F32), ALU.subtract).then_inc(gw_split, 1)
            for t in range(ADA_SLABS - LAYERS * NG):
                ada_sum(LAYERS * NG + t, adab_tail[:, t, :, :], ADA_SLABS)
                ada_out(LAYERS * NG + t)
            past(dve, ada_evac, ADA_SLABS)
            fold(3, 40, PC_POSTMLP)
            dve.wait_ge(zeroed, 1)
            for kv in range(2):
                for g in range(2):
                    dve.wait_ge(kkh_ready, 2 * kv + g + 1)
                    b = 4 + 2 * kv + g
                    dve.tensor_tensor(kkl[0:HD, kv, g, 0:S], ps[0:HD, b, :], kkh[0:HD, kv, g, 0:S].bitcast(F32), ALU.subtract)
                    dve.tensor_tensor(kkl[HD:P, kv, g, 0:S - 1], ps[HD:P, b, 1:S], kkh[HD:P, kv, g, 0:S - 1].bitcast(F32), ALU.subtract)
                    dve.tensor_tensor(kkl[:, kv, g, S:S + 31:2], col(PC_POS + 16 * kv, 16), kkh[:, kv, g, S:S + 31:2].bitcast(F32),
                                      ALU.subtract).then_inc(kk_split, 1)
            dve.wait_ge(gates_sig, 1)
            dve.tensor_scalar(gates[:, 0, 0:8], gates[:, 0, 0:8], seen, None, ALU.mult).then_inc(gates_ready, 1)
            for c in range(2):
                for tap in (1, 2, 3):
                    for m in range(2):
                        i = 2 * c + m
                        if tap == 1:
                            dve.wait_ge(cx_init, i + 1)
                        else:
                            dve.wait_ge(cx_mid, 4 * c + 2 * (tap - 2) + m + 1)
                        dve.scalar_tensor_tensor(cx[:, i, tap:S], ps[:, i, 0:S - tap], col(PC_RCONV + 5 * i + 3 - tap), cx[:, i, tap:S],
                                                 ALU.mult, ALU.add).then_inc(cx_mid if tap < 3 else cx_done, 1)
            dve.wait_ge(cx_done, 4)
            dve.wait_ge(sig_ready, 8)
            for i in range(4):
                dve.tensor_tensor(ii[:, i, :], ii[:, i, :], cx[:, i, :], ALU.mult)
            for i in range(4):
                dve.wait_ge(th_ready, i + 1)
                dve.tensor_scalar(dd[:, i, :], rr[:, i, :], -1.0, 1.0, ALU.mult, ALU.add).then_inc(dd_ready, 1)
            for i in range(4):
                dve.wait_ge(dd_ready, i + 1)
                dve.reciprocal(dd[:, i, :], dd[:, i, :]).then_inc(dd_ready, 1)
            for i in range(4):
                dve.wait_ge(dd_ready, 5 + i)
                dve.wait_ge(sqrt_ready, i + 1)
                dve.scalar_tensor_tensor(rr[:, i, :], rr[:, i, :], 1.0, dd[:, i, :], ALU.add, ALU.mult)
                dve.scalar_tensor_tensor(mm[:, i, :], mm[:, i, :], 2.0, dd[:, i, :], ALU.mult, ALU.mult).then_inc(aa_ready, 1)
            for i in range(4):
                dve.wait_ge(aa_ready, i + 1)
                dve.tensor_tensor(mm[:, i, :], mm[:, i, :], ii[:, i, :], ALU.mult).then_inc(uu_ready, 1)
            for i in range(4):
                dve.wait_ge(uu_ready, i + 1)
                dve.tensor_tensor_scan(cx[:, i, :], rr[:, i, :], mm[:, i, :], 0.0, ALU.mult, ALU.add).then_inc(scan_ready, 1)
            dve.wait_ge(proj2_evac, 7)
            for i in range(4):
                dve.wait_ge(scan_ready, i + 1)
                dve.tensor_tensor(cx[:, i, :], cx[:, i, :], gg[:, i, :], ALU.mult).then_inc(rnn_ready, 1)

            dve.wait_ge(gates_ready, 1)
            with dve.Fori(0, 4) as r:
                dve.wait_ge(staged2, r + 1)

                def minima(U):
                    g, v = U // 9, U % 9
                    past(dve, s2_done, r * 18 + U + 1)
                    past(dve, t_done, r * 18 + (U - 2 if U >= 3 else 0))
                    if v < 8:
                        i = v % 4
                        w = (i + 1) * P
                        dve.memset(soft[:, 3, U:U + 1], 0.0)
                        dve.tensor_tensor_reduce(out=pb[:, U % 3, 0:w], in0=ps[:, U % 3, 0:w], in1=tsl[:, g, S - w:S], scale=1.0,
                                                 scalar=3e38, op0=ALU.add, op1=ALU.min, accum_out=soft[:, 0, U:U + 1]).then_inc(sc_done, 1)
                    else:
                        s3 = pb[:, U % 3, 0:P].rearrange("p (i c) -> p i c", c=32)
                        c31 = s3[:, :, 0:N_CMP]
                        base = r * 12 + 6 * g
                        dve.memset(pb[:, U % 3, 0:P], 0.0).then_inc(cmp_step, 1)
                        dve.wait_ge(cmp_step, base + 1)
                        dve.scalar_tensor_tensor(c31, alibi_c[:, :, 0:N_CMP], slopes[:, bass.ds(r + 4 * g, 1)],
                                                 ps[:, U % 3, 0:P].rearrange("p (i c) -> p i c", c=32)[:, :, 0:N_CMP],
                                                 ALU.mult, ALU.add).then_inc(cmp_step, 1)
                        dve.wait_ge(cmp_step, base + 2)
                        dve.tensor_reduce(cst[:, 0, :], c31, AX.X, ALU.min).then_inc(cmp_step, 1)
                        dve.wait_ge(cmp_step, base + 3)
                        dve.tensor_tensor(c31, c31, cst[:, 0, :].rearrange("p (i a) -> p i a", a=1).broadcast_to((P, NT, N_CMP)),
                                          ALU.subtract).then_inc(sc_done, 1)

                def weigh(U):
                    g, v = U // 9, U % 9
                    dve.wait_ge(exp_done, r * 18 + U + 1)
                    if v < 8:
                        i = v % 4
                        w = (i + 1) * P
                        dve.reciprocal(soft[:, 2, U:U + 1], soft[:, 1, U:U + 1]).then_inc(rs_ready, 1)
                        dve.wait_ge(rs_ready, r * 16 + 8 * g + v + 1)
                        dve.tensor_scalar(pb[:, U % 3, 0:w], pb[:, U % 3, 0:w], soft[:, 2, U:U + 1],
                                          gates[:, i, bass.ds(r + ((1 + v // 4) * 8 + 4 * g), 1)], ALU.mult, ALU.mult).then_inc(p_ready, 1)
                    else:
                        c31 = pb[:, U % 3, 0:P].rearrange("p (i c) -> p i c", c=32)[:, :, 0:N_CMP]
                        base = r * 12 + 6 * g
                        dve.tensor_reduce(cst[:, 1, :], c31, AX.X, ALU.add).then_inc(cmp_step, 1)
                        dve.wait_ge(cmp_step, base + 4)
                        dve.reciprocal(cst[:, 2, :], cst[:, 1, :]).then_inc(cmp_step, 1)
                        dve.wait_ge(cmp_step, base + 5)
                        dve.tensor_tensor(cst[:, 3, :], cst[:, 2, :], gates[:, :, bass.ds(r + 4 * g, 1)].rearrange("p i a -> p (i a)"),
                                          ALU.mult).then_inc(cmp_step, 1)
                        dve.wait_ge(cmp_step, base + 6)
                        dve.tensor_tensor(c31, c31, cst[:, 3, :].rearrange("p (i a) -> p i a", a=1).broadcast_to((P, NT, N_CMP)),
                                          ALU.mult).then_inc(p_ready, 1)

                for U in range(18):
                    minima(U)
                    if U >= 1:
                        weigh(U - 1)
                weigh(17)

            for b, (src, g) in enumerate(((cx, PC_NRNN), (att, PC_NATT))):
                dve.wait_ge(std4_ready, b + 1)
                dve.reciprocal(rstd[:, :], std[:, :]).then_inc(rstd4_ready, 1)
                dve.wait_ge(rstd4_ready, b + 1)

                def low4(i):
                    dve.wait_ge(nh4_ready, 4 * b + i + 1)
                    dve.tensor_tensor(xl[:, 4 * b + i, :], nt2[:, i % 2, :], xh[:, 4 * b + i, :].bitcast(F32), ALU.subtract).then_inc(nl4_ready, 1)

                for i in range(4):
                    if 4 * b + i >= 2:
                        dve.wait_ge(nl4_ready, 4 * b + i - 1)
                    dve.scalar_tensor_tensor(nt2[:, i % 2, :], src[:, i, :], col(g + i), rstd[:, :], ALU.mult, ALU.mult).then_inc(nt4_ready, 1)
                    if i >= 1:
                        low4(i - 1)
                low4(3)

            def post_norm(nk, n, first):
                inverse(nk)
                for i in range(KT + 1):
                    if i < KT:
                        dve.scalar_tensor_tensor(ymix[:, i, :], ymix[:, i, :], gains[:, n, i:i + 1], rstd[:, :], ALU.mult, ALU.mult)\
                           .then_inc(pn_ready, 1)
                    if i >= 1:
                        dve.wait_ge(pn_ready, first + i)
                        dve.tensor_tensor(x[:, i - 1, :], x[:, i - 1, :], ymix[:, i - 1, :], ALU.add).then_inc(x2_ready, 1)

            for i in range(1, KT - 1):
                add_square(6, 4, i, sqb2)
            dve.wait_ge(gains_ready, 4)
            post_norm(6, 1, 0)
            dve.wait_ge(x2_ready, KT)
            dve.memset(ymix[:, :, :], 0.0).then_inc(y_zero, 1)
            normalise(7, 5, nt2, lambda i: gains[:, 2, i:i + 1], shift=24)
            dve.wait_ge(y_zero, 1)

            def relu_square(g, r):
                past(dve, act2_split, g * 2)
                past(dve, rl_ready, g * 2 + r + 1)
                dve.tensor_tensor(ab2[:, r, :], rl[:, r, :], rl[:, r, :], ALU.mult).then_inc(ab_ready, 1)

            def relu_low(g, par, r):
                past(dve, ab_ready, g * 2 + r + 1)
                past(dve, ah2_ready, g * 2 + r + 1)
                dve.tensor_tensor(al2[:, par, r, :], ab2[:, r, :], ah2[:, par, r, :].bitcast(F32), ALU.subtract).then_inc(act2_split, 1)

            def add_down2(g, n, between):
                for o in range(KT):
                    if o < KT - 1:
                        dve.wait_ge(down2_done, g * (KT - 1) + o + 1)
                    else:
                        dve.wait_ge(slab_used, n + 1 + RING)
                    dve.tensor_tensor(ymix[:, o, :], ymix[:, o, :], bank(2 + o % 4), ALU.add).then_inc(y2_added, 1)
                    between(o)

            for r in range(2):
                relu_square(0, r)
            for r in range(2):
                relu_low(0, 0, r)
            with dve.Fori(0, (NG2 - 1) // 3) as it:
                for v in range(3):
                    def activation(o):
                        if o in (1, 2):
                            relu_square(it * 3 + (1 + v), o - 1)
                        if o in (3, 4):
                            relu_low(it * 3 + (1 + v), (1 + v) % 3, o - 3)

                    add_down2(it * 3 + v, it * 6 + (FF0 + 2 + 2 * v), activation)

            def last_norm(o):
                if o >= 2:
                    add_square(8, 5, o - 1, sqb2)

            add_down2(NG2 - 1, SLABS - 1, last_norm)
            post_norm(8, 3, KT)


def slab8(w):
    return w.reshape(KT, P, GRP).transpose(1, 0, 2).reshape(P, SLABW)


def slab2(w):
    return w.reshape(2, P, D).transpose(1, 0, 2).reshape(P, SLABW)


def columns(v):
    return v.reshape(-1, P).T


def kernel(**inputs):
    import concourse.bacc as bacc
    from concourse.bass_utils import run_bass_kernel_spmd

    a = {n: np.asarray(v) for n, v in inputs.items()}
    f = np.float32
    pairs = np.concatenate([np.r_[r * HD:(r + 1) * HD, (4 + r) * HD:(5 + r) * HD] for r in range(4)])

    slabs = np.empty((SLABS, P, SLABW), f)
    n = 0

    def add(slab):
        nonlocal n
        slabs[n] = slab
        n += 1

    for l in range(LAYERS):
        for c in range(W_IN):
            add(slab8(a["w_in"][l][:, c * GRP:(c + 1) * GRP]))
        for c in range(W_OUT):
            add(slab8(a["w_out"][l][:, c * GRP:(c + 1) * GRP]))
        for j in range(NG):
            add(slab8(a["w_up"][l][:, j * GRP:(j + 1) * GRP]))
            add(slab8(a["w_up"][l][:, DFF + j * GRP:DFF + (j + 1) * GRP]))
            if j:
                add(slab2(a["w_down"][l][(j - 1) * GRP:j * GRP]))
        add(slab2(a["w_down"][l][DFF - GRP:]))
    w2 = a["w_in_2"][0]
    heads = w2[:, 1024:1536][:, pairs]
    rest = {m: w2[:, 1536 + P * i:1536 + P * (i + 1)] for i, m in enumerate(("kc", "vc", "ks", "vs", "kw", "vw"))}
    add(slab8(np.concatenate([rest["kc"], rest["vc"]], 1)))
    add(slab8(np.concatenate([rest["ks"], rest["kw"]], 1)))
    add(slab8(np.concatenate([rest["vs"], rest["vw"]], 1)))
    add(slab8(heads[:, 0:GRP]))
    add(slab8(heads[:, GRP:]))
    for w1 in (a["cmp_w1_k_2"][0], a["cmp_w1_v_2"][0]):
        for part in range(2):
            add(slab8(w1[part * D:(part + 1) * D]))
    for c in (2, 3, 0, 1):
        add(slab8(w2[:, c * GRP:(c + 1) * GRP]))
    wo = a["w_out_2"][0]
    wo = np.concatenate([wo[0:512], wo[512:][pairs]], 0)
    for c in range(4):
        add(slab8(wo[:, c * GRP:(c + 1) * GRP]))
    for g in range(NG2):
        add(slab8(a["w_ff1_2"][0][:, g * GRP:(g + 1) * GRP]))
        if g:
            add(slab2(a["w_ff2_2"][0][(g - 1) * GRP:g * GRP]))
    add(slab2(a["w_ff2_2"][0][DFF2 - GRP:]))
    assert n == SLABS

    ada = np.stack([slab8(a["ada_w_2"][0][:, i * GRP:(i + 1) * GRP]) for i in range(ADA_SLABS)])

    prm = []
    for l in range(LAYERS):
        prm += [columns(a[m][l]) for m in ("norm1_g", "a_vnorm_g", "b_scale", "c_norm_g", "norm2_g")]
    for l in range(LAYERS):
        taps = np.concatenate([a["conv_w"][l], a["conv_b"][l][None]], 0).reshape(4, 2, NG, 2, P)
        prm.append(taps.transpose(4, 2, 1, 3, 0).reshape(P, PC_CONVN))
    prm += [columns(a["final_g"]), columns(a["c_2"][0]), columns(a["ada_b_2"][0])]
    prm += [columns(a[m][0]) for m in ("pre_norm_mix_2", "post_norm_mix_2", "pre_norm_mlp_2", "post_norm_mlp_2")]
    taps = np.concatenate([a["conv_w_2"][0], a["conv_b_2"][0][None]], 0).reshape(5, 4, P)
    prm.append(taps.transpose(2, 1, 0).reshape(P, 20))
    prm += [columns(a[m][0]) for m in ("lru_ba_2", "lru_bx_2", "lru_lambda_2", "norm_rnn_out_2")]
    prm.append(columns(a["norm_att_out_2"][0][pairs]))
    prm += [columns(a["cmp_pos_k_2"][0].reshape(-1)), columns(a["cmp_pos_v_2"][0].reshape(-1))]
    prm = np.ascontiguousarray(np.concatenate(prm, 1))

    def half_pairs(w):
        out = np.zeros((P, len(w) // 2, P), f)
        for i in range(len(w)):
            o = HD * (i % 2)
            out[o:o + HD, i // 2, o:o + HD] = w[i]
        return out

    bs = a["a_bs"].reshape(LAYERS * 2, 2, P)
    w2k = np.zeros((P, 2, 2, P), f)
    for m in range(2):
        for g in range(2):
            w2k[:, m, g, g * HD:(g + 1) * HD] = a["cmp_w2_k_2"][0][m * P:(m + 1) * P]
    c1, c2 = constants()
    arrays = {
        "weights": slabs,
        "ada": ada,
        "params": prm,
        "xin": a["x"][0].T.reshape(KT, P, S).transpose(1, 0, 2),
        "wsT": a["a_ws"].reshape(LAYERS * 4, P, P).transpose(2, 0, 1),
        "bsb": np.repeat(bs.transpose(1, 0, 2), HD, axis=0),
        "bw": half_pairs(a["b_w"].reshape(LAYERS * 4, HD, HD)),
        "cst1": c1,
        "cst2": c2,
        "gatew": w2[:, 2304:2328].reshape(KT, P, 24).transpose(1, 0, 2),
        "w2k": w2k,
        "w2v": a["cmp_w2_v_2"][0].reshape(2, P, HD).transpose(1, 0, 2),
        "lruw": np.stack([half_pairs(a["lru_wa_2"][0]), half_pairs(a["lru_wx_2"][0])], 1),
    }
    nc = bacc.Bacc("TRN2", target_bir_lowering=False, num_devices=1)
    args = []
    feed = {}
    for name, v in arrays.items():
        feed[f"in_{name}"] = np.ascontiguousarray(v)
        args.append(nc.dram_tensor(f"in_{name}", v.shape, F32, kind="ExternalInput").ap())
    yout = nc.dram_tensor("out_y", (P, KT, S), F32, kind="ExternalOutput").ap()
    build(nc, *args, yout)
    got = run_bass_kernel_spmd(nc, [feed], core_ids=[0]).results[0]["out_y"]
    return np.ascontiguousarray(got.transpose(1, 0, 2).reshape(D, S).T)[None]
```

```python
import numpy as np
import concourse.bass as bass
from concourse import mybir
from contextlib import ExitStack

F32 = mybir.dt.float32
F32R = mybir.dt.float32r
ALU = mybir.AluOpType
ACT = mybir.ActivationFunctionType
AX = mybir.AxisListType

P = 128
S = 512
D = 1024
KT = D // P
LAYERS = 2
NT = S // P
DFF = 2816
GRP = 2 * P
NG = DFF // GRP
DFF2 = 4096
NG2 = DFF2 // GRP
HD = 64
CHUNK = 64
RET_HEADS = 8
EPS = 1e-6
SLABW = 2048
RING = 3
ADA_SLABS = 24

W_IN, W_OUT = 11, 4
MLP0 = W_IN + W_OUT
LAYER_SLABS = MLP0 + 3 * NG
B2 = LAYERS * LAYER_SLABS
RNN0 = B2 + 3
Q0 = RNN0 + 4
CMP0 = Q0 + 2
WO2 = CMP0 + 4
FF0 = WO2 + 4
SLABS = FF0 + 2 * NG2

PC_L, PC_LN = 0, 24
PC_CONV, PC_CONVN = 48, 16 * NG
PC_FINAL = PC_CONV + LAYERS * PC_CONVN
PC_C = PC_FINAL + 8
PC_ADAB = PC_C + 8
PC_PREMIX = PC_ADAB + 48
PC_POSTMIX = PC_PREMIX + 8
PC_PREMLP = PC_POSTMIX + 8
PC_POSTMLP = PC_PREMLP + 8
PC_RCONV = PC_POSTMLP + 8
PC_BA = PC_RCONV + 20
PC_BX = PC_BA + 4
PC_LAM = PC_BX + 4
PC_NRNN = PC_LAM + 4
PC_NATT = PC_NRNN + 4
PC_POS = PC_NATT + 4
PC_N = PC_POS + 32

N_CMP = 31
CMPC = 34
KKW = 16 * CMPC + 16
BANDW = 144
POOL_WINDOWS = (2, 4, 8, 16)
POS_COL = 32

C1 = {}
_at = 0
for _name, _w in (("ident", P), ("ones", P), ("head_mean", P), ("rot", P), ("cos", S), ("sin", S),
                  ("decay", RET_HEADS * S), ("band", 2 * 4 * BANDW)):
    C1[_name] = (_at, _w)
    _at += _w
C1_KEEP = 2 * P
C1_N = _at
C2 = {}
_at = 0
for _name, _w in (("dup", 2 * P), ("alibi", S), ("alibi_c", NT * 32), ("slopes", 8), ("seen", 1)):
    C2[_name] = (_at, _w)
    _at += _w
C2_N = _at


def constants():
    p = np.arange(P)
    t = np.arange(S)
    c1 = np.zeros((P, C1_N), np.float32)

    def put(table, where, name, value):
        a, w = where[name]
        table[:, a:a + w] = np.asarray(value, np.float32).reshape(P, w)

    put(c1, C1, "ident", np.eye(P))
    put(c1, C1, "ones", np.ones((P, P)))
    put(c1, C1, "head_mean", (p[:, None] // HD == p[None, :] // HD) / HD)
    rot = np.zeros((P, P))
    for m in range(P):
        if m % HD < HD // 2:
            rot[m + HD // 2, m] = -1.0
        else:
            rot[m - HD // 2, m] = 1.0
    put(c1, C1, "rot", rot)
    half = HD // 2
    inv = np.float32(10000.0) ** (-np.arange(half, dtype=np.float32) / np.float32(half))
    ang = (t.astype(np.float32)[None, :] * inv[p % half][:, None]).astype(np.float64)
    put(c1, C1, "cos", np.cos(ang))
    put(c1, C1, "sin", np.sin(ang))
    lg = np.log1p(-np.exp2(-5.0 - np.arange(RET_HEADS)))
    dist = np.abs(t[None, :] - p[:, None])
    ok = t[None, :] // CHUNK >= p[:, None] // CHUNK
    put(c1, C1, "decay", np.stack([np.where(ok, np.exp(g * dist), 0.0) * HD ** -0.5 for g in lg], 1))
    tb = np.arange(BANDW)
    band = np.zeros((P, 2, 4, BANDW))
    for first in range(2):
        for g, w in enumerate(POOL_WINDOWS):
            lag = tb[None, :] - p[:, None]
            cnt = np.minimum(tb + 1, w) if first == 0 else np.full(BANDW, w)
            band[:, first, g] = np.where((lag >= 0) & (lag < w), 1.0 / cnt[None, :], 0.0) - (lag == 0)
    put(c1, C1, "band", band)

    c2 = np.zeros((P, C2_N), np.float32)
    put(c2, C2, "dup", np.concatenate([(p[:, None] == g * HD + p[None, :] % HD) for g in range(2)], 1))
    d = p[:, None] + 384 - t[None, :]
    put(c2, C2, "alibi", np.where(d >= 0, d, 1e32))
    end = 16 * np.arange(32) + 31
    dc = (np.arange(NT) * P)[None, :, None] + p[:, None, None] - end[None, None, :]
    put(c2, C2, "alibi_c", np.where(dc >= 0, dc, 1e32))
    put(c2, C2, "slopes", np.broadcast_to(2.0 ** -(np.arange(8) + 1.0), (P, 8)))
    put(c2, C2, "seen", (p >= 31))
    return c1, c2


def build(nc, weights, ada, params, xin, wsT, bsb_in, bw_in, cst1, cst2, gatew, w2k, w2v_in, lruw, yout):
    ctx = ExitStack()
    with ctx:
        top = [16512]

        def at(name, shape, dt, offset):
            return nc.alloc_sbuf_tensor_at(name, shape, dt, offset=offset)

        def size(shape):
            return 4 * int(np.prod(shape[1:]))

        def keep(name, shape, dt=F32):
            t = at(name, shape, dt, top[0])
            top[0] += -(-size(shape) // 32) * 32
            return t

        def sem(name):
            return ctx.enter_context(nc.semaphore(name))

        x = keep("x", [P, KT, S])
        xh = keep("xh", [P, KT, S], F32R)
        xl = keep("xl", [P, KT, S], F32R)
        wh = keep("wh", [P, RING, SLABW], F32R)
        raw_at = top[0]
        raw = keep("raw", [P, RING, SLABW])
        wl = at("wl", [P, RING, SLABW], F32R, raw_at)
        prm = keep("prm", [P, PC_N])
        keep1 = keep("keep1", [P, C1_KEEP])
        mod = keep("mod", [P, 48])
        silu_c = keep("silu_c", [P, KT])
        eps = keep("eps", [P, 1])
        std = keep("std", [P, S])
        rstd = keep("rstd", [P, S])
        rtok = keep("rtok", [P, NT])
        gains = keep("gains", [P, 4, KT])
        inv_tok = keep("inv_tok", [P, 5, NT])
        lru_c = keep("lru_c", [P, 6, 4])
        ada_acc = keep("ada_acc", [P, GRP])
        arena = top[0]
        ident = keep1[:, 0:P]
        ones = keep1[:, P:2 * P]

        t1 = keep("t1", [P, C1_N - C1_KEEP])

        def c1(name):
            a, w = C1[name]
            return t1[:, a - C1_KEEP:a - C1_KEEP + w]

        head_mean, rot, cos, sin = c1("head_mean"), c1("rot"), c1("cos"), c1("sin")
        decay = c1("decay")
        band = c1("band").rearrange("p (f g t) -> p f g t", f=2, g=4)
        ws = keep("ws", [P, LAYERS * 4, P])
        bsb = keep("bsb", [P, LAYERS * 2, P])
        bw = keep("bw", [P, LAYERS * 2, P])
        bw_cur = keep("bw_cur", [P, 2, P])
        kpad = keep("kpad", [P, 2, 2, S])
        va_at = top[0]
        u = keep("u", [P, 2, S])
        va = keep("va", [P, NT, GRP])
        sqb = at("sqb", [P, 2, S], F32, va_at)
        y = at("y", [P, 4, S], F32, va_at)
        st_at = top[0]
        xb = keep("xb", [P, NT, GRP])
        pooled = keep("pooled", [P, 2, S])
        rtmp = keep("rtmp", [P, 2, S])
        sT = at("sT", [P, 2, 1280], F32, st_at)
        gsq = at("gsq", [P, 2, S], F32, st_at)
        q_at = top[0]
        q = keep("q", [P, 4, S])
        k = keep("k", [P, 4, S])
        vr = keep("vr", [P, NT, S])
        sg = keep("sg", [P, 4, S])
        ya = keep("ya", [P, 2, S])
        vcur = keep("vcur", [P, 2, NT, P])
        vss = keep("vss", [P, 3, NT])
        mix_end = top[0]
        ah = at("ah", [P, 2, 2, S], F32R, q_at)
        al = at("al", [P, 2, 2, S], F32R, q_at + 8192)
        cv = at("cv", [P, 4, S], F32, q_at + 16384)
        ab = at("ab", [P, 2, S], F32, q_at + 24576)
        upb = at("upb", [P, 4, S], F32, q_at + 28672)
        adab = at("adab", [P, 8, GRP], F32, va_at + 8192)
        assert mix_end <= 229368, mix_end

        top[0] = arena
        t2 = keep("t2", [P, C2_N])

        def c2(name):
            a, w = C2[name]
            return t2[:, a:a + w]

        dup, alibi, slopes, seen = c2("dup"), c2("alibi"), c2("slopes"), c2("seen")
        alibi_c = c2("alibi_c").rearrange("p (i c) -> p i c", c=32)
        gw = keep("gw", [P, KT, 24])
        gwh = keep("gwh", [P, KT, 24], F32R)
        gwl = keep("gwl", [P, KT, 24], F32R)
        w2kp = keep("w2kp", [P, 2, 2, P])
        w2v = keep("w2v", [P, 2, HD])
        lru = keep("lru", [P, 2, 4, P])
        hid = keep("hid", [P, 2, 2, 2, 32])
        hbias = keep("hbias", [P, 4])
        kcT = keep("kcT", [P, 32])
        vcs = keep("vcs", [32, P])
        ptc = keep("ptc", [32, S])
        gates = keep("gates", [P, NT, 24])
        soft = keep("soft", [P, 4, 18])
        cst = keep("cst", [P, 4, NT])
        kcv_at = top[0]
        kcv = keep("kcv", [P, 2, S])
        vv = keep("vv", [P, NT, GRP])
        sqb2 = at("sqb2", [P, 2, S], F32, kcv_at)
        nt2 = at("nt2", [P, 2, S], F32, kcv_at + 4096)
        ksw = keep("ksw", [P, 2, S])
        q2 = keep("q2", [P, 4, S])
        qc = keep("qc", [P, 2, S])
        gg = keep("gg", [P, 4, S])
        cx = keep("cx", [P, 4, S])
        big = top[0]
        rr = at("rr", [P, 4, S], F32, big)
        ii = at("ii", [P, 4, S], F32, big + 8192)
        mm = at("mm", [P, 4, S], F32, big + 16384)
        kkh = at("kkh", [P, 2, 2, KKW], F32R, big + 24576)
        kkl = at("kkl", [P, 2, 2, KKW], F32R, big + 24576 + size([P, 2, 2, KKW]))
        assert big + 24576 + 2 * size([P, 2, 2, KKW]) <= 229368, big
        att = at("att", [P, 4, S], F32, big)
        pb = at("pb", [P, 3, S], F32, big + 8192)
        tsl = at("tsl", [P, 2, S], F32, big + 14336)
        pt = at("pt", [P, 2, NT, S], F32, big + 18432)
        adab_tail = at("adab_tail", [P, ADA_SLABS - LAYERS * NG, KT, GRP], F32, big)
        assert big + 18432 + 16384 <= 229368, big
        ymix = at("ymix", [P, KT, S], F32, big)
        ff_at = kcv_at + 8192
        ah2 = at("ah2", [P, 3, 2, S], F32R, ff_at)
        al2 = at("al2", [P, 3, 2, S], F32R, ff_at + 12288)
        rl = at("rl", [P, 2, S], F32, ff_at + 24576)
        ab2 = at("ab2", [P, 2, S], F32, ff_at + 28672)
        assert ff_at + 32768 <= big

        ps = ctx.enter_context(nc.psum_tensor("ps", [P, 8, S], F32))

        def bank(b):
            return ps[:, b, :]

        raw_loaded = [sem(f"raw_loaded{s}") for s in range(RING)]
        hi_made = sem("hi_made")
        hi_copied = sem("hi_copied")
        slab_split = sem("slab_split")
        slab_used = sem("slab_used")
        x_loaded = [sem(f"x_loaded{i}") for i in range(2)]
        params_loaded, keep1_loaded = sem("params_loaded"), sem("keep1_loaded")
        ws_loaded = sem("ws_loaded")
        tables_loaded = sem("tables_loaded")
        eps_set = sem("eps_set")
        silu_c_ready = sem("silu_c_ready")
        lru_exp = sem("lru_exp")
        lru_step = sem("lru_step")
        sq_ready, sq_used = sem("sq_ready"), sem("sq_used")
        sq_added, sum_done = sem("sq_added"), sem("sum_done")
        std_ready, rstd_ready = sem("std_ready"), sem("rstd_ready")
        inv_step = sem("inv_step")
        diag_ready, spread_done = sem("diag_ready"), sem("spread_done")
        nt_ready, nh_ready, nl_ready = sem("nt_ready"), sem("nh_ready"), sem("nl_ready")
        bw_ready = sem("bw_ready")
        kpad_zero = sem("kpad_zero")
        ws_masked = sem("ws_masked")
        fm_evac, tm_evac = sem("fm_evac"), sem("tm_evac")
        u_ready, sg_ready = sem("u_ready"), sem("sg_ready")
        rt_done, rt_ready = sem("rt_done"), sem("rt_ready")
        vss_ready, vstd_ready, vr_ready, va_ready = sem("vss_ready"), sem("vstd_ready"), sem("vrstd_ready"), sem("va_ready")
        rot_ready, rope_part, rope_done = sem("rot_ready"), sem("rope_part"), sem("rope_done")
        sv_ready, ya_part, ya_ready = sem("sv_ready"), sem("ya_part"), sem("ya_ready")
        pool_ready, pooled_ready, yb_ready = sem("pool_ready"), sem("pooled_ready"), sem("yb_ready")
        mix_hi, mix_split = sem("mix_hi"), sem("mix_split")
        staged, s_done, sT_ready = sem("staged"), sem("s_done"), sem("sT_ready")
        pv_done, y_evac = sem("pv_done"), sem("y_evac")
        mean_ready, yc_ready, gsq_ready = sem("mean_ready"), sem("yc_ready"), sem("gsq_ready")
        var_ready, gv_ready, gr_ready, gsd_ready = sem("var_ready"), sem("gv_ready"), sem("gr_ready"), sem("gsd_ready")
        yn_ready, gm_ready = sem("yn_ready"), sem("gm_ready")
        half_done, mix_added = sem("half_done"), sem("mix_added")
        up_scaled = sem("up_scaled")
        cv_init, conv_mid, conv_done = sem("cv_init"), sem("conv_mid"), sem("conv_done")
        sil_ready, a_ready, ah_ready, act_split = sem("sil_ready"), sem("a_ready"), sem("ah_ready"), sem("act_split")
        down_done, ffn_added = sem("down_done"), sem("ffn_added")
        ada_loaded, ada_done, ada_evac = sem("ada_loaded"), sem("ada_done"), sem("ada_evac")
        ada_term, ada_summed = sem("ada_term"), sem("ada_summed")
        xf_ready = sem("xf_ready")
        tables2_loaded = sem("tables2_loaded")
        gains_ready = sem("gains_ready")
        zeroed = sem("zeroed")
        gwh_ready, gw_split = sem("gwh_ready"), sem("gw_split")
        proj2_evac = sem("proj2_evac")
        dup_ready, kkh_ready, kk_split = sem("dup_ready"), sem("kkh_ready"), sem("kk_split")
        gate_ready, gates_sig, gates_ready = sem("gate_ready"), sem("gates_sig"), sem("gates_ready")
        hbias_ready, hid_ready = sem("hbias_ready"), sem("hid_ready")
        kcv_ready, kcv_evac = sem("kcv_ready"), sem("kcv_evac")
        cx_init, cx_mid, cx_done = sem("cx_init"), sem("cx_mid"), sem("cx_done")
        lru_ready, sig_ready, th_ready, sqrt_ready = sem("lru_ready"), sem("sig_ready"), sem("th_ready"), sem("sqrt_ready")
        ix_ready = sem("ix_ready")
        decay_ready, aa_ready, uu_ready, scan_ready, rnn_ready = (sem("decay_ready"), sem("aa_ready"), sem("uu_ready"),
                                                              sem("scan_ready"), sem("rnn_ready"))
        staged2, s2_done, sc_done, exp_done, rs_ready, p_ready = (sem("staged2"), sem("s2_done"), sem("sc_done"),
                                                                 sem("exp_done"), sem("rs_ready"), sem("p_ready"))
        cmp_step = sem("cmp_step")
        t_done, pt_evac, values_used, att_evac = sem("t_done"), sem("pt_evac"), sem("values_used"), sem("att_evac")
        sq4_ready, sq4_used, std4_ready, rstd4_ready = sem("sq4_ready"), sem("sq4_used"), sem("std4_ready"), sem("rstd4_ready")
        nt4_ready, nh4_ready, nl4_ready = sem("nt4_ready"), sem("nh4_ready"), sem("nl4_ready")
        y_ready = sem("y_ready")
        pn_ready, x2_ready = sem("pn_ready"), sem("x2_ready")
        y_zero = sem("y_zero")
        rl_ready, ab_ready, ah2_ready, act2_split = sem("rl_ready"), sem("ab_ready"), sem("ah2_ready"), sem("act2_split")
        down2_done, y2_added = sem("down2_done"), sem("y2_added")
        stored = sem("stored")

        block = ctx.enter_context(nc.Block())

        tensor_counts = (ada_done, pv_done, pv_done, pv_done, t_done, s2_done, values_used, values_used, values_used)
        scalar_counts = (y_evac, y_evac, pt_evac, att_evac, rl_ready, ah2_ready)
        vector_counts = (ada_evac, gv_ready, ada_summed, up_scaled, conv_done, ffn_added, sc_done, a_ready, act_split, y2_added, act2_split, ab_ready)

        def past(eng, s, n):
            eng.wait_ge(s, n + 1)

        def col(i, n=1):
            return prm[:, i:i + n] if isinstance(i, int) else prm[:, bass.ds(i, n)]

        def cols(t, i, n):
            return t[:, i:i + n] if isinstance(i, int) else t[:, bass.ds(i, n)]

        q_f, D_f = q[:, :, :].rearrange("p a b -> p (a b)"), decay
        k_f, y_f = k[:, :, :].rearrange("p a b -> p (a b)"), y[:, :, :].rearrange("p a b -> p (a b)")
        q2_f, att_f = q2[:, :, :].rearrange("p a b -> p (a b)"), att[:, :, :].rearrange("p a b -> p (a b)")
        ya_f = ya[:, :, :].rearrange("p a b -> p (a b)")
        bsb_f = bsb[:, :, :].rearrange("p a b -> p (a b)")
        ws_f = ws[:, :, :].rearrange("p a b -> p (a b)")
        bw_f = bw[:, :, :].rearrange("p a b -> p (a b)")
        turn_order = (0, 2, 1, 3)
        soffs = [0, 512, 896, 1152]
        sbank = [(0, 0), (1, 0), (2, 0), (1, 384)]

        @block.sync
        def _(sp):
            def load(n, s):
                sp.wait_ge(slab_used, n + 1)
                sp.dma_start(raw[:, s, :], cols_dram(n)).then_inc(raw_loaded[s], 16)

            def cols_dram(n):
                return weights[n, :, :] if isinstance(n, int) else weights[bass.ds(n, 1), :, :].rearrange("a p c -> p (a c)")

            load(0, 0)
            for i in range(2):
                f = slice(i * KT // 2, (i + 1) * KT // 2)
                sp.dma_start(x[:, f, :], xin[:, f, :]).then_inc(x_loaded[i], 16)
            load(1, 1)
            sp.dma_start(ws[:, :, :], wsT).then_inc(ws_loaded, 16)
            load(2, 2)
            with sp.Fori(1, SLABS // RING) as i:
                for s in range(RING):
                    load(i * RING + s, s)
            for n in range(SLABS // RING * RING, SLABS):
                load(n, n % RING)
            for i in range(KT):
                sp.wait_ge(x2_ready, KT + i + 1)
                sp.dma_start(yout[:, i, :], x[:, i, :]).then_inc(stored, 16)
            sp.wait_ge(stored, 16 * KT)

        @block.gpsimd
        def _(pool):
            pool.memset(kpad[:, :, :, :], 0.0).then_inc(kpad_zero, 1)

            def low(n, s):
                pool.wait_ge(hi_made, n + 1)
                pool.tensor_tensor(wl[:, s, :], raw[:, s, :], wh[:, s, :].bitcast(F32), ALU.subtract).then_inc(slab_split, 1)

            low(0, 0)
            pool.wait_ge(raw_loaded[1], 16)
            pool.tensor_copy(wh[:, 1, :], raw[:, 1, :]).then_inc(hi_copied, 1)
            pool.wait_ge(hi_copied, 1)
            pool.sem_inc(hi_made, 1)
            low(1, 1)
            low(2, 2)
            with pool.Fori(1, SLABS // RING) as i:
                for s in range(RING):
                    low(i * RING + s, s)
            for n in range(SLABS // RING * RING, SLABS):
                low(n, n % RING)

        @block.tensor
        def _(pe):
            pe.sem_inc(slab_used, RING)
            for s in tensor_counts:
                pe.sem_inc(s, 1)

            def product(out, w_hi, w_lo, m_hi, m_lo, start, stop):
                pe.matmul(out, w_hi, m_hi, start=start, stop=False)
                pe.matmul(out, w_hi, m_lo, start=False, stop=False)
                return pe.matmul(out, w_lo, m_hi, start=False, stop=stop)

            def slab_fm(n, s, b0, fresh=None, half=None, kts=tuple(range(KT)), start=True, stop=True):
                pe.wait_ge(slab_split, n + 1)
                order = [(m, i) for m in range(2) for i in range(len(kts))]
                if fresh is not None:
                    order.sort(key=lambda o: o[1])
                for m, i in order:
                    if fresh is not None and m == 0:
                        pe.wait_ge(fresh[0], fresh[1] + i + 1)
                    kt = kts[i]
                    w = slice(kt * GRP + m * P, kt * GRP + m * P + P)
                    last = product(bank(b0 + m), wh[:, s, w], wl[:, s, w], xh[:, kt, :], xl[:, kt, :],
                                   start and i == 0, stop and i == len(kts) - 1)
                    if half is not None and m == 0 and i == len(kts) - 1:
                        last.then_inc(half, 1)
                if stop:
                    last.then_inc(slab_used, 1)

            def slab_tm(n, s, b0):
                pe.wait_ge(slab_split, n + 1)
                for i in range(NT):
                    out = ps[:, b0 + i // 2, (i % 2) * GRP:(i % 2 + 1) * GRP]
                    tok = slice(i * P, (i + 1) * P)
                    for kt in range(KT):
                        w = slice(kt * GRP, (kt + 1) * GRP)
                        last = product(out, xh[:, kt, tok], xl[:, kt, tok], wh[:, s, w], wl[:, s, w], kt == 0, kt == KT - 1)
                last.then_inc(slab_used, 1)

            def token_sums(squares, start, stop, b=7):
                for t in range(NT):
                    last = pe.matmul(ps[:, b, t:t + 1], squares[:, t * P:(t + 1) * P], ones[:, 0:1], start=start and t == 0,
                                     stop=stop and t == NT - 1)
                return last

            def sum_squares(nk, buf):
                for i in range(KT):
                    pe.wait_ge(sq_ready, nk * KT + i + 1)
                    pe.matmul(bank(7), ones, buf[:, i % 2, :], start=(i == 0), stop=(i == KT - 1)).then_inc(sq_used, 1)

            def sum_added_tokens(nk, th, buf, added=std, b=7):
                pe.wait_ge(sq_added, th * (KT - 2) + (KT - 2))
                token_sums(added, True, False, b)
                pe.wait_ge(sq_ready, nk * KT + KT)
                token_sums(buf[:, 1, :], False, True, b).then_inc(sum_done, 1)

            def spread(k):
                pe.wait_ge(diag_ready, k + 1)
                pe.matmul(bank(6), ones, rstd[:, :], start=True, stop=True).then_inc(spread_done, 1)

            def sum_added(nk, th, buf):
                pe.wait_ge(sq_added, th * (KT - 2) + (KT - 2))
                pe.matmul(bank(7), ones, std[:, :], start=True, stop=False)
                pe.wait_ge(sq_ready, nk * KT + KT)
                pe.matmul(bank(7), ones, buf[:, 1, :], start=False, stop=True).then_inc(sum_done, 1)

            def ada_part(a):
                past(pe, ada_summed, a + 1)
                past(pe, ada_evac, a)
                for m in range(2):
                    last = pe.matmul(ps[:, 7, m:m + 1], ada_acc[:, m * P:(m + 1) * P], ones[:, 0:1], start=True, stop=True)
                last.then_inc(ada_done, 1)

            fm_slabs, tm_slabs = (0, 3, 4, 5, 6, 9, 10), (1, 2, 7, 8)
            pe.wait_ge(keep1_loaded, 16)
            with pe.Fori(0, LAYERS) as l:
                n0 = l * LAYER_SLABS
                def evacuated(c):
                    if c in fm_slabs:
                        pe.wait_ge(fm_evac, l * len(fm_slabs) + fm_slabs.index(c) + 1)
                    else:
                        pe.wait_ge(tm_evac, l * len(tm_slabs) + tm_slabs.index(c) + 1)

                for c in range(W_IN):
                    if c >= 2:
                        evacuated(c - 2)
                    if c in fm_slabs:
                        slab_fm(n0 + c, c % RING, 2 * (c % 2), fresh=(nl_ready, l * 2 * KT) if c == 0 else None)
                    else:
                        slab_tm(n0 + c, c % RING, 2 * (c % 2))
                    if c == 0:
                        past(pe, ada_evac, l * NG)
                        sum_added(l * 2, l * 2, sqb)
                    if c == 1:
                        pe.wait_ge(rstd_ready, l * 2 + 1)
                        for i in range(NT):
                            last = pe.matmul(ps[:, 7, i:i + 1], rstd[:, i * P:(i + 1) * P], ident[:, 0:1], start=True, stop=True)
                        last.then_inc(rt_done, 1)
                    if c in (5, 7):
                        src, o = (q, 0) if c == 5 else (k, 4)
                        pe.wait_ge(tables_loaded, 16 * 3)
                        evacuated(4 if c == 5 else 6)
                        pe.wait_ge(rt_ready, l + 1)
                        for i in range(4):
                            if o:
                                pe.wait_ge(rope_part, l * 8 + i + 1)
                            pe.matmul(bank(4 + i), rot, src[:, i, :], start=True, stop=True).then_inc(rot_ready, 1)
                pe.wait_ge(va_ready, l + 1)
                pe.wait_ge(rope_part, l * 8 + 8)
                for i in range(NT):
                    for j in range(2):
                        last = pe.matmul(ps[:, 4 + i, j * 256:(j + 1) * 256], va[:, i, j * P:(j + 1) * P],
                                         cols(ws_f, l * 512 + j * 256, 256), start=True, stop=True)
                last.then_inc(sv_ready, 1)
                evacuated(W_IN - 3)
                evacuated(W_IN - 1)
                for g in range(4):
                    pair = slice((g // 2) * P, (g // 2 + 1) * P)
                    for j in range(NT):
                        pe.matmul(ps[:, g, j * P:(j + 1) * P], xb[:, j, pair], band[:, min(j, 1), g, 0:P], start=(j == 0), stop=False)
                    for j in range(NT - 1):
                        last = pe.matmul(ps[:, g, (j + 1) * P:(j + 1) * P + BANDW - P], xb[:, j, pair], band[:, 1, g, P:BANDW],
                                         start=False, stop=(j == NT - 2))
                    last.then_inc(pool_ready, 1)
                pe.wait_ge(bw_ready, l + 1)
                pe.wait_ge(ya_ready, l * 2 + 2)
                pe.wait_ge(pooled_ready, l * 4 + 4)
                for j in range(2):
                    pe.matmul(bank(4 + j), bw_cur[:, j, :], pooled[:, j, :], start=True, stop=True).then_inc(yb_ready, 1)
                with pe.Fori(0, 2) as it:
                    def ret_scores(p, hh):
                        if hh == 0:
                            pe.wait_ge(staged, l * 4 + it * 2 + p + 1)
                        for j in range(NT):
                            b, o = sbank[j]
                            w = S - j * P
                            last = pe.matmul(ps[:, 3 * hh + b, o:o + w], kpad[:, p, hh, j * P:(j + 1) * P],
                                             cols(q_f, it * (2 * S) + (p * S + j * P), w), start=True, stop=True)
                        last.then_inc(s_done, 1)

                    def ret_values(p, hh):
                        head = l * 8 + it * 4 + (2 * p + hh)
                        pe.wait_ge(sT_ready, head + 1)
                        pe.wait_ge(y_evac, head + 1)
                        for j in range(NT):
                            w = S - j * P
                            last = pe.matmul(ps[:, 6 + hh, j * P:S], vcur[:, p, j, :], sT[:, hh, soffs[j]:soffs[j] + w],
                                             start=(j == 0), stop=(j == NT - 1))
                        last.then_inc(pv_done, 1)

                    ret_scores(0, 0)
                    pe.wait_ge(mix_split, l * 8 + 4)
                    past(pe, gv_ready, l * 4 + it)
                    ret_scores(0, 1)
                    ret_values(0, 0)
                    ret_scores(1, 0)
                    ret_values(0, 1)
                    ret_scores(1, 1)
                    ret_values(1, 0)
                    pe.wait_ge(y_evac, l * 8 + it * 4 + 4)
                    pe.matmul(bank(2), head_mean, y_f[:, bass.ds(it * (2 * S), S)], start=True, stop=True).then_inc(mean_ready, 1)
                    ret_values(1, 1)
                    pe.wait_ge(gsq_ready, l * 4 + it + 1)
                    pe.matmul(bank(5), head_mean, ya_f[:, bass.ds(it * S, S)], start=True, stop=True).then_inc(var_ready, 1)
                past(pe, gv_ready, l * 4 + 2)
                for t in range(2):
                    pe.wait_ge(y_evac, l * 8 + 4 * t + 6)
                    pe.matmul(bank(4 + t), head_mean, y[:, 2 * t + 1, :], start=True, stop=True).then_inc(mean_ready, 1)
                others, turned = (0, 1, 2, 3), tuple(4 + i for i in turn_order)
                bank0 = [2 * ((W_IN + w) % 2) for w in range(W_OUT)]
                pe.wait_ge(mix_split, l * 8 + 4)
                slab_fm(n0 + W_IN, W_IN % RING, bank0[0], kts=others, stop=False)
                for t in range(2):
                    pe.wait_ge(gsq_ready, l * 4 + t + 3)
                    pe.matmul(bank(6 + t), head_mean, gsq[:, t, :], start=True, stop=True).then_inc(var_ready, 1)
                slab_fm(n0 + W_IN + 1, (W_IN + 1) % RING, bank0[1], kts=others, stop=False)
                for w in range(2):
                    slab_fm(n0 + W_IN + w, (W_IN + w) % RING, bank0[w], fresh=(mix_split, l * 8 + 4), kts=turned[:2], start=False,
                            stop=False)
                for w in range(2):
                    slab_fm(n0 + W_IN + w, (W_IN + w) % RING, bank0[w], fresh=(mix_split, l * 8 + 6), half=half_done,
                            kts=turned[2:], start=False)
                for w in range(2, W_OUT):
                    pe.wait_ge(mix_added, l * KT + 2 * (w - 1))
                    slab_fm(n0 + W_IN + w, (W_IN + w) % RING, bank0[w], half=half_done)

                def up(j, n, s, fresh=None):
                    past(pe, up_scaled, l * 4 * NG + j * 4)
                    slab_fm(n, s, 0, fresh)
                    if fresh is not None:
                        sum_added(l * 2 + 1, l * 2 + 1, sqb)
                    slab_fm(n + 1, (s + 1) % RING, 2)

                def down(j, par, n, s):
                    past(pe, act_split, l * 2 * NG + j * 2 + 2)
                    pe.wait_ge(slab_split, n + 1)
                    past(pe, ffn_added, l * 8 * NG + j * 8)
                    for o in range(KT):
                        if o >= 3:
                            past(pe, ffn_added, l * 8 * NG + j * 8 + o - 2)
                        for kt in range(2):
                            w = slice(kt * D + o * P, kt * D + o * P + P)
                            last = product(bank(4 + o % 3), wh[:, s, w], wl[:, s, w], ah[:, par, kt, :], al[:, par, kt, :],
                                           kt == 0, kt == 1)
                        last.then_inc(down_done if o < KT - 1 else slab_used, 1)

                up(0, n0 + MLP0, MLP0 % RING, fresh=(nl_ready, l * 2 * KT + KT))
                pe.wait_ge(std_ready, l * 2 + 2)
                ada_part(l * NG)
                with pe.Fori(0, (NG - 1) // 2) as it:
                    for v in range(2):
                        j = it * 2 + (1 + v)
                        n = n0 + it * 6 + (MLP0 + 2 + 3 * v)
                        up(j, n, (MLP0 + 2) % RING)
                        down(it * 2 + v, v, n + 2, (MLP0 + 4) % RING)
                        ada_part(l * NG + j)
                down(NG - 1, 0, n0 + (LAYER_SLABS - 1), (LAYER_SLABS - 1) % RING)

            past(pe, ada_evac, LAYERS * NG)
            sum_added_tokens(4, 4, sqb)
            sum_added_tokens(5, 5, sqb2, added=rstd, b=6)
            spread(0)
            pe.wait_ge(tables2_loaded, 16 * 5)
            evacs = (None, None, 1, 2, 3, None, None, 4, 5)
            for c in range(CMP0 - B2):
                n = B2 + c
                if evacs[c]:
                    pe.wait_ge(proj2_evac, evacs[c])
                if c in (5, 6):
                    pe.wait_ge(cx_done, 2 * (c - 4))
                if c == 2:
                    slab_tm(n, n % RING, 2 * (c % 2))
                else:
                    slab_fm(n, n % RING, 2 * (c % 2), fresh=(nl_ready, 4 * KT) if c == 0 else None)
                if c == 0:
                    spread(1)
                if c in (1, 2):
                    ada_part(LAYERS * NG + c - 1)
                if c == 2:
                    for kv in range(2):
                        for g in range(2):
                            if kv == 1 and g == 1:
                                past(pe, ada_evac, ADA_SLABS)
                            pe.matmul(bank(4 + 2 * kv + g), dup[:, g * P:(g + 1) * P], kcv[:, kv, :], start=True,
                                      stop=True).then_inc(dup_ready, 1)
                if c in (5, 6):
                    pe.wait_ge(cx_done, 4)
                    for i in range(4):
                        if c == 5:
                            pe.wait_ge(kk_split, i + 1)
                        else:
                            pe.wait_ge(sig_ready, i + 1)
                        pe.matmul(bank(4 + i), lru[:, c - 5, i, :], cx[:, i, :], start=True, stop=True).then_inc(lru_ready, 1)
            pe.wait_ge(gw_split, 1)
            pe.wait_ge(zeroed, 1)
            pe.wait_ge(sig_ready, 5)
            for i in range(NT):
                tok = slice(i * P, (i + 1) * P)
                for kt in range(KT):
                    last = product(ps[:, 4, i * 24:(i + 1) * 24], xh[:, kt, tok], xl[:, kt, tok], gwh[:, kt, :], gwl[:, kt, :],
                                   kt == 0, kt == KT - 1)
            last.then_inc(gate_ready, 1)
            pe.wait_ge(proj2_evac, 6)
            pe.wait_ge(sig_ready, 8)
            for kv in range(2):
                for part in range(2):
                    n = CMP0 + 2 * kv + part
                    s = n % RING
                    pe.wait_ge(slab_split, n + 1)
                    for a8 in range(8):
                        a = part * 8 + a8
                        mh = kkh[:, kv, :, 2 * a:2 * a + 16 * (CMPC - 1) + 1:16]
                        ml = kkl[:, kv, :, 2 * a:2 * a + 16 * (CMPC - 1) + 1:16]
                        for m in range(2):
                            w = slice(a8 * GRP + m * P, a8 * GRP + m * P + P)
                            out = ps[:, 2 + 4 * kv + m, 0:2 * CMPC].rearrange("p (g c) -> p g c", g=2)
                            last = product(out, wh[:, s, w], wl[:, s, w], mh, ml, a == 0, a == 15)
                    last.then_inc(slab_used, 1)
                    if kv == 0 and part == 0:
                        pe.wait_ge(proj2_evac, 7)
                        for i in range(4):
                            pe.wait_ge(sq4_ready, i + 1)
                            pe.matmul(bank(0), ones, rr[:, i, :], start=(i == 0), stop=(i == 3)).then_inc(sq4_used, 1)
            pe.wait_ge(gates_sig, 1)
            pe.wait_ge(hid_ready, 4)
            for m in range(2):
                for g in range(2):
                    last = pe.matmul(ps[:, 4, 0:N_CMP], w2kp[:, m, g, :], hid[:, 0, m, g, 0:N_CMP],
                                     start=(m == 0 and g == 0), stop=(m == 1 and g == 1))
            last.then_inc(kcv_ready, 1)
            pe.wait_ge(hid_ready, 8)
            for g in range(2):
                for m in range(2):
                    last = pe.matmul(ps[0:N_CMP, 5, g * HD:(g + 1) * HD], hid[:, 1, m, g, 0:N_CMP], w2v[:, m, :],
                                     start=(m == 0), stop=(m == 1))
            last.then_inc(kcv_ready, 1)
            pe.wait_ge(kcv_evac, 2)
            pe.wait_ge(std4_ready, 1)

            def attend(r, first, last_turn):
                def scores(U):
                    g, v = U % 18 // 9, U % 9
                    past(pe, sc_done, r * 18 + U - 2 if U >= 3 or not first else 0)
                    if v < 8:
                        i = v % 4
                        w = (i + 1) * P
                        pe.matmul(ps[:, U % 3, 0:w], qc[:, g, i * P:(i + 1) * P], ksw[:, v // 4, 0:w], start=True,
                                  stop=True).then_inc(s2_done, 1)
                    else:
                        for i in range(NT):
                            last = pe.matmul(ps[:, U % 3, i * 32:i * 32 + N_CMP], qc[:, g, i * P:(i + 1) * P], kcT[:, 0:N_CMP],
                                             start=True, stop=True)
                        last.then_inc(s2_done, 1)

                def turn(U):
                    v = U % 9
                    pe.wait_ge(p_ready, r * 18 + U + 1)
                    past(pe, pt_evac, r * 18 + U - 2 if U >= 3 or not first else 0)
                    if v < 8:
                        for j in range(v % 4 + 1):
                            last = pe.transpose(ps[:, 3 + U % 3, j * P:(j + 1) * P], pb[:, U % 3, j * P:(j + 1) * P], ident)
                    else:
                        for i in range(NT):
                            last = pe.transpose(ps[0:N_CMP, 3 + U % 3, i * P:(i + 1) * P], pb[:, U % 3, i * 32:i * 32 + N_CMP],
                                                ident)
                    last.then_inc(t_done, 1)

                if not first:
                    for U, js in ((0, (0,)), (1, (1,)), (2, (2, 3))):
                        plan[U] = (1, 1, js)
                    plan[3] = (1, 2, ())

                if first:
                    pe.wait_ge(staged2, 1)
                    scores(0)
                    scores(1)
                for U in range(18):
                    if U + 2 < 18 or not last_turn:
                        if U + 2 in (9, 18):
                            pe.wait_ge(staged2, 2 * r + (U + 2) // 9 + 1)
                        scores(U + 2)
                    if U in plan:
                        values(r if U > 3 else r - 1, *plan[U])
                    turn(U)

            def values(r, g, part, js):
                past(pe, pt_evac, r * 18 + (9 * g + 4 * part + 4 if part < 2 else 9 * g + 9))
                if part == 0:
                    past(pe, att_evac, max(0, r * 2 + g - 1) if isinstance(r, int) else r * 2 + g - 1)
                for j in js:
                    last = pe.matmul(ps[:, 6 + g, j * P:S], vv[:, j, part * P:(part + 1) * P], pt[:, part, j, j * P:S],
                                     start=(part == 0 and j == 0), stop=False)
                if part == 2:
                    last = pe.matmul(bank(6 + g), vcs[0:N_CMP, :], ptc[0:N_CMP, :], start=False, stop=True)
                if part == 2 or 3 in js:
                    last.then_inc(values_used, 1)

            plan = {5: (0, 0, (0,)), 6: (0, 0, (1,)), 7: (0, 0, (2, 3)),
                    9: (0, 1, (0,)), 10: (0, 1, (1,)), 11: (0, 1, (2, 3)), 12: (0, 2, ()),
                    14: (1, 0, (0,)), 15: (1, 0, (1,)), 16: (1, 0, (2, 3))}
            attend(0, True, False)
            with pe.Fori(1, 3) as r:
                attend(r, False, False)
            attend(3, False, True)
            values(3, 1, 1, (0, 1, 2, 3))
            values(3, 1, 2, ())

            pe.wait_ge(nl4_ready, 4)
            slab_fm(WO2, WO2 % RING, 0, kts=(0, 1), stop=False)
            past(pe, att_evac, 8)
            for i in range(4):
                pe.wait_ge(sq4_ready, 4 + i + 1)
                pe.matmul(bank(7), ones, sqb2[:, i % 2, :], start=(i == 0), stop=(i == 3)).then_inc(sq4_used, 1)
            slab_fm(WO2, WO2 % RING, 0, kts=(2, 3), start=False, stop=False)
            slab_fm(WO2 + 1, (WO2 + 1) % RING, 2, kts=(0, 1, 2, 3), stop=False)
            for w in range(2):
                slab_fm(WO2 + w, (WO2 + w) % RING, 2 * w, fresh=(nl4_ready, 4), kts=(4, 5, 6, 7), start=False)
            for w in range(2, 4):
                pe.wait_ge(y_ready, 2 * (w - 1))
                slab_fm(WO2 + w, (WO2 + w) % RING, 2 * (w % 2))
            sum_added_tokens(6, 6, sqb2)
            spread(2)
            sum_squares(7, sqb2)

            def up2(g, n, s, fresh=None):
                past(pe, rl_ready, g * 2)
                slab_fm(n, s, 0, fresh)

            def down2(g, par, n, s):
                past(pe, act2_split, g * 2 + 2)
                pe.wait_ge(slab_split, n + 1)
                past(pe, y2_added, g * 8)
                for o in range(KT):
                    if o >= 4:
                        past(pe, y2_added, g * 8 + o - 3)
                    for kt in range(2):
                        w = slice(kt * D + o * P, kt * D + o * P + P)
                        last = product(bank(2 + o % 4), wh[:, s, w], wl[:, s, w], ah2[:, par, kt, :], al2[:, par, kt, :],
                                       kt == 0, kt == 1)
                    last.then_inc(down2_done if o < KT - 1 else slab_used, 1)

            up2(0, FF0, FF0 % RING, fresh=(nl_ready, 5 * KT))
            with pe.Fori(0, (NG2 - 1) // 3) as it:
                for v in range(3):
                    n = it * 6 + (FF0 + 1 + 2 * v)
                    up2(it * 3 + (1 + v), n, (FF0 + 1 + 2 * v) % RING)
                    down2(it * 3 + v, v, n + 1, (FF0 + 2 + 2 * v) % RING)
            down2(NG2 - 1, (NG2 - 1) % 3, SLABS - 1, (SLABS - 1) % RING)
            sum_added_tokens(8, 7, sqb2)
            spread(3)

        @block.scalar
        def _(act):
            for s in scalar_counts:
                act.sem_inc(s, 1)
            act.dma_start(prm[:, :], params).then_inc(params_loaded, 16)
            act.dma_start(keep1[:, :], cst1[:, 0:C1_KEEP]).then_inc(keep1_loaded, 16)

            def high(n, s, third):
                act.wait_ge(raw_loaded[s], third * 16 + 16)
                act.activation(wh[:, s, :], raw[:, s, :], ACT.Copy).then_inc(hi_made, 1)

            def used(n):
                act.wait_ge(slab_used, n + 1 + RING)

            def ahead(c, base, thirds):
                high(base + c + RING, (c + RING) % RING, thirds + (c + RING) // RING)

            def square(nk, i, buf, src, alone=None, th=None, gain=1.0):
                if i >= 2 and alone is not None:
                    act.wait_ge(sq_used, alone * KT + i - 1)
                elif i >= 2:
                    act.wait_ge(sq_added, th * (KT - 2) + max(1, i - 2))
                act.activation(buf[:, i % 2, :], src[:, i, :], ACT.Square, scale=gain).then_inc(sq_ready, 1)

            def root(th=None):
                if th is None:
                    act.wait_ge(sq_used, KT)
                else:
                    act.wait_ge(sum_done, th + 1)
                act.activation(std[:, :], bank(7), ACT.Sqrt, bias=eps[:, :], scale=1.0 / D).then_inc(std_ready, 1)

            def root_tokens(th):
                act.wait_ge(sum_done, th + 1)
                act.activation(inv_tok[:, 0, :], ps[:, 7, 0:NT], ACT.Sqrt, bias=eps[:, :], scale=1.0 / D).then_inc(std_ready, 1)

            def highs(sk, buf, shift):
                for i in range(KT):
                    act.wait_ge(nt_ready, (sk - 2 * LAYERS) * KT + i + 1)
                    act.activation(xh[:, i, :], buf[:, i % 2, :], ACT.Identity, bias=mod[:, shift + i:shift + i + 1])\
                       .then_inc(nh_ready, 1)

            def high_x(i, gain):
                act.activation(xh[:, i, :], x[:, i, :], ACT.Copy, scale=gain).then_inc(nh_ready, 1)

            act.wait_ge(params_loaded, 16)
            act.activation(silu_c[:, :], col(PC_C, KT), ACT.Silu).then_inc(silu_c_ready, 1)
            act.wait_ge(lru_step, 1)
            act.activation(lru_c[:, 1, :], lru_c[:, 0, :], ACT.Exp, scale=-1.0).then_inc(lru_exp, 1)
            act.wait_ge(eps_set, 1)
            high(0, 0, 0)
            for i in range(KT):
                if i % (KT // 2) == 0:
                    act.wait_ge(x_loaded[i // (KT // 2)], 16)
                square(0, i, sqb, x, th=0)
            for dst, src in ((t1[:, :], cst1[:, C1_KEEP:C1_N]), (bsb[:, :, :], bsb_in), (bw[:, :, :], bw_in)):
                act.dma_start(dst, src).then_inc(tables_loaded, 16)

            with act.Fori(0, LAYERS) as l:
                n0 = l * LAYER_SLABS
                n3 = l * (LAYER_SLABS // RING)
                for i in range(KT):
                    high_x(i, col(l * PC_LN + (PC_L + i)))
                high(n0 + 2, 2, n3)
                root(th=l * 2)

                def stage_pair(it, p):
                    act.wait_ge(pv_done, l * 8 + (it * 4 + 2 * p + 1))
                    for hh in range(2):
                        h = slice(HD * hh, HD * hh + HD)
                        act.activation(kpad[h, p, hh, :], k[h, 2 * it + p, :], ACT.Copy)
                    act.activation(vcur[:, p, :, :], vr[:, :, (2 * it + p) * P:(2 * it + p + 1) * P], ACT.Copy).then_inc(staged, 1)

                for c in range(W_IN):
                    used(n0 + c)
                    b0 = 2 * (c % 2)
                    if c == 0:
                        act.wait_ge(fm_evac, l * 7 + 1)
                        for m in range(2):
                            last = act.activation(u[:, m, :], u[:, m, :], ACT.Gelu_apprx_tanh)
                        last.then_inc(u_ready, 1)
                    if c == 1:
                        act.wait_ge(rt_done, l + 1)
                        act.activation(rtok[:, :], ps[:, 7, 0:NT], ACT.Copy).then_inc(rt_ready, 1)
                        act.wait_ge(rt_ready, l + 1)
                    if c in (1, 2, 7, 8):
                        for i in range(NT):
                            src = ps[:, b0 + i // 2, (i % 2) * GRP:(i % 2 + 1) * GRP]
                            dst = va[:, i, :] if c == 1 else xb[:, i, :] if c == 2 else vr[:, i, (c - 7) * GRP:(c - 6) * GRP]
                            last = act.activation(dst, src, ACT.Gelu_apprx_tanh if c == 1 else ACT.Copy, scale=rtok[:, i:i + 1])
                        last.then_inc(tm_evac, 1)
                    if c in (9, 10):
                        act.wait_ge(fm_evac, l * 7 + c - 3)
                        for i in (2 * (c - 9), 2 * (c - 9) + 1):
                            act.activation(sg[:, i, :], sg[:, i, :], ACT.Silu).then_inc(sg_ready, 1)
                    if c == 1:
                        act.wait_ge(tm_evac, l * 4 + 1)
                        for i in range(NT):
                            last = act.activation(ya[:, i // 2, (i % 2) * GRP:(i % 2 + 1) * GRP], va[:, i, :], ACT.Square, accum_out=vss[:, 0, i:i + 1])
                        last.then_inc(vss_ready, 1)
                        act.wait_ge(vss_ready, l + 1)
                        act.activation(vss[:, 1, :], vss[:, 0, :], ACT.Sqrt, bias=eps[:, :], scale=1.0 / GRP).then_inc(vstd_ready, 1)
                    ahead(c, n0, n3)
                    if c == 9:
                        act.wait_ge(kpad_zero, 1)
                        act.wait_ge(rope_done, l * 8 + 8)
                        for p in range(2):
                            stage_pair(0, p)
                act.wait_ge(tables_loaded, 16 * 3)
                act.activation(bw_cur[:, :, :].rearrange("p a b -> p (a b)"), cols(bw_f, l * 256, 256), ACT.Copy).then_inc(bw_ready, 1)
                for g in range(4):
                    act.wait_ge(pool_ready, l * 4 + g + 1)
                    h = slice(HD * (g % 2), HD * (g % 2) + HD)
                    act.activation(pooled[h, g // 2, :], ps[h, g, :], ACT.Copy).then_inc(pooled_ready, 1)
                for j in range(2):
                    act.wait_ge(ya_ready, l * 2 + j + 1)
                    act.activation(xh[:, j, :], ya[:, j, :], ACT.Copy).then_inc(mix_hi, 1)
                for j in range(2):
                    act.wait_ge(yb_ready, l * 2 + j + 1)
                    act.activation(xh[:, 2 + j, :], bank(4 + j), ACT.Copy, scale=col(l * PC_LN + (PC_L + 10 + j))).then_inc(mix_hi, 1)
                for it in range(2):
                    for p in range(2):
                        for hh in range(2):
                            h = slice(HD * hh, HD * hh + HD)
                            act.wait_ge(pv_done, l * 8 + (it * 4 + 2 * p + hh + 4))
                            act.activation(y[h, 2 * it + p, :], ps[h, 6 + hh, :], ACT.Copy).then_inc(y_evac, 1)
                        if it == 0:
                            stage_pair(1, p)
                for t in range(2):
                    act.wait_ge(gr_ready, l * 4 + t + 1)
                    act.activation(ya[:, t, :], ya[:, t, :], ACT.Sqrt).then_inc(gsd_ready, 1)
                for t in range(2):
                    act.wait_ge(yc_ready, l * 4 + t + 3)
                    act.activation(gsq[:, t, :], y[:, 2 * t + 1, :], ACT.Square).then_inc(gsq_ready, 1)
                for turn, i in enumerate(turn_order):
                    if turn == 2:
                        for t in range(2):
                            act.wait_ge(gr_ready, l * 4 + t + 3)
                            act.activation(gsq[:, t, :], gsq[:, t, :], ACT.Sqrt).then_inc(gsd_ready, 1)
                    act.wait_ge(gm_ready, l * 4 + turn + 1)
                    act.activation(xh[:, 4 + i, :], y[:, i, :], ACT.Copy).then_inc(mix_hi, 1)

                def ada_load(a):
                    past(act, ada_summed, a)
                    act.dma_start(adab[:, :, :].rearrange("p k c -> p (k c)"),
                                  ada[bass.ds(a, 1), :, :].rearrange("a p c -> p (a c)")).then_inc(ada_loaded, 16)

                ada_load(l * NG)
                for i in range(KT):
                    if i == KT - 1:
                        used(n0 + MLP0 - 1)
                        for t in range(2):
                            high_x(t, col(l * PC_LN + (PC_L + 16 + t)))
                    act.wait_ge(mix_added, l * KT + i + 1)
                    square(l * 2 + 1, i, sqb, x, th=l * 2 + 1)
                    if i % 2 and i < KT - 1:
                        used(n0 + W_IN + i // 2)
                        ahead(W_IN + i // 2, n0, n3)
                for t in range(2, KT):
                    high_x(t, col(l * PC_LN + (PC_L + 16 + t)))
                ahead(MLP0 - 1, n0, n3)
                root(th=l * 2 + 1)

                def conv_tap(r, j):
                    c = l * PC_CONVN + j * 16 + (PC_CONV + r * 4)
                    past(act, up_scaled, l * 4 * NG + j * 4 + r + 1)
                    act.activation(cv[:, r, :], upb[:, r, :], ACT.Identity, bias=col(c + 3), scale=col(c + 2)).then_inc(cv_init, 1)

                def mlp_step(j, base, thirds, c, par):
                    used(base + c)
                    for r in range(2):
                        conv_tap(r, j)
                    ahead(c, base, thirds)
                    past(act, conv_done, l * 4 * NG + j * 4 + 2)
                    for r in range(2):
                        act.activation(cv[:, r, :], cv[:, r, :], ACT.Silu).then_inc(sil_ready, 1)
                    used(base + c + 1)
                    for r in range(2, 4):
                        conv_tap(r, j)
                    ahead(c + 1, base, thirds)
                    for r in range(2):
                        past(act, a_ready, l * 2 * NG + j * 2 + r + 1)
                        act.activation(ah[:, par, r, :], ab[:, r, :], ACT.Copy).then_inc(ah_ready, 1)

                mlp_step(0, n0, n3, MLP0, 0)
                with act.Fori(0, (NG - 1) // 2) as it:
                    for v in range(2):
                        j = it * 2 + (1 + v)
                        base, thirds, c = n0 + it * 6, n3 + it * 2, MLP0 + 2 + 3 * v
                        ada_load(l * NG + j)
                        mlp_step(j, base, thirds, c, (1 + v) % 2)
                        used(base + c + 2)
                        ahead(c + 2, base, thirds)
                for i in range(KT):
                    past(act, ffn_added, l * 8 * NG + (8 * NG - 8 + i + 1))
                    square(l * 2 + 2, i, sqb, x, th=l * 2 + 2)

            for i in range(KT):
                square(5, i, sqb2, x, th=5, gain=col(PC_FINAL + i))
            root_tokens(4)
            for dst, src in ((t2[:, :], cst2), (gw[:, :, :], gatew), (w2kp[:, :, :, :], w2k), (w2v[:, :, :], w2v_in),
                             (lru[:, :, :, :], lruw)):
                act.dma_start(dst, src).then_inc(tables2_loaded, 16)
            for t in range(ADA_SLABS - LAYERS * NG):
                act.dma_start(adab_tail[:, t, :, :].rearrange("p k c -> p (k c)"), ada[LAYERS * NG + t, :, :]).then_inc(ada_loaded, 16)
            act.wait_ge(inv_step, 2)
            act.activation(inv_tok[:, 3, :], inv_tok[:, 2, :], ACT.Sqrt, bias=eps[:, :], scale=1.0 / D).then_inc(std_ready, 1)
            highs(4, nt2, shift=0)
            act.wait_ge(tables2_loaded, 16 * 5)
            act.activation(gwh[:, :, :], gw[:, :, :], ACT.Copy).then_inc(gwh_ready, 1)
            high(B2 + 2, (B2 + 2) % RING, (B2 + 2) // RING)

            def after(n):
                if n + RING < SLABS:
                    high(n + RING, n % RING, (n + RING) // RING)

            for c in range(CMP0 - B2):
                n = B2 + c
                used(n)
                b0 = 2 * (c % 2)
                for m in range(2):
                    if c == 0:
                        last = act.activation(kcv[:, m, :], bank(b0 + m), ACT.Copy)
                    elif c == 1:
                        last = act.activation(ksw[:, m, :], bank(b0 + m), ACT.Copy)
                    elif c == 2:
                        last = act.activation(vv[:, 2 * m:2 * m + 2, :], ps[:, b0 + m, :].rearrange("p (i d) -> p i d", i=2), ACT.Copy)
                    elif c in (3, 4):
                        i = 2 * (c - 3) + m
                        act.activation(cx[:, i, :], bank(b0 + m), ACT.Identity, bias=col(PC_RCONV + 5 * i + 4),
                                       scale=col(PC_RCONV + 5 * i + 3)).then_inc(cx_init, 1)
                    elif c in (5, 6):
                        last = act.activation(gg[:, 2 * (c - 5) + m, :], bank(b0 + m), ACT.Gelu_apprx_tanh)
                    else:
                        last = act.activation(q2[:, 2 * (c - 7) + m, :], bank(b0 + m), ACT.Copy, scale=-HD ** -0.5)
                if c not in (3, 4):
                    last.then_inc(proj2_evac, 1)
                if c == 2:
                    act.wait_ge(zeroed, 1)
                    for kv in range(2):
                        for g in range(2):
                            act.wait_ge(dup_ready, 2 * kv + g + 1)
                            act.activation(kkh[0:HD, kv, g, 0:S], ps[0:HD, 4 + 2 * kv + g, :], ACT.Copy)
                            act.activation(kkh[HD:P, kv, g, 0:S - 1], ps[HD:P, 4 + 2 * kv + g, 1:S], ACT.Copy)
                            act.activation(kkh[:, kv, g, S:S + 31:2], col(PC_POS + 16 * kv, 16), ACT.Copy).then_inc(kkh_ready, 1)
                if c in (5, 6):
                    for i in range(4):
                        act.wait_ge(lru_ready, 4 * (c - 5) + i + 1)
                        act.activation((rr, ii)[c - 5][:, i, :], bank(4 + i), ACT.Sigmoid, bias=col((PC_BA, PC_BX)[c - 5] + i))\
                           .then_inc(sig_ready, 1)
                if c == 6:
                    act.wait_ge(sig_ready, 8)
                    act.wait_ge(lru_step, 15)
                    for i in range(4):
                        act.activation(mm[:, i, :], rr[:, i, :], ACT.Tanh, scale=lru_c[:, 5, i:i + 1]).then_inc(th_ready, 1)
                    act.wait_ge(th_ready, 4)
                    for i in range(4):
                        act.activation(rr[:, i, :], rr[:, i, :], ACT.Exp, scale=lru_c[:, 4, i:i + 1]).then_inc(decay_ready, 1)
                    for i in range(4):
                        act.activation(mm[:, i, :], mm[:, i, :], ACT.Sqrt, scale=-1.0).then_inc(sqrt_ready, 1)
                after(n)
            act.wait_ge(gate_ready, 1)
            act.activation(gates[:, :, :].rearrange("p i c -> p (i c)"), ps[:, 4, 0:NT * 24], ACT.Sigmoid).then_inc(gates_sig, 1)
            for i in range(4):
                act.wait_ge(rnn_ready, i + 1)
                act.activation(rr[:, i, :], cx[:, i, :], ACT.Square).then_inc(sq4_ready, 1)
            act.wait_ge(sq4_used, 4)
            act.activation(std[:, :], bank(0), ACT.Sqrt, bias=eps[:, :], scale=2.0 / D).then_inc(std4_ready, 1)
            for kv in range(2):
                for part in range(2):
                    if part == 0 and kv == 1:
                        for i in range(4):
                            act.wait_ge(nt4_ready, i + 1)
                            act.activation(xh[:, i, :], mm[:, i, :], ACT.Copy).then_inc(nh4_ready, 1)
                    used(CMP0 + 2 * kv + part)
                    if kv + part < 2:
                        after(CMP0 + 2 * kv + part)
                for m in range(2):
                    act.activation(hbias[:, 2 * kv + m:2 * kv + m + 1], ps[:, 2 + 4 * kv + m, POS_COL:POS_COL + 1], ACT.Copy)\
                       .then_inc(hbias_ready, 1)
                act.wait_ge(hbias_ready, 2 * kv + 2)
                for m in range(2):
                    for g in range(2):
                        act.activation(hid[:, kv, m, g, 0:N_CMP], ps[:, 2 + 4 * kv + m, g * CMPC:g * CMPC + N_CMP],
                                       ACT.Gelu_apprx_tanh, bias=hbias[:, 2 * kv + m:2 * kv + m + 1]).then_inc(hid_ready, 1)
            act.wait_ge(kcv_ready, 1)
            act.activation(kcT[:, 0:N_CMP], ps[:, 4, 0:N_CMP], ACT.Copy).then_inc(kcv_evac, 1)
            act.wait_ge(kcv_ready, 2)
            act.activation(vcs[0:N_CMP, :], ps[0:N_CMP, 5, 0:P], ACT.Copy).then_inc(kcv_evac, 1)
            act.wait_ge(nl4_ready, 4)

            def stage(r, g):
                h = slice(HD * g, HD * g + HD)
                act.activation(qc[h, g, :], cols(q2_f[h, :], r * S, S), ACT.Copy)
                act.activation(tsl[:, g, :], alibi, ACT.Copy, scale=cols(slopes, r + 4 * g, 1)).then_inc(staged2, 1)

            def attend(r, first, last_turn):
                def exps(U):
                    past(act, sc_done, r * 18 + U + 1)
                    if U % 9 < 8:
                        w = (U % 9 % 4 + 1) * P
                        act.activation(pb[:, U % 3, 0:w], pb[:, U % 3, 0:w], ACT.Exp, bias=soft[:, 0, U:U + 1], scale=-1.0,
                                       accum_out=soft[:, 1, U:U + 1]).then_inc(exp_done, 1)
                    else:
                        act.activation(pb[:, U % 3, 0:P], pb[:, U % 3, 0:P], ACT.Exp, scale=-1.0).then_inc(exp_done, 1)

                def keep_turned(U):
                    g, v = U // 9, U % 9
                    past(act, t_done, r * 18 + U + 1)
                    act.wait_ge(values_used, r * 6 + 3 * g + min(v // 4, 2) + 1)
                    if v < 8:
                        i = v % 4
                        act.activation(pt[:, v // 4, 0:i + 1, i * P:(i + 1) * P],
                                       ps[:, 3 + U % 3, 0:(i + 1) * P].rearrange("p (j t) -> p j t", t=P), ACT.Copy)\
                           .then_inc(pt_evac, 1)
                    else:
                        act.activation(ptc[0:N_CMP, :], ps[0:N_CMP, 3 + U % 3, :], ACT.Copy).then_inc(pt_evac, 1)

                for U in range(18):
                    exps(U)
                    if U == 0:
                        past(act, s2_done, r * 18)
                        past(act, sc_done, r * 18)
                        stage(r, 1)
                    if U == 3 and first:
                        after(CMP0 + 3)
                    if U >= 2 or not first:
                        keep_turned(U - 2)
                    if U == 5 and not first:
                        head_out(r - 1, 1)
                    if U == 12 and not last_turn:
                        past(act, s2_done, r * 18 + 9)
                        past(act, sc_done, r * 18 + 9)
                        stage(r + 1, 0)
                    if U == 14:
                        head_out(r, 0)
                if last_turn:
                    keep_turned(16)
                    keep_turned(17)

            def head_out(r, g):
                h = slice(HD * g, HD * g + HD)
                act.wait_ge(values_used, r * 6 + 3 * g + 6)
                act.activation(cols(att_f[h, :], r * S, S), ps[h, 6 + g, :], ACT.Copy).then_inc(att_evac, 1)

            stage(0, 0)
            attend(0, True, False)
            with act.Fori(1, 3) as r:
                attend(r, False, False)
            attend(3, False, True)
            head_out(3, 1)

            past(act, att_evac, 8)
            for i in range(4):
                if i >= 2:
                    act.wait_ge(sq4_used, 4 + i - 1)
                act.activation(sqb2[:, i % 2, :], att[:, i, :], ACT.Square).then_inc(sq4_ready, 1)
            act.wait_ge(sq4_used, 8)
            act.wait_ge(rstd4_ready, 1)
            act.activation(std[:, :], bank(7), ACT.Sqrt, bias=eps[:, :], scale=2.0 / D).then_inc(std4_ready, 1)
            for i in range(4):
                act.wait_ge(nt4_ready, 4 + i + 1)
                act.activation(xh[:, 4 + i, :], nt2[:, i % 2, :], ACT.Copy).then_inc(nh4_ready, 1)
            for w in range(4):
                n = WO2 + w
                used(n)
                for m in range(2):
                    act.activation(ymix[:, 2 * w + m, :], bank(2 * (w % 2) + m), ACT.Copy).then_inc(y_ready, 1)
                for m in range(2):
                    act.wait_ge(y_ready, 2 * w + m + 1)
                    square(6, 2 * w + m, sqb2, ymix, th=6)
                if w < 3:
                    after(n)
            root_tokens(6)
            for i in range(KT):
                act.wait_ge(x2_ready, i + 1)
                square(7, i, sqb2, x, alone=0)
            root()
            highs(5, nt2, shift=24)
            after(FF0 - 1)

            def relu_step(g, n, thirds, n_s, par):
                used(n)
                past(act, ab_ready, g * 2)
                past(act, ah2_ready, g * 2)
                for r in range(2):
                    act.activation(rl[:, r, :], bank(r), ACT.Relu).then_inc(rl_ready, 1)
                for r in range(2):
                    past(act, rl_ready, g * 2 + r + 1)
                    act.activation(ah2[:, par, r, :], rl[:, r, :], ACT.Square).then_inc(ah2_ready, 1)
                if n_s is not None:
                    high(n + RING, n_s, thirds)

            relu_step(0, FF0, (FF0 + RING) // RING, FF0 % RING, 0)
            with act.Fori(0, (NG2 - 1) // 3 - 1) as it:
                for v in range(3):
                    c = FF0 + 1 + 2 * v
                    n = it * 6 + c
                    relu_step(it * 3 + (1 + v), n, it * 2 + (c + RING) // RING, c % RING, (1 + v) % 3)
                    used(n + 1)
                    high(n + 1 + RING, (c + 1) % RING, it * 2 + (c + 1 + RING) // RING)
            for g in range(NG2 - 3, NG2):
                n = FF0 - 1 + 2 * g
                relu_step(g, n, (n + RING) // RING, n % RING if n + RING < SLABS else None, g % 3)
                used(n + 1)
                after(n + 1)
            for i in range(KT):
                past(act, y2_added, 8 * NG2 - 8 + i + 1)
                square(8, i, sqb2, ymix, th=7)
            root_tokens(7)

        @block.vector
        def _(dve):
            for s in vector_counts:
                dve.sem_inc(s, 1)
            dve.memset(eps[:, :], EPS).then_inc(eps_set, 1)
            dve.wait_ge(params_loaded, 16)
            dve.wait_ge(silu_c_ready, 1)
            lam = col(PC_LAM, 4)
            step = [0]

            def lru_op(ins):
                step[0] += 1
                ins.then_inc(lru_step, 1)
                dve.wait_ge(lru_step, step[0])

            lru_op(dve.scalar_tensor_tensor(lru_c[:, 0, :], lam, -1.0, lam, ALU.mult, ALU.max))
            dve.wait_ge(lru_exp, 1)
            lru_op(dve.tensor_scalar(lru_c[:, 2, :], lru_c[:, 1, :], 2.0, None, ALU.add))
            lru_op(dve.reciprocal(lru_c[:, 2, :], lru_c[:, 2, :]))
            lru_op(dve.tensor_tensor(lru_c[:, 3, :], lru_c[:, 1, :], lru_c[:, 2, :], ALU.mult))
            lru_op(dve.tensor_tensor(lru_c[:, 4, :], lru_c[:, 3, :], lru_c[:, 3, :], ALU.mult))
            lru_op(dve.tensor_scalar(lru_c[:, 5, :], lru_c[:, 4, :], 1.0 / 15, None, ALU.mult))
            for odd in (13, 11, 9, 7, 5, 3):
                lru_op(dve.scalar_tensor_tensor(lru_c[:, 5, :], lru_c[:, 5, :], 1.0 / odd, lru_c[:, 4, :], ALU.add, ALU.mult))
            lru_op(dve.scalar_tensor_tensor(lru_c[:, 3, :], lru_c[:, 5, :], 1.0, lru_c[:, 3, :], ALU.add, ALU.mult))
            lru_op(dve.tensor_scalar(lru_c[:, 2, :], lam, 0.0, 4.0, ALU.min, ALU.mult))
            lru_op(dve.scalar_tensor_tensor(lru_c[:, 5, :], lru_c[:, 3, :], -8.0, lru_c[:, 2, :], ALU.mult, ALU.add))
            dve.tensor_scalar(lru_c[:, 4, :], lru_c[:, 5, :], 2.0, None, ALU.mult).then_inc(lru_step, 1)

            def add_square(nk, th, i, buf, into=std):
                dve.wait_ge(sq_ready, nk * KT + i + 1)
                if i == 1:
                    ins = dve.tensor_tensor(into[:, :], buf[:, 0, :], buf[:, 1, :], ALU.add)
                else:
                    dve.wait_ge(sq_added, th * (KT - 2) + i - 1)
                    ins = dve.tensor_tensor(into[:, :], into[:, :], buf[:, i % 2, :], ALU.add)
                ins.then_inc(sq_added, 1)

            def inverse(nk):
                dve.wait_ge(std_ready, nk + 1)
                dve.reciprocal(rstd[:, :], std[:, :]).then_inc(rstd_ready, 1)
                dve.wait_ge(rstd_ready, nk + 1)

            def inverse_tokens(nk, k):
                dve.wait_ge(std_ready, nk + 1)
                dve.reciprocal(inv_tok[:, 1, :], inv_tok[:, 0, :]).then_inc(rstd_ready, 1)
                dve.wait_ge(rstd_ready, nk + 1)
                diagonals(1)
                dve.wait_ge(spread_done, k + 1)

            def diagonals(row):
                dve.tensor_tensor(rstd[:, :].rearrange("p (i t) -> p i t", i=NT),
                                  ident.rearrange("p (a t) -> p a t", a=1).broadcast_to((P, NT, P)),
                                  inv_tok[:, row, :].rearrange("p (i a) -> p i a", a=1).broadcast_to((P, NT, P)),
                                  ALU.mult).then_inc(diag_ready, 1)

            def low_x(sk, gain):
                for i in range(KT):
                    dve.wait_ge(nh_ready, sk * KT + i + 1)
                    dve.scalar_tensor_tensor(xl[:, i, :], x[:, i, :], gain(i), xh[:, i, :].bitcast(F32), ALU.mult, ALU.subtract)\
                       .then_inc(nl_ready, 1)

            def normalise(sk, buf, gain, shift, by):
                def low(i):
                    dve.wait_ge(nh_ready, sk * KT + i + 1)
                    dve.scalar_tensor_tensor(xl[:, i, :], buf[:, i % 2, :], mod[:, shift + i:shift + i + 1],
                                             xh[:, i, :].bitcast(F32), ALU.add, ALU.subtract).then_inc(nl_ready, 1)

                for i in range(KT):
                    if i >= 2:
                        dve.wait_ge(nl_ready, sk * KT + i - 1)
                    dve.scalar_tensor_tensor(buf[:, i % 2, :], x[:, i, :], gain(i), by, ALU.mult, ALU.mult).then_inc(nt_ready, 1)
                    if i >= 1:
                        low(i - 1)
                low(KT - 1)

            def ada_sum(a, buf, loaded):
                dve.wait_ge(ada_loaded, loaded * 16)
                past(dve, ada_done, a)
                for kt in range(KT):
                    if kt == 0:
                        ins = dve.tensor_scalar(ada_acc[:, :], buf[:, 0, :], silu_c[:, 0:1], None, ALU.mult)
                    else:
                        dve.wait_ge(ada_term, a * (KT - 1) + kt)
                        ins = dve.scalar_tensor_tensor(ada_acc[:, :], buf[:, kt, :], silu_c[:, kt:kt + 1], ada_acc[:, :],
                                                       ALU.mult, ALU.add)
                    ins.then_inc(ada_term if kt < KT - 1 else ada_summed, 1)

            def ada_out(a):
                past(dve, ada_done, a + 1)
                dve.tensor_tensor(cols(mod, a * 2, 2), ps[:, 7, 0:2], col(a * 2 + PC_ADAB, 2), ALU.add).then_inc(ada_evac, 1)

            for i in range(1, KT - 1):
                add_square(0, 0, i, sqb)
            dve.wait_ge(ws_loaded, 16)
            dve.memset(ws[HD:P, :, 0:HD], 0.0).then_inc(ws_masked, 1)
            with dve.Fori(0, LAYERS) as l:
                n0 = l * LAYER_SLABS
                low_x(l * 2, lambda i: col(l * PC_LN + (PC_L + i)))
                inverse(l * 2)

                def evacuate(c, dst, i0):
                    dve.wait_ge(slab_used, n0 + (c + 1 + RING))
                    for m in range(2):
                        last = dve.tensor_tensor(dst[:, i0 + m, :], bank(2 * (c % 2) + m), rstd[:, :], ALU.mult)
                    last.then_inc(fm_evac, 1)

                def rope(i0):
                    t = k if i0 else q
                    for i in range(i0, i0 + 4):
                        dve.wait_ge(rot_ready, l * 8 + i + 1)
                        if i >= 2:
                            dve.wait_ge(rope_done, l * 8 + i - 1)
                        dve.tensor_tensor(rtmp[:, i % 2, :], bank(4 + i % 4), sin, ALU.mult)
                        dve.tensor_tensor(t[:, i % 4, :], t[:, i % 4, :], cos, ALU.mult).then_inc(rope_part, 1)
                        dve.wait_ge(rope_part, l * 8 + i + 1)
                        dve.tensor_tensor(t[:, i % 4, :], t[:, i % 4, :], rtmp[:, i % 2, :], ALU.add).then_inc(rope_done, 1)

                evacuate(0, u, 0)
                dve.wait_ge(vstd_ready, l + 1)
                dve.reciprocal(vss[:, 2, :], vss[:, 1, :]).then_inc(vr_ready, 1)
                dve.wait_ge(vr_ready, l + 1)
                for i in range(NT):
                    last = dve.tensor_scalar(va[:, i, :], va[:, i, :], vss[:, 2, i:i + 1], None, ALU.mult)
                last.then_inc(va_ready, 1)
                evacuate(3, q, 0)
                evacuate(4, q, 2)
                evacuate(5, k, 0)
                rope(0)
                evacuate(6, k, 2)
                rope(4)
                evacuate(9, sg, 0)
                evacuate(10, sg, 2)
                dve.wait_ge(sv_ready, l + 1)
                for j in range(2):
                    for hh in range(2):
                        h = slice(HD * hh, HD * hh + HD)
                        o = ya[h, j, :].rearrange("p (i t) -> p i t", i=NT)
                        b = bsb_f[h, bass.ds(l * 256 + j * P, P)].rearrange("p (a t) -> p a t", a=1).broadcast_to((HD, NT, P))
                        dve.scalar_tensor_tensor(o, ps[h, 4:8, j * 256 + hh * P:j * 256 + hh * P + P],
                                                 prm[h, bass.ds(l * PC_LN + (PC_L + 8 + j), 1)], b, ALU.mult, ALU.add).then_inc(ya_part, 1)
                dve.wait_ge(u_ready, l + 1)
                for j in range(2):
                    dve.wait_ge(ya_part, l * 4 + 2 * j + 2)
                    dve.tensor_tensor(ya[:, j, :], ya[:, j, :], u[:, j, :], ALU.mult).then_inc(ya_ready, 1)
                for j in range(2):
                    dve.wait_ge(mix_hi, l * 8 + j + 1)
                    dve.tensor_tensor(xl[:, j, :], ya[:, j, :], xh[:, j, :].bitcast(F32), ALU.subtract).then_inc(mix_split, 1)
                for j in range(2):
                    dve.wait_ge(mix_hi, l * 8 + j + 3)
                    dve.scalar_tensor_tensor(xl[:, 2 + j, :], bank(4 + j), col(l * PC_LN + (PC_L + 10 + j)),
                                             xh[:, 2 + j, :].bitcast(F32), ALU.mult, ALU.subtract).then_inc(mix_split, 1)
                def decayed(i):
                    dve.wait_ge(pv_done, l * 8 + (i + 2))
                    dve.wait_ge(s_done, l * 8 + (i + 1))
                    for j in range(NT):
                        b, o = sbank[j]
                        w = S - j * P
                        last = dve.tensor_tensor(sT[:, i % 2, soffs[j]:soffs[j] + w], ps[:, 3 * (i % 2) + b, o:o + w],
                                                 D_f[:, i * S:i * S + w], ALU.mult)
                    last.then_inc(sT_ready, 1)

                def even_squares(t):
                    dve.wait_ge(mean_ready, l * 4 + t + 1)
                    dve.tensor_tensor(y[:, 2 * t, :], y[:, 2 * t, :], bank(2), ALU.subtract).then_inc(yc_ready, 1)
                    dve.wait_ge(yc_ready, l * 4 + t + 1)
                    dve.tensor_tensor(ya[:, t, :], y[:, 2 * t, :], y[:, 2 * t, :], ALU.mult).then_inc(gsq_ready, 1)

                def even_variance(t):
                    dve.wait_ge(var_ready, l * 4 + t + 1)
                    dve.tensor_scalar(ya[:, t, :], bank(5), EPS, None, ALU.add).then_inc(gv_ready, 1)

                def even_inverse(t):
                    past(dve, gv_ready, l * 4 + t + 1)
                    dve.reciprocal(ya[:, t, :], ya[:, t, :]).then_inc(gr_ready, 1)

                for i in range(4):
                    decayed(i)
                even_squares(0)
                decayed(4)
                even_variance(0)
                decayed(5)
                even_inverse(0)
                decayed(6)
                decayed(7)
                even_squares(1)
                even_variance(1)
                even_inverse(1)
                for t in range(2):
                    dve.wait_ge(mean_ready, l * 4 + t + 3)
                    dve.tensor_tensor(y[:, 2 * t + 1, :], y[:, 2 * t + 1, :], bank(4 + t), ALU.subtract).then_inc(yc_ready, 1)
                for half in range(2):
                    turns = [(2 * half + t, turn_order[2 * half + t], (gsq if half else ya)[:, t, :]) for t in range(2)]
                    for turn, i, dev in turns[:2 * half]:
                        dve.wait_ge(var_ready, l * 4 + turn + 1)
                        dve.tensor_scalar(dev, bank(4 + turn), EPS, None, ALU.add).then_inc(gv_ready, 1)
                        past(dve, gv_ready, l * 4 + turn + 1)
                        dve.reciprocal(dev, dev).then_inc(gr_ready, 1)
                    for turn, i, dev in turns:
                        dve.wait_ge(gsd_ready, l * 4 + turn + 1)
                        dve.scalar_tensor_tensor(y[:, i, :], y[:, i, :], col(l * PC_LN + (PC_L + 12 + i)), dev, ALU.mult,
                                                 ALU.mult).then_inc(yn_ready, 1)
                    for turn, i, dev in turns:
                        dve.wait_ge(sg_ready, l * 4 + i + 1)
                        dve.wait_ge(yn_ready, l * 4 + turn + 1)
                        dve.tensor_tensor(y[:, i, :], y[:, i, :], sg[:, i, :], ALU.mult).then_inc(gm_ready, 1)
                    for turn, i, dev in turns:
                        dve.wait_ge(mix_hi, l * 8 + turn + 5)
                        dve.tensor_tensor(xl[:, 4 + i, :], y[:, i, :], xh[:, 4 + i, :].bitcast(F32), ALU.subtract).then_inc(mix_split, 1)
                for i in range(KT):
                    w = i // 2
                    if i == KT - 1:
                        add_square(l * 2 + 1, l * 2 + 1, i - 1, sqb)
                    if i % 2 == 0:
                        dve.wait_ge(half_done, l * W_OUT + w + 1)
                    else:
                        dve.wait_ge(slab_used, l * LAYER_SLABS + (W_IN + w + 1 + RING))
                    dve.tensor_tensor(x[:, i, :], x[:, i, :], bank(2 * ((W_IN + w) % 2) + i % 2), ALU.add).then_inc(mix_added, 1)
                    if 2 <= i < KT - 1:
                        add_square(l * 2 + 1, l * 2 + 1, i - 1, sqb)
                low_x(l * 2 + 1, lambda i: col(l * PC_LN + (PC_L + 16 + i)))
                ada_sum(l * NG, adab, l * NG + 1)
                inverse(l * 2 + 1)

                def scale_up(j, n, r):
                    if r % 2 == 0:
                        dve.wait_ge(slab_used, n + (r // 2 + 1 + RING))
                    dve.tensor_tensor(upb[:, r, :], bank(r), rstd[:, :], ALU.mult).then_inc(up_scaled, 1)

                def conv_middle(j, r):
                    c0 = l * PC_CONVN + j * 16 + PC_CONV
                    dve.wait_ge(cv_init, l * 4 * NG + j * 4 + r + 1)
                    dve.scalar_tensor_tensor(cv[:, r, 1:S], upb[:, r, 0:S - 1], col(c0 + (r * 4 + 1)), cv[:, r, 1:S],
                                             ALU.mult, ALU.add).then_inc(conv_mid, 1)

                def conv_first(j, r):
                    c0 = l * PC_CONVN + j * 16 + PC_CONV
                    dve.wait_ge(conv_mid, l * 4 * NG + j * 4 + r + 1)
                    dve.scalar_tensor_tensor(cv[:, r, 2:S], upb[:, r, 0:S - 2], col(c0 + r * 4), cv[:, r, 2:S],
                                             ALU.mult, ALU.add).then_inc(conv_done, 1)

                def each(step, j, tiles):
                    for r in tiles:
                        step(j, r)

                def gate(j, r):
                    past(dve, conv_done, l * 4 * NG + j * 4 + r + 3)
                    past(dve, act_split, l * 2 * NG + j * 2)
                    dve.wait_ge(sil_ready, l * 2 * NG + j * 2 + r + 1)
                    dve.tensor_tensor(ab[:, r, :], cv[:, r, :], cv[:, 2 + r, :], ALU.mult).then_inc(a_ready, 1)

                def gate_low(j, par, r):
                    dve.wait_ge(ah_ready, l * 2 * NG + j * 2 + r + 1)
                    dve.tensor_tensor(al[:, par, r, :], ab[:, r, :], ah[:, par, r, :].bitcast(F32), ALU.subtract).then_inc(act_split, 1)

                def add_down(j, n, between):
                    for o in range(KT):
                        if o < KT - 1:
                            dve.wait_ge(down_done, l * (KT - 1) * NG + j * (KT - 1) + o + 1)
                        else:
                            dve.wait_ge(slab_used, n + 1 + RING)
                        dve.tensor_tensor(x[:, o, :], x[:, o, :], bank(4 + o % 3), ALU.add).then_inc(ffn_added, 1)
                        between(o)

                for r in range(2):
                    scale_up(0, n0 + MLP0, r)
                each(conv_middle, 0, (0, 1))
                each(conv_first, 0, (0, 1))
                for r in range(2, 4):
                    scale_up(0, n0 + MLP0, r)
                each(conv_middle, 0, (2, 3))
                each(conv_first, 0, (2, 3))
                each(gate, 0, (0, 1))
                for r in range(2):
                    gate_low(0, 0, r)
                ada_out(l * NG)
                with dve.Fori(0, (NG - 1) // 2) as it:
                    for v in range(2):
                        j = it * 2 + (1 + v)
                        n = n0 + it * 6 + (MLP0 + 2 + 3 * v)

                        def values_part(o):
                            if o < 2:
                                conv_middle(j, 2 + o)
                            elif o < 4:
                                conv_first(j, o)
                            elif o < 6:
                                gate(j, o - 4)
                            else:
                                gate_low(j, (1 + v) % 2, o - 6)

                        for r in range(2):
                            scale_up(j, n, r)
                        each(conv_middle, j, (0, 1))
                        each(conv_first, j, (0, 1))
                        ada_sum(l * NG + j, adab, l * NG + j + 1)
                        for r in range(2, 4):
                            scale_up(j, n, r)
                        add_down(it * 2 + v, n + 2, values_part)
                        ada_out(l * NG + j)

                def next_norm(o):
                    if o >= 2:
                        add_square(l * 2 + 2, l * 2 + 2, o - 1, sqb)

                add_down(NG - 1, n0 + (LAYER_SLABS - 1), next_norm)

            past(dve, ada_evac, LAYERS * NG)

            def fold(n, scale, g):
                dve.scalar_tensor_tensor(gains[:, n, :], mod[:, scale:scale + KT], 1.0, col(g, KT), ALU.add, ALU.mult).then_inc(gains_ready, 1)

            for n, (scale, g) in enumerate(((8, PC_PREMIX), (16, PC_POSTMIX), (32, PC_PREMLP))):
                fold(n, scale, g)
            dve.wait_ge(gains_ready, 1)
            dve.tensor_tensor(gains[:, 0, :], gains[:, 0, :], col(PC_FINAL, KT), ALU.mult).then_inc(gains_ready, 1)
            for i in range(1, KT - 1):
                add_square(5, 5, i, sqb2, into=rstd)
            dve.wait_ge(std_ready, 5)
            dve.reciprocal(inv_tok[:, 1, :], inv_tok[:, 0, :]).then_inc(rstd_ready, 1)
            dve.wait_ge(rstd_ready, 5)
            dve.tensor_tensor(inv_tok[:, 2, :], inv_tok[:, 1, :], inv_tok[:, 1, :], ALU.mult).then_inc(inv_step, 1)
            dve.wait_ge(inv_step, 1)
            dve.wait_ge(sum_done, 6)
            dve.tensor_tensor(inv_tok[:, 2, :], inv_tok[:, 2, :], ps[:, 6, 0:NT], ALU.mult).then_inc(inv_step, 1)
            dve.wait_ge(std_ready, 6)
            dve.reciprocal(inv_tok[:, 4, :], inv_tok[:, 3, :]).then_inc(rstd_ready, 1)
            dve.wait_ge(rstd_ready, 6)
            dve.tensor_tensor(inv_tok[:, 4, :], inv_tok[:, 4, :], inv_tok[:, 1, :], ALU.mult).then_inc(inv_step, 1)
            dve.wait_ge(inv_step, 3)
            diagonals(4)
            dve.wait_ge(spread_done, 1)
            dve.wait_ge(gains_ready, 4)
            normalise(4, nt2, lambda i: gains[:, 0, i:i + 1], shift=0, by=bank(6))
            diagonals(1)
            dve.wait_ge(gwh_ready, 1)
            dve.tensor_tensor(gwl[:, :, :], gw[:, :, :], gwh[:, :, :].bitcast(F32), ALU.subtract).then_inc(gw_split, 1)
            dve.wait_ge(spread_done, 2)
            dve.tensor_scalar(std[:, :], bank(6), 1.0, None, ALU.mult).then_inc(inv_step, 1)
            for t in range(ADA_SLABS - LAYERS * NG):
                ada_sum(LAYERS * NG + t, adab_tail[:, t, :, :], ADA_SLABS)
                if t == 0:
                    dve.memset(kkh[:, :, :, :].bitcast(F32), 0.0)
                    dve.memset(kkl[:, :, :, :].bitcast(F32), 0.0)
                    dve.memset(qc[:, :, :], 0.0).then_inc(zeroed, 1)
                ada_out(LAYERS * NG + t)
            past(dve, ada_evac, ADA_SLABS)
            fold(3, 40, PC_POSTMLP)
            dve.wait_ge(zeroed, 1)
            for kv in range(2):
                for g in range(2):
                    dve.wait_ge(kkh_ready, 2 * kv + g + 1)
                    b = 4 + 2 * kv + g
                    dve.tensor_tensor(kkl[0:HD, kv, g, 0:S], ps[0:HD, b, :], kkh[0:HD, kv, g, 0:S].bitcast(F32), ALU.subtract)
                    dve.tensor_tensor(kkl[HD:P, kv, g, 0:S - 1], ps[HD:P, b, 1:S], kkh[HD:P, kv, g, 0:S - 1].bitcast(F32), ALU.subtract)
                    dve.tensor_tensor(kkl[:, kv, g, S:S + 31:2], col(PC_POS + 16 * kv, 16), kkh[:, kv, g, S:S + 31:2].bitcast(F32),
                                      ALU.subtract).then_inc(kk_split, 1)
            dve.wait_ge(inv_step, 4)
            for i in range(KT):
                dve.scalar_tensor_tensor(x[:, i, :], x[:, i, :], col(PC_FINAL + i), std[:, :], ALU.mult, ALU.mult).then_inc(xf_ready, 1)
            for c in range(2):
                for tap in (1, 2, 3):
                    for m in range(2):
                        i = 2 * c + m
                        if tap == 1:
                            dve.wait_ge(cx_init, i + 1)
                        else:
                            dve.wait_ge(cx_mid, 4 * c + 2 * (tap - 2) + m + 1)
                        dve.scalar_tensor_tensor(cx[:, i, tap:S], ps[:, 2 * ((c + 1) % 2) + m, 0:S - tap],
                                                 col(PC_RCONV + 5 * i + 3 - tap), cx[:, i, tap:S],
                                                 ALU.mult, ALU.add).then_inc(cx_mid if tap < 3 else cx_done, 1)
            dve.wait_ge(cx_done, 4)
            dve.wait_ge(sig_ready, 8)
            for i in range(4):
                dve.tensor_tensor(ii[:, i, :], ii[:, i, :], cx[:, i, :], ALU.mult).then_inc(ix_ready, 1)
            for i in range(4):
                dve.wait_ge(decay_ready, i + 1)
                dve.wait_ge(sqrt_ready, i + 1)
                dve.scalar_tensor_tensor(mm[:, i, :], rr[:, i, :], 1.0, mm[:, i, :], ALU.add, ALU.mult).then_inc(aa_ready, 1)
            for i in range(4):
                dve.wait_ge(aa_ready, i + 1)
                dve.wait_ge(ix_ready, i + 1)
                dve.tensor_tensor(mm[:, i, :], mm[:, i, :], ii[:, i, :], ALU.mult).then_inc(uu_ready, 1)
            for i in range(4):
                dve.wait_ge(uu_ready, i + 1)
                dve.tensor_tensor_scan(cx[:, i, :], rr[:, i, :], mm[:, i, :], 0.0, ALU.mult, ALU.add).then_inc(scan_ready, 1)
            dve.wait_ge(proj2_evac, 5)
            for i in range(4):
                dve.wait_ge(scan_ready, i + 1)
                dve.tensor_tensor(cx[:, i, :], cx[:, i, :], gg[:, i, :], ALU.mult).then_inc(rnn_ready, 1)
            dve.wait_ge(gates_sig, 1)
            dve.tensor_scalar(gates[:, 0, 0:8], gates[:, 0, 0:8], seen, None, ALU.mult).then_inc(gates_ready, 1)

            def branch_norm(b, src, g, buf):
                dve.wait_ge(std4_ready, b + 1)
                dve.reciprocal(rstd[:, :], std[:, :]).then_inc(rstd4_ready, 1)
                dve.wait_ge(rstd4_ready, b + 1)

                def low4(i):
                    dve.wait_ge(nh4_ready, 4 * b + i + 1)
                    dve.tensor_tensor(xl[:, 4 * b + i, :], buf(i), xh[:, 4 * b + i, :].bitcast(F32), ALU.subtract).then_inc(nl4_ready, 1)

                for i in range(4):
                    if 4 * b + i >= 2:
                        dve.wait_ge(nl4_ready, 4 * b + i - 1)
                    dve.scalar_tensor_tensor(buf(i), src[:, i, :], col(g + i), rstd[:, :], ALU.mult, ALU.mult).then_inc(nt4_ready, 1)
                    if i >= 1:
                        low4(i - 1)
                low4(3)

            dve.wait_ge(rnn_ready, 4)
            branch_norm(0, cx, PC_NRNN, lambda i: mm[:, i, :])

            dve.wait_ge(gates_ready, 1)

            def attend(r, first, last_turn):
                def minima(U):
                    g, v, at = U % 18 // 9, U % 9, U % 18
                    past(dve, s2_done, r * 18 + U + 1)
                    past(dve, t_done, r * 18 + U - 2 if U >= 3 or not first else 0)
                    if v < 8:
                        i = v % 4
                        w = (i + 1) * P
                        dve.memset(soft[:, 3, at:at + 1], 0.0)
                        dve.tensor_tensor_reduce(out=pb[:, U % 3, 0:w], in0=ps[:, U % 3, 0:w], in1=tsl[:, g, S - w:S], scale=1.0,
                                                 scalar=3e38, op0=ALU.add, op1=ALU.min, accum_out=soft[:, 0, at:at + 1]).then_inc(sc_done, 1)
                    else:
                        s3 = pb[:, U % 3, 0:P].rearrange("p (i c) -> p i c", c=32)
                        c31 = s3[:, :, 0:N_CMP]
                        base = r * 12 + 6 * g
                        dve.memset(pb[:, U % 3, 0:P], 0.0).then_inc(cmp_step, 1)
                        dve.wait_ge(cmp_step, base + 1)
                        dve.scalar_tensor_tensor(c31, alibi_c[:, :, 0:N_CMP], cols(slopes, r + 4 * g, 1),
                                                 ps[:, U % 3, 0:P].rearrange("p (i c) -> p i c", c=32)[:, :, 0:N_CMP],
                                                 ALU.mult, ALU.add).then_inc(cmp_step, 1)
                        dve.wait_ge(cmp_step, base + 2)
                        dve.tensor_reduce(cst[:, 0, :], c31, AX.X, ALU.min).then_inc(cmp_step, 1)
                        dve.wait_ge(cmp_step, base + 3)
                        dve.tensor_tensor(c31, c31, cst[:, 0, :].rearrange("p (i a) -> p i a", a=1).broadcast_to((P, NT, N_CMP)),
                                          ALU.subtract).then_inc(sc_done, 1)

                def weigh(U):
                    g, v = U // 9, U % 9
                    dve.wait_ge(exp_done, r * 18 + U + 1)
                    if v < 8:
                        i = v % 4
                        w = (i + 1) * P
                        dve.reciprocal(soft[:, 2, U:U + 1], soft[:, 1, U:U + 1]).then_inc(rs_ready, 1)
                        dve.wait_ge(rs_ready, r * 16 + 8 * g + v + 1)
                        dve.tensor_scalar(pb[:, U % 3, 0:w], pb[:, U % 3, 0:w], soft[:, 2, U:U + 1],
                                          cols(gates[:, i, :], r + ((1 + v // 4) * 8 + 4 * g), 1), ALU.mult, ALU.mult).then_inc(p_ready, 1)
                    else:
                        c31 = pb[:, U % 3, 0:P].rearrange("p (i c) -> p i c", c=32)[:, :, 0:N_CMP]
                        base = r * 12 + 6 * g
                        dve.tensor_reduce(cst[:, 1, :], c31, AX.X, ALU.add).then_inc(cmp_step, 1)
                        dve.wait_ge(cmp_step, base + 4)
                        dve.reciprocal(cst[:, 2, :], cst[:, 1, :]).then_inc(cmp_step, 1)
                        dve.wait_ge(cmp_step, base + 5)
                        dve.tensor_tensor(cst[:, 3, :], cst[:, 2, :], gate_cols(r + 4 * g),
                                          ALU.mult).then_inc(cmp_step, 1)
                        dve.wait_ge(cmp_step, base + 6)
                        dve.tensor_tensor(c31, c31, cst[:, 3, :].rearrange("p (i a) -> p i a", a=1).broadcast_to((P, NT, N_CMP)),
                                          ALU.mult).then_inc(p_ready, 1)

                def gate_cols(c):
                    g = gates[:, :, c:c + 1] if isinstance(c, int) else gates[:, :, bass.ds(c, 1)]
                    return g.rearrange("p i a -> p (i a)")

                if first:
                    dve.wait_ge(staged2, 1)
                    minima(0)
                for U in range(18):
                    if U + 1 < 18 or not last_turn:
                        if U + 1 in (9, 18):
                            dve.wait_ge(staged2, 2 * r + (U + 1) // 9 + 1)
                        minima(U + 1)
                    weigh(U)

            attend(0, True, False)
            with dve.Fori(1, 3) as r:
                attend(r, False, False)
            attend(3, False, True)
            branch_norm(1, att, PC_NATT, lambda i: nt2[:, i % 2, :])

            def post_norm(nk, n, first, k):
                inverse_tokens(nk, k)
                for i in range(KT + 1):
                    if i < KT:
                        dve.scalar_tensor_tensor(ymix[:, i, :], ymix[:, i, :], gains[:, n, i:i + 1], bank(6), ALU.mult, ALU.mult)\
                           .then_inc(pn_ready, 1)
                    if i >= 1:
                        dve.wait_ge(pn_ready, first + i)
                        dve.tensor_tensor(x[:, i - 1, :], x[:, i - 1, :], ymix[:, i - 1, :], ALU.add).then_inc(x2_ready, 1)

            for i in range(1, KT - 1):
                add_square(6, 6, i, sqb2)
            dve.wait_ge(gains_ready, 5)
            dve.wait_ge(xf_ready, KT)
            post_norm(6, 1, 0, 2)
            inverse(7)
            normalise(5, nt2, lambda i: gains[:, 2, i:i + 1], shift=24, by=rstd[:, :])
            dve.wait_ge(x2_ready, KT)
            dve.memset(ymix[:, :, :], 0.0).then_inc(y_zero, 1)
            dve.wait_ge(y_zero, 1)

            def relu_square(g, r):
                past(dve, act2_split, g * 2)
                past(dve, rl_ready, g * 2 + r + 1)
                dve.tensor_tensor(ab2[:, r, :], rl[:, r, :], rl[:, r, :], ALU.mult).then_inc(ab_ready, 1)

            def relu_low(g, par, r):
                past(dve, ab_ready, g * 2 + r + 1)
                past(dve, ah2_ready, g * 2 + r + 1)
                dve.tensor_tensor(al2[:, par, r, :], ab2[:, r, :], ah2[:, par, r, :].bitcast(F32), ALU.subtract).then_inc(act2_split, 1)

            def add_down2(g, n, between):
                for o in range(KT):
                    if o < KT - 1:
                        dve.wait_ge(down2_done, g * (KT - 1) + o + 1)
                    else:
                        dve.wait_ge(slab_used, n + 1 + RING)
                    dve.tensor_tensor(ymix[:, o, :], ymix[:, o, :], bank(2 + o % 4), ALU.add).then_inc(y2_added, 1)
                    between(o)

            for r in range(2):
                relu_square(0, r)
            for r in range(2):
                relu_low(0, 0, r)
            with dve.Fori(0, (NG2 - 1) // 3) as it:
                for v in range(3):
                    def activation(o):
                        if o in (1, 2):
                            relu_square(it * 3 + (1 + v), o - 1)
                        if o in (3, 4):
                            relu_low(it * 3 + (1 + v), (1 + v) % 3, o - 3)

                    add_down2(it * 3 + v, it * 6 + (FF0 + 2 + 2 * v), activation)

            def last_norm(o):
                if o >= 2:
                    add_square(8, 7, o - 1, sqb2)

            add_down2(NG2 - 1, SLABS - 1, last_norm)
            post_norm(8, 3, KT, 3)


def slab8(w):
    return w.reshape(KT, P, GRP).transpose(1, 0, 2).reshape(P, SLABW)


def slab2(w):
    return w.reshape(2, P, D).transpose(1, 0, 2).reshape(P, SLABW)


def columns(v):
    return v.reshape(-1, P).T


def kernel(**inputs):
    import concourse.bacc as bacc
    from concourse.bass_utils import run_bass_kernel_spmd

    a = {n: np.asarray(v) for n, v in inputs.items()}
    f = np.float32
    pairs = np.concatenate([np.r_[r * HD:(r + 1) * HD, (4 + r) * HD:(5 + r) * HD] for r in range(4)])

    slabs = np.empty((SLABS, P, SLABW), f)
    n = 0

    def add(slab):
        nonlocal n
        slabs[n] = slab
        n += 1

    for l in range(LAYERS):
        for c in range(W_IN):
            add(slab8(a["w_in"][l][:, c * GRP:(c + 1) * GRP]))
        for c in range(W_OUT):
            add(slab8(a["w_out"][l][:, c * GRP:(c + 1) * GRP]))
        for j in range(NG):
            add(slab8(a["w_up"][l][:, j * GRP:(j + 1) * GRP]))
            add(slab8(a["w_up"][l][:, DFF + j * GRP:DFF + (j + 1) * GRP]))
            if j:
                add(slab2(a["w_down"][l][(j - 1) * GRP:j * GRP]))
        add(slab2(a["w_down"][l][DFF - GRP:]))
    w2 = a["w_in_2"][0]
    heads = w2[:, 1024:1536][:, pairs]
    rest = {m: w2[:, 1536 + P * i:1536 + P * (i + 1)] for i, m in enumerate(("kc", "vc", "ks", "vs", "kw", "vw"))}
    add(slab8(np.concatenate([rest["kc"], rest["vc"]], 1)))
    add(slab8(np.concatenate([rest["ks"], rest["kw"]], 1)))
    add(slab8(np.concatenate([rest["vs"], rest["vw"]], 1)))
    for c in (2, 3, 0, 1):
        add(slab8(w2[:, c * GRP:(c + 1) * GRP]))
    add(slab8(heads[:, 0:GRP]))
    add(slab8(heads[:, GRP:]))
    for w1 in (a["cmp_w1_k_2"][0], a["cmp_w1_v_2"][0]):
        for part in range(2):
            add(slab8(w1[part * D:(part + 1) * D]))
    wo = a["w_out_2"][0]
    wo = np.concatenate([wo[0:512], wo[512:][pairs]], 0)
    for c in range(4):
        add(slab8(wo[:, c * GRP:(c + 1) * GRP]))
    for g in range(NG2):
        add(slab8(a["w_ff1_2"][0][:, g * GRP:(g + 1) * GRP]))
        if g:
            add(slab2(a["w_ff2_2"][0][(g - 1) * GRP:g * GRP]))
    add(slab2(a["w_ff2_2"][0][DFF2 - GRP:]))
    assert n == SLABS

    ada = np.stack([slab8(a["ada_w_2"][0][:, i * GRP:(i + 1) * GRP]) for i in range(ADA_SLABS)])

    prm = []
    for l in range(LAYERS):
        prm += [columns(a[m][l]) for m in ("norm1_g", "a_vnorm_g", "b_scale", "c_norm_g", "norm2_g")]
    for l in range(LAYERS):
        taps = np.concatenate([a["conv_w"][l], a["conv_b"][l][None]], 0).reshape(4, 2, NG, 2, P)
        prm.append(taps.transpose(4, 2, 1, 3, 0).reshape(P, PC_CONVN))
    prm += [columns(a["final_g"]), columns(a["c_2"][0]), columns(a["ada_b_2"][0])]
    prm += [columns(a[m][0]) for m in ("pre_norm_mix_2", "post_norm_mix_2", "pre_norm_mlp_2", "post_norm_mlp_2")]
    taps = np.concatenate([a["conv_w_2"][0], a["conv_b_2"][0][None]], 0).reshape(5, 4, P)
    prm.append(taps.transpose(2, 1, 0).reshape(P, 20))
    prm += [columns(a[m][0]) for m in ("lru_ba_2", "lru_bx_2", "lru_lambda_2", "norm_rnn_out_2")]
    prm.append(columns(a["norm_att_out_2"][0][pairs]))
    prm += [columns(a["cmp_pos_k_2"][0].reshape(-1)), columns(a["cmp_pos_v_2"][0].reshape(-1))]
    prm = np.ascontiguousarray(np.concatenate(prm, 1))

    def half_pairs(w):
        out = np.zeros((P, len(w) // 2, P), f)
        for i in range(len(w)):
            o = HD * (i % 2)
            out[o:o + HD, i // 2, o:o + HD] = w[i]
        return out

    bs = a["a_bs"].reshape(LAYERS * 2, 2, P)
    w2k = np.zeros((P, 2, 2, P), f)
    for m in range(2):
        for g in range(2):
            w2k[:, m, g, g * HD:(g + 1) * HD] = a["cmp_w2_k_2"][0][m * P:(m + 1) * P]
    c1, c2 = constants()
    arrays = {
        "weights": slabs,
        "ada": ada,
        "params": prm,
        "xin": a["x"][0].T.reshape(KT, P, S).transpose(1, 0, 2),
        "wsT": a["a_ws"].reshape(LAYERS * 4, P, P).transpose(2, 0, 1),
        "bsb": np.repeat(bs.transpose(1, 0, 2), HD, axis=0),
        "bw": half_pairs(a["b_w"].reshape(LAYERS * 4, HD, HD)),
        "cst1": c1,
        "cst2": c2,
        "gatew": w2[:, 2304:2328].reshape(KT, P, 24).transpose(1, 0, 2),
        "w2k": w2k,
        "w2v": a["cmp_w2_v_2"][0].reshape(2, P, HD).transpose(1, 0, 2),
        "lruw": np.stack([half_pairs(a["lru_wa_2"][0]), half_pairs(a["lru_wx_2"][0])], 1),
    }
    nc = bacc.Bacc("TRN2", target_bir_lowering=False, num_devices=1)
    args = []
    feed = {}
    for name, v in arrays.items():
        feed[f"in_{name}"] = np.ascontiguousarray(v)
        args.append(nc.dram_tensor(f"in_{name}", v.shape, F32, kind="ExternalInput").ap())
    yout = nc.dram_tensor("out_y", (P, KT, S), F32, kind="ExternalOutput").ap()
    build(nc, *args, yout)
    got = run_bass_kernel_spmd(nc, [feed], core_ids=[0]).results[0]["out_y"]
    return np.ascontiguousarray(got.transpose(1, 0, 2).reshape(D, S).T)[None]
```
